# Optimizing a Trainium2 kernel written in Bass

```python
import math
import jax, jax.numpy as jnp
from jax import lax
import numpy as np

D_MODEL = 1024
BATCH = 1
SEQ = 256
DEPTH = 2

CHUNK = 64
N_MIXERS = 2
N_A_LAYERS = (DEPTH + 1) // 2
N_B_LAYERS = DEPTH // 2
EPS = 1e-6

RET_HEADS = 4
RET_QK_DIM = D_MODEL // RET_HEADS
RET_V_DIM = 2 * RET_QK_DIM
RET_V_WIDTH = RET_HEADS * RET_V_DIM
RET_IN_WIDTH = 2 * D_MODEL + 2 * RET_V_WIDTH
ROPE_BASE = 10000.0

SGU_BLOCK = 128
SGU_GROUPS = 8
SGU_FFN = 6 * D_MODEL
SGU_HALF = SGU_FFN // 2
SGU_GROUP_DIM = SGU_HALF // SGU_GROUPS

PEER_HEADS = 8
PEER_NKEYS = 128
PEER_EXPERTS = PEER_NKEYS * PEER_NKEYS
PEER_KEY_DIM = 256
PEER_HALF = PEER_KEY_DIM // 2
PEER_TOPK = 16
PEER_TOKEN_BLOCK = 128


def rmsnorm(x, gain):
    x32 = x.astype(jnp.float32)
    y = x32 * lax.rsqrt(jnp.mean(x32 * x32, axis=-1, keepdims=True) + EPS)
    return (y * gain.astype(jnp.float32)).astype(x.dtype)

def layernorm(x, gain, bias):
    x32 = x.astype(jnp.float32)
    mu = jnp.mean(x32, axis=-1, keepdims=True)
    xc = x32 - mu
    y = xc * lax.rsqrt(jnp.mean(xc * xc, axis=-1, keepdims=True) + EPS)
    return (y * gain.astype(jnp.float32) + bias.astype(jnp.float32)).astype(x.dtype)

def modulate(h, shift, scale):
    return h * (1 + scale[:, None, :]) + shift[:, None, :]

def rotary(x, positions):
    half = x.shape[-1] // 2
    inv_freq = 1.0 / (ROPE_BASE ** (jnp.arange(half, dtype=jnp.float32) / half))
    ang = positions.astype(jnp.float32)[..., None] * inv_freq
    cos = jnp.cos(ang)[:, :, None, :]
    sin = jnp.sin(ang)[:, :, None, :]
    x32 = x.astype(jnp.float32)
    x1, x2 = x32[..., :half], x32[..., half:]
    return jnp.concatenate([x1 * cos - x2 * sin, x1 * sin + x2 * cos], axis=-1)

def retention_mixer(h, positions, w_in, w_out):
    B, S, _ = h.shape
    nc = S // CHUNK
    H, Dk, Dv = RET_HEADS, RET_QK_DIM, RET_V_DIM
    proj = h @ w_in
    q, k, v, g = jnp.split(proj, [D_MODEL, 2 * D_MODEL, 2 * D_MODEL + RET_V_WIDTH], axis=-1)
    q = rotary(q.reshape(B, S, H, Dk), positions)
    k = rotary(k.reshape(B, S, H, Dk), positions) * (Dk ** -0.5)
    v = v.reshape(B, S, H, Dv).astype(jnp.float32)
    log_gamma = jnp.log(1.0 - 2.0 ** (-5.0 - jnp.arange(H, dtype=jnp.float32)))
    idx = jnp.arange(CHUNK, dtype=jnp.float32)
    d_intra = jnp.exp(log_gamma[:, None, None] * jnp.abs(idx[:, None] - idx[None, :]))
    xi = jnp.exp(log_gamma[None, :] * (idx[:, None] + 1.0))
    zeta = jnp.exp(log_gamma[None, :] * (CHUNK - 1.0 - idx[:, None]))
    gamma_chunk = jnp.exp(log_gamma * CHUNK)

    def to_chunks(t):
        return jnp.moveaxis(t.reshape(B, nc, CHUNK, H, t.shape[-1]), 1, 0)

    def step(state, inp):
        qi, ki, vi = inp
        scores = jnp.einsum('bihd,bjhd->bhij', qi, ki) * d_intra[None]
        intra = jnp.einsum('bhij,bjhe->bihe', scores, vi)
        cross = jnp.einsum('bihd,bhde->bihe', qi * xi[None, :, :, None], state)
        state = state * gamma_chunk[None, :, None, None] + jnp.einsum(
            'bjhd,bjhe->bhde', ki * zeta[None, :, :, None], vi)
        return state, intra + cross

    state0 = jnp.zeros((B, H, Dk, Dv), jnp.float32)
    _, y = lax.scan(step, state0, (to_chunks(q), to_chunks(k), to_chunks(v)))
    y = jnp.moveaxis(y, 0, 1).reshape(B, S, H, Dv)
    y = y * lax.rsqrt(jnp.mean(y * y, axis=-1, keepdims=True) + EPS)
    y = y.reshape(B, S, RET_V_WIDTH).astype(h.dtype)
    return (jax.nn.silu(g) * y) @ w_out

def sgu_mixer(h, w_in, b_in, ln_g, ln_b, w_s, b_s, w_out):
    B, S, _ = h.shape
    nb = S // SGU_BLOCK
    z = jax.nn.gelu(h @ w_in + b_in)
    u, v = jnp.split(z, 2, axis=-1)
    v = layernorm(v, ln_g, ln_b)
    pos_chunk = jnp.arange(SGU_BLOCK) // CHUNK
    mask = (pos_chunk[None, :] <= pos_chunk[:, None]).astype(w_s.dtype)
    vb = v.reshape(B, nb, SGU_BLOCK, SGU_GROUPS, SGU_GROUP_DIM)
    s = jnp.einsum('gij,bnjgc->bnigc', w_s * mask[None], vb) + b_s.T[None, None, :, :, None]
    s = s.reshape(B, S, SGU_HALF)
    return (u * s) @ w_out

def peer_ffn(h, w_query, sub_keys, expert_u, expert_v):
    B, S, D = h.shape
    T = B * S
    Hh, K = PEER_HEADS, PEER_TOPK
    ht = h.reshape(T, D)
    q = (ht @ w_query).reshape(T, Hh, 2, PEER_HALF).astype(jnp.float32)
    scores = jnp.einsum('thpd,hpkd->thpk', q, sub_keys.astype(jnp.float32))
    s_top, i_top = lax.top_k(scores, K)
    cand = (s_top[:, :, 0, :, None] + s_top[:, :, 1, None, :]).reshape(T, Hh, K * K)
    cand_idx = (i_top[:, :, 0, :, None] * PEER_NKEYS + i_top[:, :, 1, None, :]).reshape(T, Hh, K * K)
    best, pos = lax.top_k(cand, K)
    expert_idx = jnp.take_along_axis(cand_idx, pos, axis=-1)
    gates = jax.nn.softmax(best, axis=-1).astype(h.dtype)
    nb = T // PEER_TOKEN_BLOCK

    def block(args):
        xb, idx, g = args
        u = expert_u[idx]
        a = jax.nn.gelu(jnp.einsum('tkd,td->tk', u, xb)) * g
        return jnp.einsum('tk,tkd->td', a, expert_v[idx])

    out = lax.map(block, (ht.reshape(nb, PEER_TOKEN_BLOCK, D),
                          expert_idx.reshape(nb, PEER_TOKEN_BLOCK, Hh * K),
                          gates.reshape(nb, PEER_TOKEN_BLOCK, Hh * K)))
    return out.reshape(B, S, D)

def first_inputs(seed: int = 0) -> dict:
    key = jax.random.key(seed)
    ks = jax.random.split(key, 24)
    f32 = jnp.float32
    D = D_MODEL

    def nrm(k, shape, scale):
        return jax.random.normal(k, shape, f32) * scale

    return {
        "x": nrm(ks[0], (BATCH, SEQ, D), 1.0),
        "c": nrm(ks[1], (BATCH, D), 1.0),
        "positions": jnp.broadcast_to(jnp.arange(SEQ, dtype=jnp.int32), (BATCH, SEQ)),
        "norm_mix": 1.0 + nrm(ks[2], (DEPTH, D), 0.05),
        "norm_ffn": 1.0 + nrm(ks[3], (DEPTH, D), 0.05),
        "ada_w": nrm(ks[4], (DEPTH, D, 6 * D), 0.5 * D ** -0.5),
        "ada_b": nrm(ks[5], (DEPTH, 6 * D), 0.02),
        "ret_w_in": nrm(ks[6], (N_A_LAYERS, D, RET_IN_WIDTH), D ** -0.5),
        "ret_w_out": nrm(ks[7], (N_A_LAYERS, RET_V_WIDTH, D), RET_V_WIDTH ** -0.5),
        "sgu_w_in": nrm(ks[8], (N_B_LAYERS, D, SGU_FFN), D ** -0.5),
        "sgu_b_in": nrm(ks[9], (N_B_LAYERS, SGU_FFN), 0.02),
        "sgu_ln_g": 1.0 + nrm(ks[10], (N_B_LAYERS, SGU_HALF), 0.05),
        "sgu_ln_b": nrm(ks[11], (N_B_LAYERS, SGU_HALF), 0.02),
        "sgu_w_s": nrm(ks[12], (N_B_LAYERS, SGU_GROUPS, SGU_BLOCK, SGU_BLOCK), SGU_BLOCK ** -0.5),
        "sgu_b_s": 1.0 + nrm(ks[13], (N_B_LAYERS, SGU_GROUPS, SGU_BLOCK), 0.1),
        "sgu_w_out": nrm(ks[14], (N_B_LAYERS, SGU_HALF, D), SGU_HALF ** -0.5),
        "peer_w_query": nrm(ks[15], (DEPTH, D, PEER_HEADS * PEER_KEY_DIM), D ** -0.5),
        "peer_sub_keys": nrm(ks[16], (DEPTH, PEER_HEADS, 2, PEER_NKEYS, PEER_HALF), PEER_HALF ** -0.5),
        "peer_u": nrm(ks[17], (DEPTH, PEER_EXPERTS, D), D ** -0.5),
        "peer_v": nrm(ks[18], (DEPTH, PEER_EXPERTS, D), 0.5),
        "norm_final": 1.0 + nrm(ks[19], (D,), 0.05),
    }

def first_block(x, c, positions, norm_mix, norm_ffn, ada_w, ada_b, ret_w_in, ret_w_out,
              sgu_w_in, sgu_b_in, sgu_ln_g, sgu_ln_b, sgu_w_s, sgu_b_s, sgu_w_out,
              peer_w_query, peer_sub_keys, peer_u, peer_v, norm_final):
    c_act = jax.nn.silu(c)
    for layer in range(DEPTH):
        mod = c_act @ ada_w[layer] + ada_b[layer]
        sh1, sc1, g1, sh2, sc2, g2 = jnp.split(mod, 6, axis=-1)
        h = modulate(rmsnorm(x, norm_mix[layer]), sh1, sc1)
        j = layer // N_MIXERS
        if layer % N_MIXERS == 0:
            y = retention_mixer(h, positions, ret_w_in[j], ret_w_out[j])
        else:
            y = sgu_mixer(h, sgu_w_in[j], sgu_b_in[j], sgu_ln_g[j], sgu_ln_b[j],
                          sgu_w_s[j], sgu_b_s[j], sgu_w_out[j])
        x = x + g1[:, None, :] * y
        h = modulate(rmsnorm(x, norm_ffn[layer]), sh2, sc2)
        x = x + g2[:, None, :] * peer_ffn(h, peer_w_query[layer], peer_sub_keys[layer],
                                          peer_u[layer], peer_v[layer])
    return rmsnorm(x, norm_final)


DEPTH_2 = 1

MEM_LEN = 256
ATT_WIDTH = D_MODEL // 2
HEAD_DIM = 64
N_ATT_HEADS = ATT_WIDTH // HEAD_DIM
CONV_WIDTH = D_MODEL - ATT_WIDTH
CONV_K = 3
DILATED_PATTERNS = ((128, 1), (512, 4), (2048, 16))
N_MEM_HEADS = 4
MEM_HEAD_DIM = D_MODEL // N_MEM_HEADS
D_FF = 4 * D_MODEL
NORM_EPS = 1e-6
NEG_INF = -1e30
IN_COLS = 3 * ATT_WIDTH + 3 * CONV_WIDTH


def rms_norm(x, g):
    xf = x.astype(jnp.float32)
    y = xf * lax.rsqrt(jnp.mean(xf * xf, axis=-1, keepdims=True) + NORM_EPS)
    return (y * g.astype(jnp.float32)).astype(x.dtype)

def dilated_window_attention(q, k, v, window, dilation):
    b, s, h, e = q.shape
    steps = window // dilation
    span = steps * dilation
    s_pad = -(-s // span) * span
    nb = s_pad // span
    pad = ((0, 0), (0, s_pad - s), (0, 0), (0, 0))

    def blocks(t):
        return jnp.pad(t, pad).reshape(b, nb, steps, dilation, h, e)

    def with_prev(t):
        prev = jnp.pad(t, ((0, 0), (1, 0), (0, 0), (0, 0), (0, 0), (0, 0)))[:, :-1]
        return jnp.concatenate([prev, t], axis=2)

    qb = blocks(q)
    kk = with_prev(blocks(k))
    vv = with_prev(blocks(v))
    scale = 1.0 / math.sqrt(e)
    scores = jnp.einsum('bnqrhe,bnkrhe->bnrhqk', qb, kk).astype(jnp.float32) * scale
    i = jnp.arange(steps)[:, None]
    j = jnp.arange(2 * steps)[None, :]
    band = (j >= i) & (j <= i + steps)
    has_prev = (jnp.arange(nb) > 0)[:, None, None]
    valid = band[None] & (has_prev | (j[None] >= steps))
    scores = jnp.where(valid[None, :, None, None], scores, NEG_INF)
    lse = jax.nn.logsumexp(scores, axis=-1)
    p = jnp.exp(scores - lse[..., None]).astype(v.dtype)
    o = jnp.einsum('bnrhqk,bnkrhe->bnqrhe', p, vv)
    o = o.reshape(b, s_pad, h, e)[:, :s]
    lse = jnp.transpose(lse, (0, 1, 4, 2, 3)).reshape(b, s_pad, h)[:, :s]
    return o, lse

def short_gated_conv(bg, cg, xc, conv_w):
    u = cg * xc
    up = jnp.pad(u, ((0, 0), (CONV_K - 1, 0), (0, 0)))
    s = u.shape[1]
    conv = sum(up[:, tap:tap + s] * conv_w[tap] for tap in range(CONV_K))
    return bg * conv

def hybrid_mixer(h, w_in, conv_w, g_attn_out, g_conv_out, w_out):
    b, s, _ = h.shape
    proj = h @ w_in
    q, k, v, bg, cg, xc = jnp.split(proj, 6, axis=-1)
    q = q.reshape(b, s, N_ATT_HEADS, HEAD_DIM)
    k = k.reshape(b, s, N_ATT_HEADS, HEAD_DIM)
    v = v.reshape(b, s, N_ATT_HEADS, HEAD_DIM)
    outs, lses = [], []
    for window, dilation in DILATED_PATTERNS:
        o, lse = dilated_window_attention(q, k, v, window, dilation)
        outs.append(o)
        lses.append(lse)
    mix_w = jax.nn.softmax(jnp.stack(lses, axis=0), axis=0)
    attn = jnp.einsum('pbsh,pbshe->bshe', mix_w, jnp.stack(outs, axis=0).astype(jnp.float32))
    attn = attn.astype(h.dtype).reshape(b, s, ATT_WIDTH)
    conv = short_gated_conv(bg, cg, xc, conv_w)
    merged = jnp.concatenate([rms_norm(attn, g_attn_out), rms_norm(conv, g_conv_out)], axis=-1)
    return merged @ w_out

def memory_cross_attention(h, mem_n, w_q_mem, w_kv_mem, w_o_mem):
    b, s, _ = h.shape
    q = (h @ w_q_mem).reshape(b, s, N_MEM_HEADS, MEM_HEAD_DIM)
    kv = mem_n @ w_kv_mem
    k, v = jnp.split(kv, 2, axis=-1)
    k = k.reshape(b, MEM_LEN, N_MEM_HEADS, MEM_HEAD_DIM)
    v = v.reshape(b, MEM_LEN, N_MEM_HEADS, MEM_HEAD_DIM)
    scores = jnp.einsum('bshe,bmhe->bhsm', q, k).astype(jnp.float32) / math.sqrt(MEM_HEAD_DIM)
    p = jax.nn.softmax(scores, axis=-1).astype(v.dtype)
    o = jnp.einsum('bhsm,bmhe->bshe', p, v).reshape(b, s, D_MODEL)
    return o @ w_o_mem

def squared_relu_mlp(h, w_up, w_down):
    a = jax.nn.relu(h @ w_up)
    return (a * a) @ w_down

def second_inputs(seed: int = 0) -> dict:
    key = jax.random.key(seed)
    ks = jax.random.split(key, 17)
    f32 = jnp.float32

    def dense(k, fan_in, shape, gain=1.0):
        return jax.random.normal(k, shape, f32) * (gain * fan_in ** -0.5)

    def gain(k, n):
        return 1.0 + 0.02 * jax.random.normal(k, (n,), f32)

    return {
        "x": jax.random.normal(ks[0], (BATCH, SEQ, D_MODEL), f32),
        "mem": jax.random.normal(ks[1], (BATCH, MEM_LEN, D_MODEL), f32),
        "g_mix": gain(ks[2], D_MODEL),
        "w_in": dense(ks[3], D_MODEL, (D_MODEL, IN_COLS)),
        "conv_w": dense(ks[4], CONV_K, (CONV_K, CONV_WIDTH)),
        "g_attn_out": gain(ks[5], ATT_WIDTH),
        "g_conv_out": gain(ks[6], CONV_WIDTH),
        "w_out": dense(ks[7], D_MODEL, (D_MODEL, D_MODEL), 0.5),
        "g_xattn": gain(ks[8], D_MODEL),
        "g_mem": gain(ks[9], D_MODEL),
        "w_q_mem": dense(ks[10], D_MODEL, (D_MODEL, D_MODEL)),
        "w_kv_mem": dense(ks[11], D_MODEL, (D_MODEL, 2 * D_MODEL)),
        "w_o_mem": dense(ks[12], D_MODEL, (D_MODEL, D_MODEL), 0.5),
        "g_mlp": gain(ks[13], D_MODEL),
        "w_up": dense(ks[14], D_MODEL, (D_MODEL, D_FF)),
        "w_down": dense(ks[15], D_FF, (D_FF, D_MODEL), 0.5),
        "g_final": gain(ks[16], D_MODEL),
    }

def second_block(x, mem, g_mix, w_in, conv_w, g_attn_out, g_conv_out, w_out,
              g_xattn, g_mem, w_q_mem, w_kv_mem, w_o_mem,
              g_mlp, w_up, w_down, g_final):
    for _ in range(DEPTH_2):
        x = x + hybrid_mixer(rms_norm(x, g_mix), w_in, conv_w, g_attn_out, g_conv_out, w_out)
        x = x + memory_cross_attention(rms_norm(x, g_xattn), rms_norm(mem, g_mem),
                                       w_q_mem, w_kv_mem, w_o_mem)
        x = x + squared_relu_mlp(rms_norm(x, g_mlp), w_up, w_down)
    return rms_norm(x, g_final)


def setup_inputs(seed=0):
    out = dict(first_inputs(seed))
    for name, value in second_inputs(seed + 1).items():
        if name != "x":
            out[name + "_2"] = value
    return out


def reference(
    x, c, positions, norm_mix, norm_ffn, ada_w, ada_b, ret_w_in, ret_w_out, sgu_w_in, sgu_b_in,
    sgu_ln_g, sgu_ln_b, sgu_w_s, sgu_b_s, sgu_w_out, peer_w_query, peer_sub_keys, peer_u,
    peer_v, norm_final, mem_2, g_mix_2, w_in_2, conv_w_2, g_attn_out_2, g_conv_out_2, w_out_2,
    g_xattn_2, g_mem_2, w_q_mem_2, w_kv_mem_2, w_o_mem_2, g_mlp_2, w_up_2, w_down_2, g_final_2,
):
    x = first_block(
        x, c, positions, norm_mix, norm_ffn, ada_w, ada_b, ret_w_in, ret_w_out, sgu_w_in,
        sgu_b_in, sgu_ln_g, sgu_ln_b, sgu_w_s, sgu_b_s, sgu_w_out, peer_w_query, peer_sub_keys,
        peer_u, peer_v, norm_final,
    )
    return second_block(
        x, mem_2, g_mix_2, w_in_2, conv_w_2, g_attn_out_2, g_conv_out_2, w_out_2, g_xattn_2,
        g_mem_2, w_q_mem_2, w_kv_mem_2, w_o_mem_2, g_mlp_2, w_up_2, w_down_2, g_final_2,
    )


_drawn_inputs = setup_inputs


def setup_inputs(seed=0):
    import zlib

    import numpy as np

    out = dict(_drawn_inputs(seed))
    spreads = {}
    factors = {'sgu_b_in': 4.619,
     'sgu_ln_g': 4.043,
     'sgu_ln_b': 7.774,
     'g_mix_2': 3.757,
     'g_attn_out_2': 8.0,
     'g_conv_out_2': 8.0,
     'g_xattn_2': 8.0,
     'g_mem_2': 8.0,
     'g_mlp_2': 4.993,
     'g_final_2': 2.736}
    for name, (base, spread) in spreads.items():
        noise = np.random.default_rng([zlib.crc32(name.encode()), seed]).standard_normal(out[name].shape)
        drawn = base * np.exp(spread * noise) if base else spread * noise
        out[name] = __import__('jax').numpy.asarray(drawn.astype(out[name].dtype))
    for name, factor in factors.items():
        out[name] = (out[name] * factor).astype(out[name].dtype)
    return out
```

```python
from contextlib import ExitStack

import numpy as np

import concourse.bass as bass
from concourse import mybir

F32 = mybir.dt.float32
I32 = mybir.dt.int32
U32 = mybir.dt.uint32
ALU = mybir.AluOpType
ACT = mybir.ActivationFunctionType
AX_X = mybir.AxisListType.X

P = 128
D = 1024
S = 256
TT = S // P
KD = D // P
EPS = 1e-6
CHUNK = 64
RET_HEADS = 4
RET_QK = D // RET_HEADS
ROPE_BASE = 10000.0
HALF = 3072
CU = HALF // P
GROUPS = 8
PEER_HEADS = 8
TOPK = 16
NKEYS = 128
EXPERTS = NKEYS * NKEYS
PICKS = PEER_HEADS * TOPK
HEADS = 8
HD = 64
MEM_HEADS = 4
NEG = -1e30
LOWEST = -3.0e38

R = 6
BN = 512
BK = 4
U_SLOTS = 4
V_SLOTS = 8
GROUP = 4

TWO_PI_1 = 6.28125
TWO_PI_2 = 0.0019350051879882812
TWO_PI_3 = float(2 * np.pi - 6.28125 - 0.0019350051879882812)
PI_SAFE = 3.1415925

NORM = {0: 0, 1: 1, 2: 2, 3: 3, 6: 4, 4: 5, 5: 6, 7: 7, 8: 8, 9: 9}


def matrices(w):
    out = [(("ada", l), w["ada_w"][l], 8, range(12)) for l in range(2)]
    out += [(("ret_in",), w["ret_w_in"][0], 8, range(12)), (("ret_out",), w["ret_w_out"][0], 16, range(2)),
            (("query", 0), w["peer_w_query"][0], 8, range(4)),
            (("sgu_v",), w["sgu_w_in"][0], 8, range(6, 12)), (("sgu_u",), w["sgu_w_in"][0], 8, range(6)),
            (("sgu_out",), w["sgu_w_out"][0], 24, range(2)),
            (("query", 1), w["peer_w_query"][1], 8, range(4)),
            (("mem_kv",), w["w_kv_mem_2"], 8, range(4)), (("w_in",), w["w_in_2"], 8, range(6)),
            (("w_out",), w["w_out_2"], 8, range(2)), (("q_mem",), w["w_q_mem_2"], 8, range(2)),
            (("o_mem",), w["w_o_mem_2"], 8, range(2)), (("up",), w["w_up_2"], 8, range(8)),
            (("down",), w["w_down_2"], 32, range(2))]
    return out


def numbered(names):
    return {name: i for i, name in enumerate(names)}


def sums_in_order():
    out = [("ada", l, c) for l in range(2) for c in range(12)]
    out += [("ret_in", c) for c in range(12)] + [("ret_y", h) for h in range(RET_HEADS)] + [("ret_out", c) for c in range(2)]
    out += [("query", 0, c) for c in range(4)] + [("peer", 0, t) for t in range(TT)]
    out += [("sgu_v", c) for c in range(6)] + [("sgu_u", c) for c in range(6)] + [("sgu_out", c) for c in range(2)]
    out += [("query", 1, c) for c in range(4)] + [("peer", 1, t) for t in range(TT)]
    out += [("mem_kv", c) for c in range(4)] + [("w_in", c) for c in range(6)] + [("att", h) for h in range(HEADS)]
    out += [("w_out", c) for c in range(2)] + [("q_mem", c) for c in range(2)] + [("matt", h) for h in range(MEM_HEADS)]
    out += [("o_mem", c) for c in range(2)] + [("up", c) for c in range(8)] + [("down", c) for c in range(2)]
    return numbered(out)


def small_in_order():
    def turned(n):
        return [("hT", n, t, g) for t in range(TT) for g in range(2)]
    out = turned(0) + [("ret_s", h) for h in range(RET_HEADS)] + [("ygT", b) for b in range(8)]
    for l in range(2):
        out += [("keysT", l, b) for b in range(4)] + turned(1 + 2 * l)
        out += [("scores", l, t, g) for t in range(TT) for g in range(4)]
        if l == 0:
            out += [("wsT", b) for b in range(2)] + [("ws_sum", b) for b in range(2)] + turned(2)
            out += [("mixed", b) for b in range(CU // 2)]
    out += turned(6) + turned(5) + [("conv_sq",)]
    for h in range(HEADS):
        out += [("attT", h), ("atto", h)]
    out += [("att_rows", t) for t in range(TT)] + turned(7)
    for h in range(MEM_HEADS):
        out += [("mattT", h), ("matto", h)]
    out += turned(8)
    return numbered(out)


def two_blocks(nc, w, out, stop=7):
    MATS = matrices(w)
    blocks, first_block_of = [], {}
    for name, ap, kt, ns in MATS:
        for n in ns:
            first_block_of[name + (n,)] = len(blocks)
            for kb in range(kt // BK):
                blocks.append(ap[kb * BK * P:(kb + 1) * BK * P, n * BN:(n + 1) * BN].rearrange("(k p) n -> p k n", p=P))
    SUM = sums_in_order()
    SMALL = small_in_order()

    ends_sum = {}
    for (name, _, kt, ns) in MATS:
        for n in ns:
            label = name + (n - 6 if name == ("sgu_v",) else n,)
            ends_sum[first_block_of[name + (n,)] + kt // BK - 1] = SUM[label] + 1

    with ExitStack() as ctx:
        def sb(name, shape, dt=F32):
            return ctx.enter_context(nc.sbuf_tensor(name, shape, dt))

        def sem(name):
            return ctx.enter_context(nc.semaphore(name))

        x = sb("x", [P, TT, D])
        mod = sb("mod", [P, 2, 6, D])
        ring = sb("ring", [P, R, BK, BN])
        gain = sb("gain", [P, 2, D])
        ident = sb("ident", [P, P])
        ones = sb("ones", [P, P])
        ss = sb("ss", [P, TT])
        ms = sb("ms", [P, TT])
        root = sb("root", [P, TT])
        rstd = sb("rstd", [P, TT])
        hp = [sb("head_even", [P, 8]), sb("head_odd", [P, 8])]
        hs = hp[0]
        col = sb("col", [P, 96])
        arena = sb("arena", [P, 22528])

        def at(offset, *shape, dt=F32):
            n = int(np.prod(shape))
            assert offset + n <= 22528
            v = arena[:, offset:offset + n]
            if dt != F32:
                v = v.bitcast(dt)
            if len(shape) == 2:
                return v.rearrange("p (a b) -> p a b", b=shape[1])
            if len(shape) == 3:
                return v.rearrange("p (a b c) -> p a b c", b=shape[1], c=shape[2])
            return v

        hT = at(0, KD, S)
        r_qT, r_kT, r_ygT = at(2048, KD, S), at(4096, KD, S), at(2048, 16, S)
        r_v, r_h, r_g = at(6144, TT, 2048), at(6144, TT, D), at(10240, TT, 2048)
        r_sT, r_decay = at(14336, RET_HEADS, 384), at(15872, RET_HEADS, 384)
        r_cos, r_sin, r_tmp = at(17408, S), at(17664, S), at(17920, 2, 512)
        r_junk = at(19968, 2, 512)
        r_pos, r_ang, r_turn = at(18944, S, dt=I32), at(19200, S), at(19456, S)
        c_bc, r_int = at(19968, KD, P), at(20992, S, dt=I32)
        u_buf, v_buf = at(0, U_SLOTS, D), at(4096, V_SLOTS, D)
        p_qT, p_keysT, p_keys = at(2048, 16, S), at(6144, 16, P), at(8192, 16, P)
        p_h, p_s = at(12288, TT, D), at(14336, TT, 16, P)
        p_top, p_pos, p_posf = at(18432, 2, TOPK), at(18464, 2, TOPK, dt=U32), at(18496, 2, TOPK)
        p_cand, p_best, p_at = at(18528, TOPK, TOPK), at(18784, TOPK), at(18800, TOPK, dt=U32)
        p_ij, p_ijf, p_eq = at(18816, 2, TOPK, dt=U32), at(18848, 2, TOPK), at(18880, 2, 256)
        p_i, p_ef, p_d, p_e = at(19392, 2, TOPK), at(19424, TOPK), at(19440, TOPK), at(19456, TOPK)
        p_idx, p_gate, p_z = at(19472, TT, PICKS, dt=I32), at(19728, TT, PICKS), at(19984, 4)
        p_dot, p_act, p_w = at(19988, 2, GROUP), at(19996, 2, GROUP), at(20004, 2, GROUP)
        p_iota, p_diag = at(20012, TOPK), at(20032, 4, P)
        s_h, s_uT, s_v = at(2048, TT, D), at(4096, CU, S), at(10240, TT, HALF)
        s_vbias, s_bs, s_wsT = at(16384, HALF), at(19456, GROUPS, P), at(20480, GROUPS, P)
        s_ws, s_wsum = at(21504, GROUPS, P), at(21504, GROUPS, P)
        s_t = s_vbias.rearrange("p (a b) -> p a b", b=S)
        m_h, m_kT, m_v = mod[:, 0, 0:2, :], mod[:, 0, 2:4, :].rearrange("p a (b t) -> p (a b) t", t=S), mod[:, 0, 4:6, :]
        b_h = at(2048, TT, D)
        b_qT, b_kT, b_v = at(4096, 4, S), at(5120, 4, S), at(6144, TT, 512)
        b_bgT, b_cgT, b_uT, b_cv, b_sq = at(7168, 4, S), at(8192, 4, S), at(9216, 4, 258), at(10248, 4, S), at(11272, 4, S)
        b_mT, b_sm, b_p, b_pT = at(12296, KD, S), at(14344, 2, 384), at(15112, 2, 384), at(15880, 2, 384)
        b_att, b_mask, b_many, b_rs = at(16648, TT, 512), at(17672, 384), at(18056, 384), at(18440, S)
        b_ga = at(18696, 512)
        n_qT, n_p, n_pT, n_oT = at(4096, KD, S), at(6144, 2, TT, S), at(7168, 2, TT, S), at(8192, KD, S)
        f_a, f_t = at(4096, 32, S), at(12288, 2, 4, S)

        pair = [ctx.enter_context(nc.psum_tensor(f"pair{i}", [P, 2, 512], F32)) for i in range(3)]
        small = [ctx.enter_context(nc.psum_tensor(f"small{i}", [P, 512], F32)) for i in range(2)]

        w_in = [sem(f"w_in{i}") for i in range(R)]
        w_used = sem("w_used")
        sum_ready = sem("sum_ready")
        sum_taken = [sem(f"sum_taken{i}") for i in range(3)]
        small_ready = sem("small_ready")
        small_taken = [sem(f"small_taken{i}") for i in range(2)]
        x_in, c_in, cst_in, bias_in = sem("x_in"), sem("c_in"), sem("cst_in"), sem("bias_in")
        rope_in, decay_in = sem("rope_in"), sem("decay_in")
        gain_in = [sem("gain_in0"), sem("gain_in1")]
        gain_used = sem("gain_used")
        c_ready, ones_ready = sem("c_ready"), sem("ones_ready")
        ms_ready, root_ready, h_ready = sem("ms_ready"), sem("root_ready"), sem("h_ready")
        rope_ang, rope_raw, rope_ready = sem("rope_ang"), sem("rope_raw"), sem("rope_ready")
        scores_ready = sem("scores_ready")
        y_sq, y_ms, y_root, yg_ready = sem("y_sq"), sem("y_ms"), sem("y_root"), sem("yg_ready")
        keys_in, iota_in = sem("keys_in"), sem("iota_in")
        best_ready, exp_ready, idx_ready = sem("best_ready"), sem("exp_ready"), sem("idx_ready")
        u_in = [sem(f"u_in{i}") for i in range(U_SLOTS)]
        v_in = [sem(f"v_in{i}") for i in range(V_SLOTS)]
        u_used, v_used = sem("u_used"), sem("v_used")
        act_ready, weight_ready, diag_ready = sem("act_ready"), sem("weight_ready"), sem("diag_ready")
        sgu_in, ws_zero = sem("sgu_in"), sem("ws_zero")
        v_raw, v_gelu, v_mean, v_sq, v_ms, v_root, v_ready = (sem(n) for n in (
            "v_raw", "v_gelu", "v_mean", "v_sq", "v_ms", "v_root", "v_ready"))
        us_ready = sem("us_ready")
        mem_in, hyb_in = sem("mem_in"), sem("hyb_in")
        sq_ready, cms_ready, croot_ready, mcv_ready = sem("sq_ready"), sem("cms_ready"), sem("croot_ready"), sem("mcv_ready")
        smax_ready, e_ready, p_ready = sem("smax_ready"), sem("e_ready"), sem("p_ready")
        arow_ready = sem("arow_ready")
        relu_ready, a_ready = sem("relu_ready"), sem("a_ready")
        out_ready, out_done = sem("out_ready"), sem("out_done")
        dve_step, act_step = sem("dve_step"), sem("act_step")

        def own(eng, step):
            count, pending = [0], {}

            def did(ins, signal=step, value=None):
                if signal is step:
                    count[0] += 1
                    value = count[0]
                ins.then_inc(signal, 1)
                pending[signal.name] = (signal, value)

            def settle():
                for signal, value in pending.values():
                    eng.wait_ge(signal, value)
                pending.clear()

            return did, settle

        def taken_sum(name):
            i = SUM[name]
            return sum_taken[i % 3], i // 3 + 1

        def taken_small(name):
            i = SMALL[name]
            return small_taken[i % 2], i // 2 + 1

        def sum_of(name):
            return pair[SUM[name] % 3]

        def small_of(name):
            return small[SMALL[name] % 2]

        block = ctx.enter_context(nc.Block())
        bc = lambda ap, shape: ap.broadcast_to(shape)

        @block.sync
        def _(sp):
            with nc.allow_non_contiguous_dma(reason="one vector of 1024"):
                sp.dma_start(col[:, 0:KD], w["c"][0].rearrange("(k p) -> p k", p=P)).then_inc(c_in, 16)
            sp.dma_start(mod[:, 0, :, :].rearrange("p a d -> p (a d)"), bc(w["ada_b"][0:1], [P, 6 * D])).then_inc(bias_in, 16)
            last = len(blocks)
            stops = {1: ("ret_out",), 2: ("query", 0), 3: ("sgu_out",), 4: ("query", 1)}
            if stop in stops:
                names = [m[0] for m in MATS]
                nxt = names[names.index(stops[stop]) + 1]
                last = min(v for k, v in first_block_of.items() if k[:len(nxt)] == nxt and len(k) == len(nxt) + 1)
            for i in range(last):
                if i >= R:
                    old = i - R
                    if old in ends_sum:
                        sp.wait_ge(sum_ready, ends_sum[old])
                    else:
                        sp.wait_ge(w_used, old + 1 - sum(e <= old for e in ends_sum))
                sp.dma_start(ring[:, i % R], blocks[i]).then_inc(w_in[i % R], 16)
                if i == 1:
                    sp.dma_start(ident[:], w["ident"]).then_inc(cst_in, 16)
                    sp.dma_start(x[:], w["x"][0].rearrange("(t p) d -> p t d", p=P)).then_inc(x_in, 16)
                if i == 3:
                    sp.dma_start(mod[:, 1, :, :].rearrange("p a d -> p (a d)"), bc(w["ada_b"][1:2], [P, 6 * D])).then_inc(bias_in, 16)
            sp.wait_ge(out_ready, 1)
            src = x if stop < 7 else b_h
            sp.dma_start(out[0].rearrange("(t p) d -> p t d", p=P), src[:, :, :]).then_inc(out_done, 16)
            sp.wait_ge(out_done, 16)

        @block.gpsimd
        def _(pool):
            def load_gain(n, row):
                if n >= 2:
                    pool.wait_ge(gain_used, n - 1)
                pool.dma_start(gain[:, n % 2, :], bc(row, [P, D])).then_inc(gain_in[n % 2], 16)

            def gathers(l, t):
                for k in range(PICKS):
                    s = (l * TT + t) * PICKS + k
                    if k % TOPK == 0:
                        pool.wait_ge(idx_ready, s // TOPK + 1)
                    if k == 0 and t == 0:
                        pool.wait_ge(small_ready, SMALL[("scores", l, TT - 1, 3)] + 1)
                    index = bass.IndirectOffsetOnAxis(ap=p_idx[:, t, k:k + 1], axis=0)
                    if s >= U_SLOTS:
                        pool.wait_ge(u_used, s - U_SLOTS + 1)
                    nc.gpsimd.indirect_dma_start(u_buf[:, s % U_SLOTS, :], None, experts_u, index)\
                        .then_inc(u_in[s % U_SLOTS], 16)
                    if s >= V_SLOTS:
                        pool.wait_ge(v_used, s - V_SLOTS + 1)
                    nc.gpsimd.indirect_dma_start(v_buf[:, s % V_SLOTS, :], None, experts_v, index)\
                        .then_inc(v_in[s % V_SLOTS], 16)

            experts_u = w["peer_u"].rearrange("l e d -> (l e) d")
            experts_v = w["peer_v"].rearrange("l e d -> (l e) d")
            for n, row in enumerate((w["norm_mix"][0:1], w["norm_ffn"][0:1], w["norm_mix"][1:2], w["norm_ffn"][1:2])):
                load_gain(n, row)
            if stop >= 2:
                for t in range(TT):
                    gathers(0, t)
            if stop >= 4:
                for t in range(TT):
                    gathers(1, t)
            if stop >= 5:
                rows = (w["g_mem_2"], w["norm_final"], w["g_mix_2"], w["g_xattn_2"], w["g_mlp_2"], w["g_final_2"])
                for n, row in enumerate(rows[:3 if stop == 5 else 4 if stop == 6 else 6]):
                    load_gain(4 + n, row.rearrange("(a d) -> a d", a=1))

        @block.tensor
        def _(pe):
            def open_sum(name):
                i = SUM[name]
                if i >= 3:
                    pe.wait_ge(sum_taken[i % 3], i // 3)

            def open_small(name):
                i = SMALL[name]
                if i >= 2:
                    pe.wait_ge(small_taken[i % 2], i // 2)

            def landed(i):
                pe.wait_ge(w_in[i % R], 16 * (i // R + 1))
                return ring[:, i % R]

            def rows_product(name, mat, n, lhs, kt):
                open_sum(name)
                acc = sum_of(name)
                for kb in range(kt // BK):
                    i = first_block_of[mat + (n,)] + kb
                    wb = landed(i)
                    for t in range(TT):
                        for k in range(BK):
                            kk = kb * BK + k
                            mm = nc.tensor.matmul(acc[:, t, :], lhs[:, kk, t * P:(t + 1) * P], wb[:, k, :],
                                                  start=(kk == 0), stop=(kk == kt - 1))
                    mm.then_inc(sum_ready if kb == kt // BK - 1 else w_used, 1)

            def columns_product(name, mat, n, rhs, kt=KD):
                open_sum(name)
                acc = sum_of(name)
                for kb in range(kt // BK):
                    i = first_block_of[mat + (n,)] + kb
                    wb = landed(i)
                    for nt in range(4):
                        for k in range(BK):
                            kk = kb * BK + k
                            mm = nc.tensor.matmul(acc[:, nt // 2, nt % 2 * S:(nt % 2 + 1) * S],
                                                  wb[:, k, nt * P:(nt + 1) * P], rhs[:, kk, :],
                                                  start=(kk == 0 and nt % 2 == 0), stop=(kk == kt - 1),
                                                  skip_group_check=True)
                    mm.then_inc(sum_ready if kb == kt // BK - 1 else w_used, 1)

            def turn_rows(n, h):
                for t in range(TT):
                    pe.wait_ge(h_ready, TT * NORM[n] + t + 1)
                    for g in range(2):
                        name = ("hT", n, t, g)
                        open_small(name)
                        for k in range(4):
                            mm = nc.tensor.transpose(small_of(name)[:, k * P:(k + 1) * P],
                                                     h[:, t, (4 * g + k) * P:(4 * g + k + 1) * P], ident[:])
                        mm.then_inc(small_ready, 1)

            def wait_hT(n):
                for t in range(TT):
                    for g in range(2):
                        pe.wait_ge(*taken_small(("hT", n, t, g)))

            def retention():
                turn_rows(0, r_h)
                wait_hT(0)
                for c in range(4):
                    columns_product(("ret_in", c), ("ret_in",), c, hT)
                for c in range(4, 12):
                    rows_product(("ret_in", c), ("ret_in",), c, hT, KD)
                for h in range(RET_HEADS):
                    name = ("ret_s", h)
                    pe.wait_ge(*taken_sum(("ret_in", h // 2)))
                    pe.wait_ge(*taken_sum(("ret_in", 2 + h // 2)))
                    pe.wait_ge(rope_ready, 4)
                    open_small(name)
                    sc = small_of(name)
                    for jt in range(TT):
                        o = sc[:, 0:S] if jt == 0 else sc[:, S:S + P]
                        for half in range(2):
                            mm = nc.tensor.matmul(o, r_kT[:, 2 * h + half, jt * P:(jt + 1) * P],
                                                  r_qT[:, 2 * h + half, jt * P:S], start=(half == 0), stop=(half == 1))
                    mm.then_inc(small_ready, 1)
                for h in range(RET_HEADS):
                    name = ("ret_y", h)
                    pe.wait_ge(scores_ready, h + 1)
                    pe.wait_ge(*taken_sum(("ret_in", 4 + h)))
                    open_sum(name)
                    acc = sum_of(name)
                    vh = r_v[:, :, h * 512:(h + 1) * 512]
                    nc.tensor.matmul(acc[:, 0, :], r_sT[:, h, 0:P], vh[:, 0, :], start=True, stop=True)
                    nc.tensor.matmul(acc[:, 1, :], r_sT[:, h, P:S], vh[:, 0, :], start=True, stop=False)
                    nc.tensor.matmul(acc[:, 1, :], r_sT[:, h, S:S + P], vh[:, 1, :], start=False, stop=True)\
                        .then_inc(sum_ready, 1)
                for b in range(8):
                    name = ("ygT", b)
                    if b % 2 == 0:
                        pe.wait_ge(yg_ready, b // 2 + 1)
                    open_small(name)
                    for q in range(4):
                        t, f = q % 2, 2 * b + q // 2
                        mm = nc.tensor.transpose(small_of(name)[:, q * P:(q + 1) * P], r_g[:, t, f * P:(f + 1) * P], ident[:])
                    mm.then_inc(small_ready, 1)
                for b in range(8):
                    pe.wait_ge(*taken_small(("ygT", b)))
                for c in range(2):
                    rows_product(("ret_out", c), ("ret_out",), c, r_ygT, 16)

            def peer(l):
                n = 1 + 2 * l
                pe.wait_ge(keys_in, 16 * (l + 1))
                for b in range(4):
                    name = ("keysT", l, b)
                    open_small(name)
                    for q in range(4):
                        mm = nc.tensor.transpose(small_of(name)[:, q * P:(q + 1) * P], p_keys[:, 4 * b + q, :], ident[:])
                    mm.then_inc(small_ready, 1)
                turn_rows(n, p_h)
                wait_hT(n)
                for c in range(4):
                    columns_product(("query", l, c), ("query", l), c, hT)
                for b in range(4):
                    pe.wait_ge(*taken_small(("keysT", l, b)))
                for c in range(4):
                    pe.wait_ge(*taken_sum(("query", l, c)))
                for t in range(TT):
                    for g in range(4):
                        name = ("scores", l, t, g)
                        open_small(name)
                        for q in range(4):
                            mm = nc.tensor.matmul(small_of(name)[:, q * P:(q + 1) * P], p_qT[:, 4 * g + q, t * P:(t + 1) * P],
                                                  p_keysT[:, 4 * g + q, :], start=True, stop=True)
                        mm.then_inc(small_ready, 1)
                for t in range(TT):
                    name = ("peer", l, t)
                    open_sum(name)
                    acc = sum_of(name)
                    for k in range(PICKS):
                        s = (l * TT + t) * PICKS + k
                        pe.wait_ge(diag_ready, s + 1)
                        pe.wait_ge(v_in[s % V_SLOTS], 16 * (s // V_SLOTS + 1))
                        for half in range(2):
                            mm = nc.tensor.matmul(acc[:, half, :], p_diag[:, s % 4, :],
                                                  v_buf[:, s % V_SLOTS, half * 512:(half + 1) * 512],
                                                  start=(k == 0), stop=(k == PICKS - 1))
                        mm.then_inc(v_used, 1)
                    pe.wait_ge(v_used, (l * TT + t + 1) * PICKS)
                    pe.sem_inc(sum_ready, 1)

            def sgu():
                pe.wait_ge(sgu_in, 16 * 6)
                for b in range(2):
                    name = ("wsT", b)
                    open_small(name)
                    for q in range(4):
                        mm = nc.tensor.transpose(small_of(name)[:, q * P:(q + 1) * P], s_ws[:, 4 * b + q, :], ident[:])
                    mm.then_inc(small_ready, 1)
                pe.wait_ge(ws_zero, 1)
                for b in range(2):
                    pe.wait_ge(*taken_small(("wsT", b)))
                for b in range(2):
                    name = ("ws_sum", b)
                    open_small(name)
                    nc.tensor.matmul(small_of(name)[:, :], ones[:], s_wsT[:, 4 * b:4 * b + 4, :].rearrange("p g i -> p (g i)"),
                                     start=True, stop=True).then_inc(small_ready, 1)
                turn_rows(2, s_h)
                wait_hT(2)
                for c in range(6):
                    rows_product(("sgu_v", c), ("sgu_v",), 6 + c, hT, KD)
                for c in range(6):
                    columns_product(("sgu_u", c), ("sgu_u",), c, hT)
                pe.wait_ge(v_ready, TT)
                for b in range(CU // 2):
                    name = ("mixed", b)
                    open_small(name)
                    for q in range(2):
                        f = 2 * b + q
                        for t in range(TT):
                            mm = nc.tensor.matmul(small_of(name)[:, q * S + t * P:q * S + (t + 1) * P],
                                                  s_v[:, t, f * P:(f + 1) * P], s_wsT[:, f // (CU // GROUPS), :],
                                                  start=True, stop=True)
                    mm.then_inc(small_ready, 1)
                pe.wait_ge(us_ready, CU // 2)
                for c in range(2):
                    rows_product(("sgu_out", c), ("sgu_out",), c, s_uT, CU)

            def softmax_turned(tag, h, lhs, blocks_of):
                name = (tag + "T", h)
                open_small(name)
                for q, src in enumerate(blocks_of):
                    mm = nc.tensor.transpose(small_of(name)[:, q * P:(q + 1) * P], src, ident[:])
                mm.then_inc(small_ready, 1)

            def hybrid():
                turn_rows(6, m_h)
                wait_hT(6)
                for c in range(2):
                    columns_product(("mem_kv", c), ("mem_kv",), c, hT)
                for c in range(2, 4):
                    rows_product(("mem_kv", c), ("mem_kv",), c, hT, KD)
                turn_rows(5, b_h)
                wait_hT(5)
                for c in range(6):
                    if c == 2:
                        rows_product(("w_in", c), ("w_in",), c, hT, KD)
                    else:
                        columns_product(("w_in", c), ("w_in",), c, hT)
                pe.wait_ge(sq_ready, 1)
                open_small(("conv_sq",))
                for q in range(4):
                    mm = nc.tensor.matmul(small_of(("conv_sq",))[:, 0:S], ones[:], b_sq[:, q, :], start=(q == 0), stop=(q == 3))
                mm.then_inc(small_ready, 1)

                def att_scores(h):
                    name = ("att", h)
                    open_sum(name)
                    acc = sum_of(name)
                    lo = h % 2 * HD
                    for t in range(TT):
                        mm = nc.tensor.matmul(acc[:, t, 0:(t + 1) * P], b_qT[lo:lo + HD, h // 2, t * P:(t + 1) * P],
                                              b_kT[lo:lo + HD, h // 2, 0:(t + 1) * P], start=True, stop=True)
                    mm.then_inc(sum_ready, 1)

                def att_out(h):
                    pe.wait_ge(p_ready, h + 1)
                    softmax_turned("att", h, None, [b_p[:, h % 2, q * P:(q + 1) * P] for q in range(3)])
                    pe.wait_ge(*taken_small(("attT", h)))
                    name = ("atto", h)
                    open_small(name)
                    o, pT = small_of(name), b_pT[:, h % 2, :]
                    vh = b_v[:, :, h * HD:(h + 1) * HD]
                    nc.tensor.matmul(o[:, 0:HD], pT[:, 0:P], vh[:, 0, :], start=True, stop=True)
                    nc.tensor.matmul(o[:, HD:2 * HD], pT[:, P:2 * P], vh[:, 0, :], start=True, stop=False)
                    nc.tensor.matmul(o[:, HD:2 * HD], pT[:, 2 * P:3 * P], vh[:, 1, :], start=False, stop=True)\
                        .then_inc(small_ready, 1)

                for c in range(2):
                    pe.wait_ge(*taken_sum(("w_in", c)))
                for h in range(HEADS):
                    att_scores(h)
                    if h == 0:
                        pe.wait_ge(*taken_sum(("w_in", 2)))
                    if h >= 1:
                        att_out(h - 1)
                att_out(HEADS - 1)
                for t in range(TT):
                    pe.wait_ge(arow_ready, t + 1)
                    name = ("att_rows", t)
                    open_small(name)
                    for q in range(4):
                        mm = nc.tensor.transpose(small_of(name)[:, q * P:(q + 1) * P], b_att[:, t, q * P:(q + 1) * P], ident[:])
                    mm.then_inc(small_ready, 1)
                for t in range(TT):
                    pe.wait_ge(*taken_small(("att_rows", t)))
                pe.wait_ge(mcv_ready, 4)
                for c in range(2):
                    rows_product(("w_out", c), ("w_out",), c, b_mT, KD)

            def memory():
                turn_rows(7, b_h)
                wait_hT(7)
                for c in range(2):
                    columns_product(("q_mem", c), ("q_mem",), c, hT)

                def scores(h):
                    name = ("matt", h)
                    open_sum(name)
                    acc = sum_of(name)
                    for t in range(TT):
                        for e in range(2):
                            mm = nc.tensor.matmul(acc[:, t, 0:S], n_qT[:, 2 * h + e, t * P:(t + 1) * P],
                                                  m_kT[:, 2 * h + e, :], start=(e == 0), stop=(e == 1))
                    mm.then_inc(sum_ready, 1)

                def attend(h):
                    pe.wait_ge(p_ready, HEADS + h + 1)
                    softmax_turned("matt", h, None, [n_p[:, h % 2, t, m * P:(m + 1) * P] for m in range(2) for t in range(TT)])
                    pe.wait_ge(*taken_small(("mattT", h)))
                    name = ("matto", h)
                    open_small(name)
                    for e in range(2):
                        for m in range(2):
                            mm = nc.tensor.matmul(small_of(name)[:, e * S:(e + 1) * S],
                                                  m_v[:, m, h * S + e * P:h * S + (e + 1) * P], n_pT[:, h % 2, m, :],
                                                  start=(m == 0), stop=(m == 1))
                    mm.then_inc(small_ready, 1)

                for c in range(2):
                    pe.wait_ge(*taken_sum(("q_mem", c)))
                    pe.wait_ge(*taken_sum(("mem_kv", c)))
                    pe.wait_ge(*taken_sum(("mem_kv", 2 + c)))
                for h in range(MEM_HEADS):
                    scores(h)
                    if h >= 1:
                        attend(h - 1)
                attend(MEM_HEADS - 1)
                for h in range(MEM_HEADS):
                    pe.wait_ge(*taken_small(("matto", h)))
                for c in range(2):
                    rows_product(("o_mem", c), ("o_mem",), c, n_oT, KD)

            def mlp():
                turn_rows(8, b_h)
                wait_hT(8)
                for c in range(8):
                    columns_product(("up", c), ("up",), c, hT)
                pe.wait_ge(a_ready, 8)
                for c in range(2):
                    rows_product(("down", c), ("down",), c, f_a, 32)

            pe.wait_ge(c_ready, KD)
            for l in range(2):
                for c in range(12):
                    name = ("ada", l, c)
                    open_sum(name)
                    for kb in range(2):
                        i = first_block_of[("ada", l, c)] + kb
                        wb = landed(i)
                        for k in range(BK):
                            kk = kb * BK + k
                            mm = nc.tensor.matmul(sum_of(name)[:, 0, :], c_bc[:, kk, :], wb[:, k, :],
                                                  start=(kk == 0), stop=(kk == KD - 1))
                        mm.then_inc(sum_ready if kb == 1 else w_used, 1)
            pe.wait_ge(cst_in, 16)
            pe.wait_ge(ones_ready, 1)
            retention()
            if stop >= 2:
                peer(0)
            if stop >= 3:
                sgu()
            if stop >= 4:
                peer(1)
            if stop >= 5:
                hybrid()
            if stop >= 6:
                memory()
            if stop >= 7:
                mlp()

        @block.vector
        def _(dve):
            did, settle = own(dve, dve_step)
            V = nc.vector

            def norm(n, src, dst, A, B=None, gain_row=None):
                i = NORM[n]
                for t in range(TT):
                    did(V.tensor_tensor_reduce(out=dst[:, t, :] if dst is not src else b_h[:, t, :], in0=src[:, t, :],
                                               in1=src[:, t, :], scale=1.0, scalar=0.0,
                                               op0=ALU.mult, op1=ALU.add, accum_out=ss[:, t:t + 1]))
                settle()
                did(V.tensor_scalar(ms[:], ss[:], 1.0 / D, EPS, ALU.mult, ALU.add), ms_ready, i + 1)
                dve.wait_ge(root_ready, i + 1)
                did(V.reciprocal(rstd[:], root[:]))
                settle()
                if gain_row is not None:
                    dve.wait_ge(gain_in[gain_row % 2], 16 * (gain_row // 2 + 1))
                for t in range(TT):
                    ins = V.scalar_tensor_tensor(out=dst[:, t, :], in0=src[:, t, :], scalar=rstd[:, t:t + 1], in1=A,
                                                 op0=ALU.mult, op1=ALU.mult)
                    if B is None:
                        did(ins, h_ready, TT * i + t + 1)
                    else:
                        did(ins)
                settle()
                if B is not None:
                    for t in range(TT):
                        did(V.tensor_tensor(dst[:, t, :], dst[:, t, :], B, ALU.add), h_ready, TT * i + t + 1)
                if gain_row is not None:
                    settle()
                    dve.sem_inc(gain_used, 1)

            def add_product(name, c, tmp, gate=None):
                dve.wait_ge(sum_ready, SUM[name] + 1)
                acc = sum_of(name)
                xc = x[:, :, c * 512:(c + 1) * 512]
                if gate is None:
                    did(V.tensor_tensor(xc, xc, acc[:, :, :], ALU.add), *taken_sum(name))
                else:
                    did(V.tensor_tensor(tmp, acc[:, :, :], bc(gate[:, c * 512:(c + 1) * 512].unsqueeze(1), [P, TT, 512]), ALU.mult),
                        *taken_sum(name))
                    settle()
                    did(V.tensor_tensor(xc, xc, tmp, ALU.add))
                settle()

            def modulations():
                for l in range(2):
                    dve.wait_ge(bias_in, 16 * (l + 1) if l else 16)
                    if l == 0:
                        dve.wait_ge(bias_in, 32)
                    flat = mod[:, l, :, :].rearrange("p a d -> p (a d)")
                    for c in range(12):
                        name = ("ada", l, c)
                        dve.wait_ge(sum_ready, SUM[name] + 1)
                        did(V.tensor_tensor(flat[:, c * BN:(c + 1) * BN], sum_of(name)[:, 0, :],
                                            flat[:, c * BN:(c + 1) * BN], ALU.add), *taken_sum(name))
                    settle()
                    for j, part in enumerate((1, 4)):
                        n = 2 * l + j
                        dve.wait_ge(gain_in[n % 2], 16 * (n // 2 + 1))
                        did(V.scalar_tensor_tensor(out=mod[:, l, part, :], in0=mod[:, l, part, :], scalar=1.0,
                                                   in1=gain[:, n % 2, :], op0=ALU.add, op1=ALU.mult), gain_used, n + 1)
                        settle()

            def rotary_tables():
                dve.wait_ge(rope_in, 32)
                did(V.tensor_copy(r_ang, r_pos))
                settle()
                did(V.tensor_scalar(r_ang, r_ang, col[:, 8:9], None, ALU.mult))
                settle()
                did(V.tensor_scalar(r_int, r_ang, float(1 / (2 * np.pi)), None, ALU.mult))
                settle()
                did(V.tensor_copy(r_turn, r_int))
                settle()
                for part in (TWO_PI_1, TWO_PI_2, TWO_PI_3):
                    did(V.scalar_tensor_tensor(out=r_ang, in0=r_turn, scalar=-part, in1=r_ang, op0=ALU.mult, op1=ALU.add))
                    settle()
                did(V.tensor_scalar(r_ang, r_ang, PI_SAFE, -PI_SAFE, ALU.min, ALU.max), rope_ang, 1)
                dve.wait_ge(rope_raw, 2)
                did(V.tensor_tensor(r_turn, r_cos, r_cos, ALU.mult))
                settle()
                did(V.tensor_scalar(r_cos, r_turn, -2.0, 1.0, ALU.mult, ALU.add))
                settle()

            def rotate(c):
                name = ("ret_in", c)
                dve.wait_ge(sum_ready, SUM[name] + 1)
                acc = sum_of(name)
                dst = r_qT if c < 2 else r_kT
                x1, x2 = acc[:, :, 0:S], acc[:, :, S:2 * S]
                both = [P, 2, S]
                cs, sn = bc(r_cos.unsqueeze(1), both), bc(r_sin.unsqueeze(1), both)
                d = dst.rearrange("p (h e) t -> p h e t", e=2)[:, 2 * (c % 2):2 * (c % 2) + 2]
                ta = r_tmp[:, 0, :].rearrange("p (h t) -> p h t", t=S)
                tb = r_tmp[:, 1, :].rearrange("p (h t) -> p h t", t=S)
                did(V.tensor_tensor(ta, x2, sn, ALU.mult))
                did(V.tensor_tensor(tb, x2, cs, ALU.mult))
                did(V.tensor_tensor(d[:, :, 0, :], x1, cs, ALU.mult))
                did(V.tensor_tensor(d[:, :, 1, :], x1, sn, ALU.mult), *taken_sum(name))
                settle()
                did(V.tensor_tensor(d[:, :, 0, :], d[:, :, 0, :], ta, ALU.subtract))
                did(V.tensor_tensor(d[:, :, 1, :], d[:, :, 1, :], tb, ALU.add), rope_ready, c + 1)
                settle()

            def retention():
                dve.wait_ge(x_in, 16)
                rotary_tables()
                norm(0, x, r_h, mod[:, 0, 1, :], mod[:, 0, 0, :])
                for c in range(4):
                    rotate(c)
                dve.wait_ge(decay_in, 16)
                for h in range(RET_HEADS):
                    name = ("ret_s", h)
                    dve.wait_ge(small_ready, SMALL[name] + 1)
                    did(V.tensor_tensor(r_sT[:, h, :], small_of(name)[:, 0:384], r_decay[:, h, :], ALU.mult),
                        *taken_small(name))
                    settle()
                    dve.sem_inc(scores_ready, 1)
                for h in range(RET_HEADS):
                    dve.wait_ge(y_sq, 2 * (h + 1))
                    did(V.tensor_scalar(hs[:, 2:4], hs[:, 0:2], 1.0 / 512, EPS, ALU.mult, ALU.add), y_ms, h + 1)
                    dve.wait_ge(y_root, h + 1)
                    did(V.reciprocal(hs[:, 6:8], hs[:, 4:6]))
                    settle()
                    dve.wait_ge(*taken_sum(("ret_in", 8 + h)))
                    name = ("ret_y", h)
                    for t in range(TT):
                        g = r_g[:, t, h * 512:(h + 1) * 512]
                        ins = V.scalar_tensor_tensor(out=g, in0=sum_of(name)[:, t, :], scalar=hs[:, 6 + t:7 + t], in1=g,
                                                     op0=ALU.mult, op1=ALU.mult)
                        did(ins, *(taken_sum(name) if t else (dve_step, None)))
                    settle()
                    dve.sem_inc(yg_ready, 1)
                for c in range(2):
                    add_product(("ret_out", c), c, r_tmp[:, :, :], mod[:, 0, 2, :])

            def first_level(l, t, h):
                for p in range(2):
                    srow = p_s[:, t, 2 * h + p, :]
                    top, pos = p_top[:, p, :], p_pos[:, p, :]
                    did(V.max(top[:, 0:8], srow))
                    settle()
                    did(V.max_index(pos[:, 0:8], top[:, 0:8], srow))
                    settle()
                    did(V.match_replace(srow, top[:, 0:8], srow, LOWEST))
                    settle()
                    did(V.max(top[:, 8:16], srow))
                    settle()
                    did(V.max_index(pos[:, 8:16], top[:, 8:16], srow))
                settle()

            def second_level(l, t, h):
                sq = [P, TOPK, TOPK]
                did(V.tensor_copy(p_posf, p_pos))
                did(V.tensor_tensor(p_cand, bc(p_top[:, 0, :].unsqueeze(2), sq), bc(p_top[:, 1, :].unsqueeze(1), sq), ALU.add))
                settle()
                cand = p_cand.rearrange("p a b -> p (a b)")
                did(V.max(p_best[:, 0:8], cand))
                settle()
                did(V.max_index(p_at[:, 0:8], p_best[:, 0:8], cand))
                settle()
                did(V.match_replace(cand, p_best[:, 0:8], cand, LOWEST))
                settle()
                did(V.max(p_best[:, 8:16], cand))
                settle()
                did(V.max_index(p_at[:, 8:16], p_best[:, 8:16], cand))
                settle()
                did(V.tensor_scalar(p_d, p_best, p_best[:, 0:1], None, ALU.subtract), best_ready, (l * TT + t) * 8 + h + 1)

            def choose(l, t, h):
                sq = [P, TOPK, TOPK]
                did(V.tensor_scalar(p_ij[:, 0, :], p_at, 4, None, ALU.logical_shift_right))
                did(V.tensor_scalar(p_ij[:, 1, :], p_at, 15, None, ALU.bitwise_and))
                settle()
                did(V.tensor_copy(p_ijf, p_ij))
                settle()
                for p in range(2):
                    eq = p_eq[:, p, :].rearrange("p (a b) -> p a b", b=TOPK)
                    did(V.tensor_tensor(eq, bc(p_ijf[:, p, :].unsqueeze(2), sq), bc(p_iota.unsqueeze(1), sq), ALU.is_equal))
                settle()
                for p in range(2):
                    eq = p_eq[:, p, :].rearrange("p (a b) -> p a b", b=TOPK)
                    did(V.tensor_tensor(eq, eq, bc(p_posf[:, p, :].unsqueeze(1), sq), ALU.mult))
                settle()
                did(V.tensor_reduce(p_i.rearrange("p a b -> p (a b)"), p_eq.rearrange("p a (b c) -> p (a b) c", c=TOPK), AX_X, ALU.add))
                settle()
                did(V.tensor_scalar(p_ef, p_i[:, 0, :], float(NKEYS), float(l * EXPERTS), ALU.mult, ALU.add))
                settle()
                did(V.tensor_tensor(p_idx[:, t, h * TOPK:(h + 1) * TOPK], p_ef, p_i[:, 1, :], ALU.add),
                    idx_ready, (l * TT + t) * 8 + h + 1)

            def gates(l, t, h):
                unit = (l * TT + t) * 8 + h
                dve.wait_ge(exp_ready, unit + 1)
                did(V.tensor_reduce(p_z[:, 0:1], p_e, AX_X, ALU.add))
                settle()
                did(V.reciprocal(p_z[:, 1:2], p_z[:, 0:1]))
                settle()
                did(V.tensor_scalar(p_gate[:, t, h * TOPK:(h + 1) * TOPK], p_e, p_z[:, 1:2], None, ALU.mult))
                settle()

            def group(l, t, q):
                for k in range(q * GROUP, (q + 1) * GROUP):
                    s = (l * TT + t) * PICKS + k
                    dve.wait_ge(u_in[s % U_SLOTS], 16 * (s // U_SLOTS + 1))
                    ub = u_buf[:, s % U_SLOTS, :]
                    did(V.tensor_tensor_reduce(out=ub, in0=ub, in1=p_h[:, t, :], scale=1.0, scalar=0.0, op0=ALU.mult,
                                               op1=ALU.add, accum_out=p_dot[:, q % 2, k % GROUP:k % GROUP + 1]), u_used, s + 1)
                n = (l * TT + t) * (PICKS // GROUP) + q
                dve.wait_ge(act_ready, n + 1)
                did(V.tensor_tensor(p_w[:, q % 2, :], p_act[:, q % 2, :], p_gate[:, t, q * GROUP:(q + 1) * GROUP], ALU.mult),
                    weight_ready, n + 1)

            def peer(l):
                n = 1 + 2 * l
                norm(n, x, p_h, mod[:, l, 4, :], mod[:, l, 3, :])
                dve.wait_ge(iota_in, 16 * (l + 1))
                units = [(t, h) for t in range(TT) for h in range(PEER_HEADS)]
                for i in range(-1, len(units)):
                    nxt = units[i + 1] if i + 1 < len(units) else None
                    if nxt is not None and nxt[1] % 2 == 0:
                        dve.wait_ge(*taken_small(("scores", l, nxt[0], nxt[1] // 2)))
                    for g in range(4):
                        if i >= 0:
                            group(l, units[i][0], units[i][1] * 4 + g)
                        if nxt is not None:
                            if g == 0:
                                first_level(l, *nxt)
                                second_level(l, *nxt)
                            if g == 1:
                                choose(l, *nxt)
                            if g == 3:
                                gates(l, *nxt)
                for t in range(TT):
                    name = ("peer", l, t)
                    dve.wait_ge(v_used, (l * TT + t + 1) * PICKS)
                    tmp = u_buf[:, 0, :].rearrange("p (a b) -> p a b", b=512)
                    did(V.tensor_tensor(tmp, sum_of(name)[:, :, :], mod[:, l, 5, :].rearrange("p (a b) -> p a b", b=512), ALU.mult),
                        *taken_sum(name))
                    settle()
                    did(V.tensor_tensor(x[:, t, :], x[:, t, :], u_buf[:, 0, :], ALU.add))
                    settle()

            def sgu():
                did(V.memset(s_wsT[CHUNK:P, :, 0:CHUNK], 0.0), ws_zero, 1)
                norm(2, x, s_h, mod[:, 1, 1, :], mod[:, 1, 0, :])
                dve.wait_ge(sgu_in, 16 * 6)
                for c in range(6):
                    name = ("sgu_v", c)
                    dve.wait_ge(sum_ready, SUM[name] + 1)
                    vc = s_v[:, :, c * BN:(c + 1) * BN]
                    did(V.tensor_tensor(vc, sum_of(name)[:, :, :], bc(s_vbias[:, c * BN:(c + 1) * BN].unsqueeze(1), [P, TT, BN]), ALU.add),
                        *taken_sum(name))
                    settle()
                    dve.sem_inc(v_raw, 1)
                dve.wait_ge(v_gelu, 6)
                for t in range(TT):
                    did(V.tensor_reduce(hs[:, t:t + 1], s_v[:, t, :], AX_X, ALU.add))
                settle()
                did(V.tensor_scalar(hs[:, 2:4], hs[:, 0:2], -1.0 / HALF, None, ALU.mult), v_mean, 1)
                dve.wait_ge(v_mean, 1)
                for t in range(TT):
                    did(V.tensor_scalar(s_v[:, t, :], s_v[:, t, :], hs[:, 2 + t:3 + t], None, ALU.add))
                settle()
                for t in range(TT):
                    did(V.tensor_tensor_reduce(out=s_t.rearrange("p a b -> p (a b)"), in0=s_v[:, t, :], in1=s_v[:, t, :],
                                               scale=1.0, scalar=0.0, op0=ALU.mult, op1=ALU.add, accum_out=hs[:, 4 + t:5 + t]))
                    settle()
                did(V.tensor_scalar(ms[:], hs[:, 4:6], 1.0 / HALF, EPS, ALU.mult, ALU.add), v_ms, 1)
                dve.wait_ge(v_root, 1)
                did(V.reciprocal(rstd[:], root[:]))
                settle()
                for t in range(TT):
                    did(V.tensor_scalar(s_v[:, t, :], s_v[:, t, :], rstd[:, t:t + 1], None, ALU.mult), v_ready, t + 1)
                for b in range(CU // 2):
                    name = ("mixed", b)
                    for q in range(2):
                        f = 2 * b + q
                        g = f // (CU // GROUPS)
                        did(V.scalar_tensor_tensor(out=s_t[:, q, 0:P], in0=s_wsum[:, g, :], scalar=col[:, 56 + f:57 + f],
                                                   in1=s_bs[:, g, :], op0=ALU.mult, op1=ALU.add))
                    settle()
                    dve.wait_ge(small_ready, SMALL[name] + 1)
                    for q in range(2):
                        f = 2 * b + q
                        ins = V.scalar_tensor_tensor(out=s_t[:, 2 + q, :].rearrange("p (t i) -> p t i", i=P),
                                                     in0=small_of(name)[:, q * S:(q + 1) * S].rearrange("p (t i) -> p t i", i=P),
                                                     scalar=col[:, 32 + f:33 + f],
                                                     in1=bc(s_t[:, q, 0:P].unsqueeze(1), [P, TT, P]), op0=ALU.mult, op1=ALU.add)
                        did(ins, *((dve_step, None) if q == 0 else taken_small(name)))
                    settle()
                    if b % 2 == 0:
                        dve.wait_ge(*taken_sum(("sgu_u", b // 2)))
                    did(V.tensor_tensor(s_uT[:, 2 * b:2 * b + 2, :], s_uT[:, 2 * b:2 * b + 2, :], s_t[:, 2:4, :], ALU.mult), us_ready, b + 1)
                    settle()
                for c in range(2):
                    add_product(("sgu_out", c), c, s_v[:, 0, 0:1024].rearrange("p (a b) -> p a b", b=512), mod[:, 1, 2, :])

            def hybrid():
                dve.wait_ge(mem_in, 16)
                norm(6, m_h, m_h, gain[:, 0, :], gain_row=4)
                norm(4, x, x, gain[:, 1, :], gain_row=5)
                norm(5, x, b_h, gain[:, 0, :], gain_row=6)
                did(V.memset(b_uT[:, :, 0:2], 0.0))
                dve.wait_ge(hyb_in, 16 * 5)
                name = ("w_in", 5)
                dve.wait_ge(sum_ready, SUM[name] + 1)
                dve.wait_ge(*taken_sum(("w_in", 4)))
                did(V.tensor_tensor(b_uT[:, :, 2:258], sum_of(name)[:, :, :].rearrange("p a (b t) -> p (a b) t", t=S), b_cgT, ALU.mult),
                    *taken_sum(name))
                settle()
                for q in range(4):
                    did(V.tensor_scalar(b_cv[:, q, :], b_uT[:, q, 0:S], col[:, 40 + q:41 + q], None, ALU.mult))
                settle()
                for tap in (1, 2):
                    for q in range(4):
                        did(V.scalar_tensor_tensor(out=b_cv[:, q, :], in0=b_uT[:, q, tap:tap + S],
                                                   scalar=col[:, 40 + 4 * tap + q:41 + 4 * tap + q], in1=b_cv[:, q, :],
                                                   op0=ALU.mult, op1=ALU.add))
                    settle()
                dve.wait_ge(*taken_sum(("w_in", 3)))
                did(V.tensor_tensor(b_cv, b_cv, b_bgT, ALU.mult))
                settle()
                did(V.tensor_tensor(b_sq, b_cv, b_cv, ALU.mult), sq_ready, 1)
                name = ("conv_sq",)
                dve.wait_ge(small_ready, SMALL[name] + 1)
                did(V.tensor_scalar(b_rs, small_of(name)[:, 0:S], 1.0 / 512, EPS, ALU.mult, ALU.add), *taken_small(name))
                settle()
                dve.sem_inc(cms_ready, 1)
                dve.wait_ge(croot_ready, 1)
                did(V.reciprocal(b_rs, b_rs))
                settle()
                for q in range(4):
                    did(V.scalar_tensor_tensor(out=b_mT[:, 4 + q, :], in0=b_cv[:, q, :], scalar=col[:, 36 + q:37 + q], in1=b_rs,
                                               op0=ALU.mult, op1=ALU.mult), mcv_ready, q + 1)

                def att_max(h):
                    name = ("att", h)
                    dve.wait_ge(sum_ready, SUM[name] + 1)
                    acc = sum_of(name)
                    sm = b_sm[:, h % 2, :]
                    did(V.tensor_tensor(sm[:, 0:P], acc[:, 0, 0:P], b_mask[:, 0:P], ALU.add))
                    did(V.tensor_tensor(sm[:, P:384], acc[:, 1, 0:S], b_mask[:, P:384], ALU.add), *taken_sum(name))
                    settle()
                    did(V.tensor_reduce(hp[h % 2][:, 0:1], sm[:, 0:P], AX_X, ALU.max))
                    did(V.tensor_reduce(hp[h % 2][:, 1:2], sm[:, P:384], AX_X, ALU.max))
                    settle()
                    did(V.tensor_scalar(hp[h % 2][:, 2:4], hp[h % 2][:, 0:2], -(HD ** -0.5), None, ALU.mult), smax_ready, h + 1)

                def att_sum(h):
                    dve.wait_ge(e_ready, 2 * (h + 1))
                    for t, (a, b) in enumerate(((0, P), (P, 384))):
                        e = b_sm[:, h % 2, a:b]
                        did(V.tensor_tensor_reduce(out=b_p[:, h % 2, a:b], in0=e, in1=b_many[:, a:b], scale=1.0, scalar=0.0,
                                                   op0=ALU.mult, op1=ALU.add, accum_out=hp[h % 2][:, 4 + t:5 + t]), *((dve_step, None) if t == 0 else (p_ready, h + 1)))
                    settle()
                    did(V.reciprocal(hp[h % 2][:, 6:8], hp[h % 2][:, 4:6]))
                    settle()

                def att_take(h):
                    name = ("atto", h)
                    dve.wait_ge(small_ready, SMALL[name] + 1)
                    for t in range(TT):
                        did(V.tensor_scalar(b_att[:, t, h * HD:(h + 1) * HD], small_of(name)[:, t * HD:(t + 1) * HD],
                                            hp[h % 2][:, 6 + t:7 + t], None, ALU.mult), *((dve_step, None) if t == 0 else taken_small(name)))
                    settle()

                att_max(0)
                for h in range(HEADS):
                    att_sum(h)
                    if h + 1 < HEADS:
                        att_max(h + 1)
                    att_take(h)
                for t in range(TT):
                    did(V.tensor_tensor_reduce(out=b_sq.rearrange("p a b -> p (a b)")[:, t * 512:(t + 1) * 512], in0=b_att[:, t, :], in1=b_att[:, t, :],
                                               scale=1.0, scalar=0.0, op0=ALU.mult, op1=ALU.add, accum_out=hs[:, t:t + 1]))
                settle()
                did(V.tensor_scalar(ms[:], hs[:, 0:2], 1.0 / 512, EPS, ALU.mult, ALU.add))
                settle()
                dve.sem_inc(cms_ready, 1)
                dve.wait_ge(croot_ready, 2)
                did(V.reciprocal(rstd[:], root[:]))
                settle()
                for t in range(TT):
                    did(V.scalar_tensor_tensor(out=b_att[:, t, :], in0=b_att[:, t, :], scalar=rstd[:, t:t + 1], in1=b_ga,
                                               op0=ALU.mult, op1=ALU.mult), arow_ready, t + 1)
                for c in range(2):
                    add_product(("w_out", c), c, None)

            def memory():
                norm(7, x, b_h, gain[:, 1, :], gain_row=7)

                def head_max(h):
                    name, hm = ("matt", h), hp[h % 2]
                    dve.wait_ge(sum_ready, SUM[name] + 1)
                    did(V.tensor_reduce(hm[:, 0:2], sum_of(name)[:, :, 0:S], AX_X, ALU.max))
                    settle()
                    did(V.tensor_scalar(hm[:, 2:4], hm[:, 0:2], -(256 ** -0.5), None, ALU.mult), smax_ready, HEADS + h + 1)

                head_max(0)
                for h in range(MEM_HEADS):
                    name, hm = ("matt", h), hp[h % 2]
                    dve.wait_ge(e_ready, 2 * (HEADS + h + 1))
                    dve.sem_inc(taken_sum(name)[0], 1)
                    did(V.reciprocal(hm[:, 6:8], hm[:, 4:6]))
                    settle()
                    for t in range(TT):
                        did(V.tensor_scalar(n_p[:, h % 2, t, :], n_p[:, h % 2, t, :], hm[:, 6 + t:7 + t], None, ALU.mult),
                            *((dve_step, None) if t == 0 else (p_ready, HEADS + h + 1)))
                    settle()
                    if h + 1 < MEM_HEADS:
                        head_max(h + 1)
                for c in range(2):
                    add_product(("o_mem", c), c, None)

            def mlp():
                norm(8, x, b_h, gain[:, 0, :], gain_row=8)
                for c in range(8):
                    dve.wait_ge(relu_ready, c + 1)
                    did(V.tensor_tensor(f_a[:, 4 * c:4 * c + 4, :], f_t[:, c % 2], f_t[:, c % 2], ALU.mult), a_ready, c + 1)
                for c in range(2):
                    add_product(("down", c), c, None)
                norm(9, x, b_h, gain[:, 1, :], gain_row=9)

            did(V.memset(ones[:], 1.0), ones_ready, 1)
            modulations()
            retention()
            if stop >= 2:
                peer(0)
            if stop >= 3:
                sgu()
            if stop >= 4:
                peer(1)
            if stop >= 5:
                hybrid()
            if stop >= 6:
                memory()
            if stop >= 7:
                mlp()
            settle()
            dve.sem_inc(out_ready, 1)

        @block.scalar
        def _(act):
            did, settle = own(act, act_step)
            A = nc.scalar

            def norm_root(n):
                act.wait_ge(ms_ready, NORM[n] + 1)
                did(A.activation(root[:], ms[:], ACT.Sqrt), root_ready, NORM[n] + 1)

            def take_hT(n):
                for t in range(TT):
                    for g in range(2):
                        name = ("hT", n, t, g)
                        act.wait_ge(small_ready, SMALL[name] + 1)
                        did(A.activation(hT[:, 4 * g:4 * g + 4, t * P:(t + 1) * P],
                                         small_of(name)[:, :].rearrange("p (k t) -> p k t", t=P), ACT.Copy), *taken_small(name))

            def take_small(name, dst, src):
                act.wait_ge(small_ready, SMALL[name] + 1)
                did(A.activation(dst, src, ACT.Copy), *taken_small(name))

            def take_sum(name, dst, func=ACT.Copy):
                act.wait_ge(sum_ready, SUM[name] + 1)
                did(A.activation(dst, sum_of(name)[:, :, :], func), *taken_sum(name))

            def columns(t):
                return t.rearrange("p (a b) t -> p a (b t)", b=2)

            def retention():
                act.wait_ge(rope_ang, 1)
                did(A.activation(r_sin, r_ang, ACT.Sin), rope_raw, 1)
                did(A.activation(r_cos, r_ang, ACT.Sin, scale=0.5), rope_raw, 2)
                norm_root(0)
                take_hT(0)
                for c in range(4):
                    take_sum(("ret_in", 4 + c), r_v[:, :, c * 512:(c + 1) * 512])
                for c in range(4):
                    take_sum(("ret_in", 8 + c), r_g[:, :, c * 512:(c + 1) * 512], ACT.Silu)
                for h in range(RET_HEADS):
                    act.wait_ge(sum_ready, SUM[("ret_y", h)] + 1)
                    if h:
                        act.wait_ge(y_ms, h)
                    for t in range(TT):
                        did(A.activation(r_junk[:, t, :], sum_of(("ret_y", h))[:, t, :], ACT.Square, accum_out=hs[:, t:t + 1]),
                            y_sq, 2 * h + t + 1)
                        settle()
                    act.wait_ge(y_ms, h + 1)
                    if h:
                        act.wait_ge(yg_ready, h)
                    did(A.activation(hs[:, 4:6], hs[:, 2:4], ACT.Sqrt), y_root, h + 1)
                for b in range(8):
                    take_small(("ygT", b), r_ygT[:, 2 * b:2 * b + 2, :].rearrange("p f t -> p (f t)"), small_of(("ygT", b))[:, :])

            def peer(l):
                n = 1 + 2 * l
                act.wait_ge(ms_ready, NORM[n] + 1)
                act.dma_start(p_keys, w["peer_sub_keys"][l].rearrange("h p k d -> k (h p) d")).then_inc(keys_in, 16)
                if l == 1:
                    act.dma_start(m_h, w["mem_2"][0].rearrange("(t p) d -> p t d", p=P)).then_inc(mem_in, 16)
                act.dma_start(p_iota, bc(w["iota"], [P, TOPK])).then_inc(iota_in, 16)
                norm_root(n)
                for b in range(4):
                    take_small(("keysT", l, b), p_keysT[:, 4 * b:4 * b + 4, :].rearrange("p a k -> p (a k)"), small_of(("keysT", l, b))[:, :])
                take_hT(n)
                for c in range(4):
                    take_sum(("query", l, c), columns(p_qT[:, 4 * c:4 * c + 4, :]))
                for t in range(TT):
                    for g in range(4):
                        take_small(("scores", l, t, g), p_s[:, t, 4 * g:4 * g + 4, :].rearrange("p a k -> p (a k)"),
                                   small_of(("scores", l, t, g))[:, :])

                def exponentials(unit):
                    act.wait_ge(best_ready, unit + 1)
                    did(A.activation(p_e, p_d, ACT.Exp), exp_ready, unit + 1)

                exponentials(l * 16)
                for t in range(TT):
                    for q in range(PICKS // GROUP):
                        i = (l * TT + t) * (PICKS // GROUP) + q
                        act.wait_ge(u_used, GROUP * (i + 1))
                        did(A.activation(p_act[:, q % 2, :], p_dot[:, q % 2, :], ACT.Gelu_apprx_tanh), act_ready, i + 1)
                        act.wait_ge(weight_ready, i + 1)
                        for k in range(GROUP):
                            s = i * GROUP + k
                            if s >= 4:
                                act.wait_ge(v_used, s - 3)
                            did(A.activation(p_diag[:, s % 4, :], ident[:], ACT.Copy, scale=p_w[:, q % 2, k:k + 1]),
                                diag_ready, s + 1)
                        if q % 4 == 2 and not (t == 1 and q // 4 == 7):
                            exponentials((l * TT + t) * 8 + q // 4 + 1)

            def sgu():
                act.wait_ge(ms_ready, NORM[2] + 1)
                act.dma_start(s_ws, w["sgu_w_s"][0].rearrange("g i j -> i g j")).then_inc(sgu_in, 16)
                act.dma_start(s_vbias, bc(w["sgu_b_in"][0:1, HALF:2 * HALF], [P, HALF])).then_inc(sgu_in, 16)
                act.dma_start(s_bs.rearrange("p g i -> p (g i)"), bc(w["sgu_b_s"].rearrange("a g i -> a (g i)"), [P, GROUPS * P])).then_inc(sgu_in, 16)
                with nc.allow_non_contiguous_dma(reason="vectors by feature"):
                    act.dma_start(col[:, 8:32], w["sgu_b_in"][0, 0:HALF].rearrange("(k p) -> p k", p=P)).then_inc(sgu_in, 16)
                    act.dma_start(col[:, 32:56], w["sgu_ln_g"][0].rearrange("(k p) -> p k", p=P)).then_inc(sgu_in, 16)
                    act.dma_start(col[:, 56:80], w["sgu_ln_b"][0].rearrange("(k p) -> p k", p=P)).then_inc(sgu_in, 16)
                norm_root(2)
                for b in range(2):
                    name = ("wsT", b)
                    act.wait_ge(small_ready, SMALL[name] + 1)
                    src = small_of(name)[:, :].rearrange("p (g i) -> p g i", i=P)
                    did(A.activation(s_wsT[0:CHUNK, 4 * b:4 * b + 4, :], src[0:CHUNK], ACT.Copy))
                    did(A.activation(s_wsT[CHUNK:P, 4 * b:4 * b + 4, CHUNK:P], src[CHUNK:P, :, CHUNK:P], ACT.Copy), *taken_small(name))
                for b in range(2):
                    take_small(("ws_sum", b), s_wsum[:, 4 * b:4 * b + 4, :].rearrange("p g i -> p (g i)"), small_of(("ws_sum", b))[:, :])
                take_hT(2)
                for c in range(6):
                    act.wait_ge(v_raw, c + 1)
                    vc = s_v[:, :, c * BN:(c + 1) * BN]
                    did(A.activation(vc, vc, ACT.Gelu_apprx_tanh), v_gelu, c + 1)
                act.wait_ge(sgu_in, 16 * 6)
                for c in range(6):
                    name = ("sgu_u", c)
                    act.wait_ge(sum_ready, SUM[name] + 1)
                    for q in range(4):
                        f = 4 * c + q
                        did(A.activation(s_uT[:, f, :], sum_of(name)[:, q // 2, q % 2 * S:(q % 2 + 1) * S], ACT.Gelu_apprx_tanh,
                                         bias=col[:, 8 + f:9 + f]), *((act_step, None) if q < 3 else taken_sum(name)))
                    settle()
                act.wait_ge(v_ms, 1)
                did(A.activation(root[:], ms[:], ACT.Sqrt), v_root, 1)

            def hybrid():
                norm_root(6)
                norm_root(4)
                act.wait_ge(ms_ready, NORM[5] + 1)
                act.dma_start(b_mask, w["att_mask"]).then_inc(hyb_in, 16)
                act.dma_start(b_many, w["att_many"]).then_inc(hyb_in, 16)
                act.dma_start(b_ga, bc(w["g_attn_out_2"].rearrange("(a d) -> a d", a=1), [P, 512])).then_inc(hyb_in, 16)
                with nc.allow_non_contiguous_dma(reason="vectors by feature"):
                    act.dma_start(col[:, 36:40], w["g_conv_out_2"].rearrange("(k p) -> p k", p=P)).then_inc(hyb_in, 16)
                    act.dma_start(col[:, 40:52].rearrange("p (a k) -> p a k", k=4), w["conv_w_2"].rearrange("a (k p) -> p a k", p=P)).then_inc(hyb_in, 16)
                norm_root(5)
                take_hT(6)
                for c in range(2):
                    take_sum(("mem_kv", c), columns(m_kT[:, 4 * c:4 * c + 4, :]))
                for c in range(2):
                    take_sum(("mem_kv", 2 + c), m_v[:, :, c * 512:(c + 1) * 512])
                take_hT(5)
                for c, dst in enumerate((columns(b_qT), columns(b_kT), b_v, columns(b_bgT), columns(b_cgT))):
                    take_sum(("w_in", c), dst)
                act.wait_ge(cms_ready, 1)
                did(A.activation(b_rs, b_rs, ACT.Sqrt), croot_ready, 1)

                def exponentials(h):
                    act.wait_ge(smax_ready, h + 1)
                    for t, (a, b) in enumerate(((0, P), (P, 384))):
                        sm = b_sm[:, h % 2, a:b]
                        did(A.activation(sm, sm, ACT.Exp, bias=hp[h % 2][:, 2 + t:3 + t], scale=HD ** -0.5), e_ready, 2 * h + t + 1)

                exponentials(0)
                for h in range(HEADS):
                    if h + 1 < HEADS:
                        exponentials(h + 1)
                    take_small(("attT", h), b_pT[:, h % 2, :], small_of(("attT", h))[:, 0:384])
                act.wait_ge(cms_ready, 2)
                did(A.activation(root[:], ms[:], ACT.Sqrt), croot_ready, 2)
                for t in range(TT):
                    take_small(("att_rows", t), b_mT[:, 0:4, t * P:(t + 1) * P], small_of(("att_rows", t))[:, :].rearrange("p (k t) -> p k t", t=P))

            def memory():
                norm_root(7)
                take_hT(7)
                for c in range(2):
                    take_sum(("q_mem", c), columns(n_qT[:, 4 * c:4 * c + 4, :]))

                def exponentials(h):
                    act.wait_ge(smax_ready, HEADS + h + 1)
                    if h >= 2:
                        act.wait_ge(*taken_small(("mattT", h - 2)))
                    for t in range(TT):
                        did(A.activation(n_p[:, h % 2, t, :], sum_of(("matt", h))[:, t, 0:S], ACT.Exp, bias=hp[h % 2][:, 2 + t:3 + t],
                                         scale=256 ** -0.5, accum_out=hp[h % 2][:, 4 + t:5 + t]), e_ready, 2 * (HEADS + h) + t + 1)

                exponentials(0)
                for h in range(MEM_HEADS):
                    if h + 1 < MEM_HEADS:
                        exponentials(h + 1)
                    take_small(("mattT", h), n_pT[:, h % 2, :, :].rearrange("p m t -> p (m t)"), small_of(("mattT", h))[:, :])
                    take_small(("matto", h), n_oT[:, 2 * h:2 * h + 2, :].rearrange("p e t -> p (e t)"), small_of(("matto", h))[:, :])

            def mlp():
                norm_root(8)
                take_hT(8)
                for c in range(8):
                    name = ("up", c)
                    act.wait_ge(sum_ready, SUM[name] + 1)
                    if c >= 2:
                        act.wait_ge(a_ready, c - 1)
                    did(A.activation(f_t[:, c % 2].rearrange("p (a b) t -> p a (b t)", b=2), sum_of(name)[:, :, :], ACT.Relu), *taken_sum(name))
                    settle()
                    act.sem_inc(relu_ready, 1)
                norm_root(9)

            act.dma_start(r_pos, bc(w["positions"], [P, S])).then_inc(rope_in, 16)
            act.dma_start(col[:, 8:9], w["inv_freq"]).then_inc(rope_in, 16)
            act.dma_start(r_decay, w["decay"].rearrange("h p i -> p h i")).then_inc(decay_in, 16)
            act.wait_ge(c_in, 16)
            act.wait_ge(ones_ready, 1)
            for k in range(KD):
                did(A.activation(c_bc[:, k, :], ones[:], ACT.Silu, scale=col[:, k:k + 1]), c_ready, k + 1)
            retention()
            if stop >= 2:
                peer(0)
            if stop >= 3:
                sgu()
            if stop >= 4:
                peer(1)
            if stop >= 5:
                hybrid()
            if stop >= 6:
                memory()
            if stop >= 7:
                mlp()


def shape_constants():
    f = np.float32
    i = np.arange(S)
    j = np.arange(S)[:, None]
    decay = np.zeros((RET_HEADS, P, 384), f)
    for h in range(RET_HEADS):
        log_gamma = np.log(1.0 - 2.0 ** (-5.0 - h))
        table = np.exp(log_gamma * np.abs(i - j)) * (j // CHUNK <= i // CHUNK) * RET_QK ** -0.5
        decay[h] = np.concatenate([table[0:P], table[P:S, P:S]], axis=1)
    q, k = np.arange(S)[:, None], np.arange(S)[None, :]
    many = np.zeros((S, S), f)
    for window, dilation in ((128, 1), (512, 4), (2048, 16)):
        many += (k <= q) & (q - k <= window) & ((q - k) % dilation == 0)
    mask = np.where(many > 0, 0.0, NEG).astype(f)
    fold = lambda m: np.ascontiguousarray(np.concatenate([m[0:P, 0:P], m[P:S]], axis=1))
    half = RET_QK // 2
    inv_freq = (1.0 / (f(ROPE_BASE) ** (np.arange(half, dtype=f) / f(half)))).astype(f)
    return {"ident": np.eye(P, dtype=f), "decay": decay, "att_mask": fold(mask), "att_many": fold(many),
            "inv_freq": inv_freq.reshape(P, 1), "iota": np.arange(TOPK, dtype=f).reshape(1, TOPK)}


INPUTS = ["x", "c", "positions", "norm_mix", "norm_ffn", "ada_w", "ada_b", "ret_w_in", "ret_w_out", "sgu_w_in",
          "sgu_b_in", "sgu_ln_g", "sgu_ln_b", "sgu_w_s", "sgu_b_s", "sgu_w_out", "peer_w_query", "peer_sub_keys",
          "peer_u", "peer_v", "norm_final", "mem_2", "g_mix_2", "w_in_2", "conv_w_2", "g_attn_out_2",
          "g_conv_out_2", "w_out_2", "g_xattn_2", "g_mem_2", "w_q_mem_2", "w_kv_mem_2", "w_o_mem_2", "g_mlp_2",
          "w_up_2", "w_down_2", "g_final_2"]


def kernel(**inputs):
    import concourse.bacc as bacc
    from concourse.bass_utils import run_bass_kernel_spmd

    nc = bacc.Bacc("TRN2", target_bir_lowering=False, num_devices=1)
    arrays = {name: np.ascontiguousarray(inputs[name]) for name in INPUTS}
    arrays.update(shape_constants())
    arrays = {f"in_{name}": a for name, a in arrays.items()}
    w = {name[3:]: nc.dram_tensor(name, a.shape, mybir.dt.from_np(a.dtype), kind="ExternalInput").ap()
         for name, a in arrays.items()}
    out = nc.dram_tensor("out", (1, S, D), F32, kind="ExternalOutput").ap()
    two_blocks(nc, w, out)
    return run_bass_kernel_spmd(nc, [arrays], core_ids=[0]).results[0]["out"]
```

```python
from contextlib import ExitStack

import numpy as np

import concourse.bass as bass
from concourse import mybir

F32 = mybir.dt.float32
F32R = mybir.dt.float32r
BF16 = mybir.dt.bfloat16
I32 = mybir.dt.int32
U32 = mybir.dt.uint32
ALU = mybir.AluOpType
ACT = mybir.ActivationFunctionType
AX_X = mybir.AxisListType.X

P = 128
D = 1024
S = 256
TT = S // P
KD = D // P
EPS = 1e-6
CHUNK = 64
RET_HEADS = 4
RET_QK = D // RET_HEADS
ROPE_BASE = 10000.0
HALF = 3072
CU = HALF // P
GROUPS = 8
PEER_HEADS = 8
TOPK = 16
NKEYS = 128
EXPERTS = NKEYS * NKEYS
PICKS = PEER_HEADS * TOPK
UNITS = TT * PEER_HEADS
HEADS = 8
HD = 64
MEM_HEADS = 4
NEG = -1e30
LOWEST = -3.0e38

R = 4
RH = 4
BN = 512
BK = 4
U_SLOTS = 4
V_SLOTS = 8
GROUP = 4

TWO_PI_1 = 6.28125
TWO_PI_2 = 0.0019350051879882812
TWO_PI_3 = float(2 * np.pi - 6.28125 - 0.0019350051879882812)
PI_SAFE = 3.1415925

NORM = {0: 0, 1: 1, 2: 2, 3: 3, 6: 4, 4: 5, 5: 6, 7: 7, 8: 8, 9: 9}


def matrices(w):
    out = [(("ada", l), w["ada_w"][l], 8, range(12)) for l in range(2)]
    out += [(("ret_in",), w["ret_w_in"][0], 8, range(12)), (("ret_out",), w["ret_w_out"][0], 16, range(2)),
            (("query", 0), w["peer_w_query"][0], 8, range(4)),
            (("sgu_v",), w["sgu_w_in"][0], 8, range(6, 12)), (("sgu_u",), w["sgu_w_in"][0], 8, range(6)),
            (("sgu_out",), w["sgu_w_out"][0], 24, range(2)),
            (("query", 1), w["peer_w_query"][1], 8, range(4)),
            (("mem_kv",), w["w_kv_mem_2"], 8, range(4)), (("w_in",), w["w_in_2"], 8, range(6)),
            (("w_out",), w["w_out_2"], 8, range(2)), (("q_mem",), w["w_q_mem_2"], 8, range(2)),
            (("o_mem",), w["w_o_mem_2"], 8, range(2)), (("up",), w["w_up_2"], 8, range(8)),
            (("down",), w["w_down_2"], 32, range(2))]
    return out


def numbered(names):
    return {name: i for i, name in enumerate(names)}


def sums_in_order():
    out = [("ada", l, c) for l in range(2) for c in range(12)]
    out += [("ret_in", c) for c in range(12)] + [("ret_y", h) for h in range(RET_HEADS)] + [("ret_out", c) for c in range(2)]
    out += [("query", 0, c) for c in range(4)] + [("peer", 0, t) for t in range(TT)]
    out += [("sgu_v", c) for c in range(6)] + [("sgu_u", c) for c in range(6)] + [("sgu_out", c) for c in range(2)]
    out += [("query", 1, c) for c in range(4)] + [("peer", 1, t) for t in range(TT)]
    out += [("w_in", c) for c in range(6)] + [("att", h) for h in range(HEADS)]
    out += [("w_out", c) for c in range(2)] + [("q_mem", c) for c in range(2)] + [("matt", h) for h in range(MEM_HEADS)]
    out += [("o_mem", c) for c in range(2)] + [("up", c) for c in range(8)] + [("down", c) for c in range(2)]
    return numbered(out)


def small_in_order():
    def turned(n):
        return [("hT", n, t, g) for t in range(TT) for g in range(2)]
    out = turned(0) + [("ret_s", h) for h in range(RET_HEADS)] + [("ygT", b) for b in range(8)]
    for l in range(2):
        out += [("keysT", l, b) for b in range(4)] + turned(1 + 2 * l)
        out += [("scores", l, 0)]
        if l == 1:
            out += turned(6)
        out += [("scores", l, i) for i in range(1, UNITS)]
        if l == 0:
            out += [("wsT", b) for b in range(2)] + [("ws_sum", b) for b in range(2)] + turned(2)
            out += [("mixed", b) for b in range(CU // 2)]
    out += turned(5) + [("conv_sq",)]
    for h in range(HEADS):
        out += [("attT", h), ("atto", h)]
    out += [("att_rows", t) for t in range(TT)] + turned(7)
    for h in range(MEM_HEADS):
        out += [("mattT", h), ("matto", h)]
    out += turned(8)
    return numbered(out)


def two_blocks(nc, w, out, stop=7):
    MATS = matrices(w)
    blocks, first_block_of = [], {}
    for name, ap, kt, ns in MATS:
        for n in ns:
            first_block_of[name + (n,)] = len(blocks)
            for kb in range(kt // BK):
                blocks.append(ap[kb * BK * P:(kb + 1) * BK * P, n * BN:(n + 1) * BN].rearrange("(k p) n -> p k n", p=P))
    SUM = sums_in_order()
    SMALL = small_in_order()

    ends_sum, mat_ends = {}, {}
    for (name, _, kt, ns) in MATS:
        for n in ns:
            label = name + (n - 6 if name == ("sgu_v",) else n,)
            last = first_block_of[name + (n,)] + kt // BK - 1
            ends_sum[last] = ("kv", n + 1) if name == ("mem_kv",) else ("sum", SUM[label] + 1)
            mat_ends[name + (n,)] = [first_block_of[name + (n,)] + kt // BK - 1]
    limit = len(blocks)
    stops = {1: ("ret_out",), 2: ("query", 0), 3: ("sgu_out",), 4: ("query", 1), 5: ("w_out",), 6: ("o_mem",)}
    if stop in stops:
        limit = max(v[0] for k, v in mat_ends.items() if k[:-1] == stops[stop]) + 1

    with ExitStack() as ctx:
        def sb(name, shape, dt=F32):
            return ctx.enter_context(nc.sbuf_tensor(name, shape, dt))

        def sem(name):
            return ctx.enter_context(nc.semaphore(name))

        mod_base = (nc.sbuf_base + 31) // 32 * 32
        mod = sb("mod", [P, 2, 3, D])
        ring_base = (nc.sbuf_base + 31) // 32 * 32
        ring = sb("ring", [P, R, BK, BN])
        arena_base = (nc.sbuf_base + 31) // 32 * 32
        ARENA = 24832
        arena = sb("arena", [P, ARENA])
        ring_low = nc.alloc_sbuf_tensor_at("ring_low", [P, R, BK, BN], F32R, offset=ring_base)
        ring_high = sb("ring_high", [P, RH, BK, BN], F32R)
        x = sb("x", [P, TT, D])
        gain_base = (nc.sbuf_base + 31) // 32 * 32
        gain = sb("gain", [P, 2, D])
        ident = sb("ident", [P, P])
        ones = sb("ones", [P, P])
        junk = sb("junk", [P, D], BF16)
        ss = sb("ss", [P, TT])
        ms = sb("ms", [P, TT])
        eps = sb("eps", [P, 2])
        root = sb("root", [P, TT])
        rstd = sb("rstd", [P, TT])
        hp = [sb("head_even", [P, 8]), sb("head_odd", [P, 8])]
        hs = hp[0]
        col = sb("col", [P, 96])

        def at(name, offset, *shape, dt=F32):
            assert offset + int(np.prod(shape)) <= ARENA, name
            return nc.alloc_sbuf_tensor_at(name, [P, *shape], dt, offset=arena_base + 4 * offset)[:]

        hT_high, hT_low = at("hT_high", 0, KD, S, dt=F32R), at("hT_low", 2048, KD, S, dt=F32R)
        hT = (hT_high, hT_low)
        m_row, m_gain = at("m_row", 0, 2, 6, D), at("m_gain", 16384, 4, D)
        c_high, c_low, c_full = at("c_high", 12288, KD, P, dt=F32R), at("c_low", 13312, KD, P, dt=F32R), at("c_full", 14336, KD, P)
        r_qT, r_kT = at("r_qT", 4096, KD, S), at("r_kT", 6144, KD, S)
        r_ygT = (at("r_yg_high", 4096, 16, S, dt=F32R), at("r_yg_low", 8192, 16, S, dt=F32R))
        r_v, r_h, r_g = at("r_v", 8192, TT, 2048), at("r_h", 8192, TT, D), at("r_g", 12288, TT, 2048)
        r_sT, r_decay = at("r_sT", 16384, RET_HEADS, 384), at("r_decay", 17920, RET_HEADS, 384)
        r_cos, r_sin, r_tmp = at("r_cos", 19456, S), at("r_sin", 19712, S), at("r_tmp", 19968, 2, 512)
        r_turn, r_int = at("r_turn", 19968, S), at("r_int", 20224, S, dt=I32)
        r_pos, r_ang = at("r_pos", 22016, S, dt=I32), at("r_ang", 22272, S)
        p_qT, p_keysT, p_keys = at("p_qT", 4096, 16, S), at("p_keysT", 8192, 16, P), at("p_keys", 14336, 16, P)
        u_buf, v_buf = at("u_buf", 10240, U_SLOTS, D), at("v_buf", 14336, V_SLOTS, D)
        p_h = nc.alloc_sbuf_tensor_at("p_h", [P, TT, D], F32, offset=gain_base)[:]
        p_tmp = at("p_tmp", 0, D)
        p_row, p_top, p_pos = at("p_row", 22528, 2, NKEYS), at("p_top", 22784, 2, TOPK), at("p_pos", 22816, 2, TOPK, dt=U32)
        p_posf = at("p_posf", 22848, 2, TOPK)
        p_cand, p_best, p_at = at("p_cand", 22880, TOPK, TOPK), at("p_best", 23136, TOPK), at("p_at", 23152, TOPK, dt=U32)
        p_ij, p_ijf, p_eq = at("p_ij", 23168, 2, TOPK, dt=U32), at("p_ijf", 23200, 2, TOPK), at("p_eq", 23232, 2, 256)
        p_i, p_ef, p_d, p_e = (at("p_i", 23744, 2, TOPK), at("p_ef", 23776, TOPK), at("p_d", 23792, TOPK),
                               at("p_e", 23808, TOPK))
        p_idx, p_gate = at("p_idx", 23824, PICKS, dt=I32), at("p_gate", 23952, PICKS)
        p_z, p_dot, p_act, p_w = (at("p_z", 24080, 8), at("p_dot", 24088, 2, GROUP), at("p_act", 24096, 2, GROUP),
                                  at("p_w", 24104, 2, GROUP))
        p_iota, p_diag = at("p_iota", 24112, TOPK), at("p_diag", 24128, 4, P)
        s_u, s_v, s_h = at("s_u", 4096, CU, S), at("s_v", 10240, TT, HALF), at("s_h", 10240, TT, D)
        s_us = (at("s_us_high", 4096, CU, S, dt=F32R), at("s_us_low", 10240, TT, CU, P, dt=F32R))
        s_vbias, s_t = at("s_vbias", 16384, HALF), at("s_t", 16384, 12, S)
        s_bs, s_wsT = at("s_bs", 19456, GROUPS, P), at("s_wsT", 20480, GROUPS, P)
        s_ws, s_wsum = at("s_ws", 21504, GROUPS, P), at("s_wsum", 21504, GROUPS, P)
        m_h = nc.alloc_sbuf_tensor_at("m_h", [P, TT, D], F32, offset=mod_base)[:]
        m_kT = nc.alloc_sbuf_tensor_at("m_kT", [P, KD, S], F32, offset=mod_base + 8192)[:]
        m_v = nc.alloc_sbuf_tensor_at("m_v", [P, TT, D], F32, offset=mod_base)[:]
        m_row_gain = nc.alloc_sbuf_tensor_at("m_row_gain", [P, D], F32, offset=mod_base + 8192)[:]
        b_h = at("b_h", 4096, TT, D)
        b_qT, b_kT, b_v = at("b_qT", 4096, 4, S), at("b_kT", 5120, 4, S), at("b_v", 6144, TT, 512)
        b_bgT, b_cgT, b_uT = at("b_bgT", 7168, 4, S), at("b_cgT", 8192, 4, S), at("b_uT", 9216, 4, 258)
        b_cv, b_sq = at("b_cv", 10248, 4, S), at("b_sq", 11272, 4, S)
        b_mT = (at("b_m_high", 12296, KD, S, dt=F32R), at("b_m_low", 14344, KD, S, dt=F32R))
        b_sm, b_p, b_pT = at("b_sm", 16392, 2, 384), at("b_p", 17160, 2, 384), at("b_pT", 17928, 2, 384)
        b_att, b_mask, b_many = at("b_att", 18696, TT, 512), at("b_mask", 19720, 384), at("b_many", 20104, 384)
        b_rs, b_ga, b_cvn = at("b_rs", 20488, S), at("b_ga", 20744, 512), b_sq
        n_qT, n_p, n_pT = at("n_qT", 6144, KD, S), at("n_p", 8192, 2, TT, S), at("n_pT", 9216, 2, TT, S)
        n_oT = (at("n_o_high", 10240, KD, S, dt=F32R), at("n_o_low", 12288, KD, S, dt=F32R))
        f_a = (at("f_a_high", 4096, 32, S, dt=F32R), at("f_a_low", 12288, 32, S, dt=F32R))
        f_t = at("f_t", 20480, 2, 4, S)
        spill = nc.dram_tensor("modulations", (2, 6, D), F32).ap()

        pair = [ctx.enter_context(nc.psum_tensor(f"pair{i}", [P, 2, 512], F32)) for i in range(3)]
        small = [ctx.enter_context(nc.psum_tensor(f"small{i}", [P, 512], F32)) for i in range(2)]

        w_in = [sem(f"w_in{i}") for i in range(R)]
        w_high, w_low = sem("w_high"), sem("w_low")
        t_high = sem("t_high")
        w_used = sem("w_used")
        sum_ready = sem("sum_ready")
        sum_taken = [sem(f"sum_taken{i}") for i in range(3)]
        small_ready = sem("small_ready")
        small_taken = [sem(f"small_taken{i}") for i in range(2)]
        x_in, c_in, cst_in, bias_in = sem("x_in"), sem("c_in"), sem("cst_in"), sem("bias_in")
        rope_in, decay_in = sem("rope_in"), sem("decay_in")
        gain_in = [sem("gain_in0"), sem("gain_in1")]
        gain_used = sem("gain_used")
        c_ready, ones_ready = sem("c_ready"), sem("ones_ready")
        x_ready, root_ready, h_ready = sem("x_ready"), sem("root_ready"), sem("h_ready")
        rows_ready, spilled, mod_used = sem("rows_ready"), sem("spilled"), sem("mod_used")
        kv_ready, kv_taken, mem_gain_in = sem("kv_ready"), sem("kv_taken"), sem("mem_gain_in")
        mod_in = [sem("mod_in0"), sem("mod_in1")]
        m_gain_in = sem("m_gain_in")
        rope_ang, rope_raw, rope_ready = sem("rope_ang"), sem("rope_raw"), sem("rope_ready")
        scores_ready = sem("scores_ready")
        y_sq, y_ms, y_root, yg_ready = sem("y_sq"), sem("y_ms"), sem("y_root"), sem("yg_ready")
        keys_in, iota_in = sem("keys_in"), sem("iota_in")
        best_ready, exp_ready, idx_ready = sem("best_ready"), sem("exp_ready"), sem("idx_ready")
        u_in = [sem(f"u_in{i}") for i in range(U_SLOTS)]
        v_in = [sem(f"v_in{i}") for i in range(V_SLOTS)]
        u_used, v_used = sem("u_used"), sem("v_used")
        act_ready, weight_ready, diag_ready = sem("act_ready"), sem("weight_ready"), sem("diag_ready")
        sgu_in, ws_zero = sem("sgu_in"), sem("ws_zero")
        v_raw, v_gelu, v_mean, v_sq, v_ms, v_root, v_ready = (sem(n) for n in (
            "v_raw", "v_gelu", "v_mean", "v_sq", "v_ms", "v_root", "v_ready"))
        us_ready, us_done = sem("us_ready"), sem("us_done")
        mem_in, hyb_in = sem("mem_in"), sem("hyb_in")
        sq_ready, cms_ready, croot_ready, mcv_ready = sem("sq_ready"), sem("cms_ready"), sem("croot_ready"), sem("mcv_ready")
        smax_ready, e_ready, p_ready = sem("smax_ready"), sem("e_ready"), sem("p_ready")
        arow_ready = sem("arow_ready")
        relu_ready, a_ready, a_low = sem("relu_ready"), sem("a_ready"), sem("a_low")
        out_ready, out_done = sem("out_ready"), sem("out_done")
        dve_step, act_step = sem("dve_step"), sem("act_step")

        def own(eng, step):
            count, pending = [0], {}

            def did(ins, signal=step, value=None):
                if signal is step:
                    count[0] += 1
                    value = count[0]
                ins.then_inc(signal, 1)
                pending[signal.name] = (signal, value)

            def settle():
                for signal, value in pending.values():
                    eng.wait_ge(signal, value)
                pending.clear()

            return did, settle

        def wait_block_free(eng, old):
            if old in ends_sum:
                which, value = ends_sum[old]
                eng.wait_ge(kv_ready if which == "kv" else sum_ready, value)
            else:
                eng.wait_ge(w_used, old + 1 - sum(e <= old for e in ends_sum))

        def block_after(mat, n):
            return min(mat_ends[mat + (n,)][0] + 2, limit - 1)

        def taken_sum(name):
            i = SUM[name]
            return sum_taken[i % 3], i // 3 + 1

        def taken_small(name):
            i = SMALL[name]
            return small_taken[i % 2], i // 2 + 1

        def sum_of(name):
            return pair[SUM[name] % 3]

        def small_of(name):
            return small[SMALL[name] % 2]

        kv_pair = (SUM[("peer", 1, 1)] + 1) % 3

        block = ctx.enter_context(nc.Block())
        bc = lambda ap, shape: ap.broadcast_to(shape)

        @block.sync
        def _(sp):
            with nc.allow_non_contiguous_dma(reason="one vector of 1024"):
                sp.dma_start(col[:, 0:KD], w["c"][0].rearrange("(k p) -> p k", p=P)).then_inc(c_in, 16)
            for i in range(limit):
                if i >= R:
                    wait_block_free(sp, i - R)
                sp.dma_start(ring[:, i % R], blocks[i]).then_inc(w_in[i % R], 16)
                if i == 1:
                    sp.dma_start(m_row[0:1].rearrange("p l a d -> p (l a d)"),
                                 w["ada_b"].rearrange("(o l) n -> o (l n)", o=1)).then_inc(bias_in, 16)
                if i == 3:
                    sp.dma_start(ident[:], w["ident"]).then_inc(cst_in, 16)
                    sp.dma_start(x[:], w["x"][0].rearrange("(t p) d -> p t d", p=P)).then_inc(x_in, 16)
            sp.wait_ge(out_ready, 1)
            src = x if stop < 7 else b_h
            sp.dma_start(out[0].rearrange("(t p) d -> p t d", p=P), src[:, :, :]).then_inc(out_done, 16)
            sp.wait_ge(out_done, 16)

        @block.gpsimd
        def _(pool):
            def load_gain(n, row):
                if n >= 2:
                    pool.wait_ge(gain_used, n - 1)
                pool.dma_start(gain[:, n % 2, :], bc(row, [P, D])).then_inc(gain_in[n % 2], 16)

            def gathers(l, t):
                for k in range(PICKS):
                    s = (l * TT + t) * PICKS + k
                    if k % TOPK == 0:
                        pool.wait_ge(idx_ready, s // TOPK + 1)
                    index = bass.IndirectOffsetOnAxis(ap=p_idx[:, k:k + 1], axis=0)
                    if s >= U_SLOTS:
                        pool.wait_ge(u_used, s - U_SLOTS + 1)
                    nc.gpsimd.indirect_dma_start(u_buf[:, s % U_SLOTS, :], None, experts_u, index)\
                        .then_inc(u_in[s % U_SLOTS], 16)
                    if s >= V_SLOTS:
                        pool.wait_ge(v_used, s - V_SLOTS + 1)
                    nc.gpsimd.indirect_dma_start(v_buf[:, s % V_SLOTS, :], None, experts_v, index)\
                        .then_inc(v_in[s % V_SLOTS], 16)

            experts_u = w["peer_u"].rearrange("l e d -> (l e) d")
            experts_v = w["peer_v"].rearrange("l e d -> (l e) d")
            def load_mod(n):
                if n >= 2:
                    pool.wait_ge(mod_used, n - 1)
                pool.dma_start(mod[:, n % 2], bc(spill[n // 2:n // 2 + 1, 3 * (n % 2):3 * (n % 2) + 3, :], [P, 3, D]))\
                    .then_inc(mod_in[n % 2], 16)

            for l in range(2):
                pool.dma_start(m_gain[0:1, 2 * l, :], w["norm_mix"][l:l + 1]).then_inc(m_gain_in, 16)
                pool.dma_start(m_gain[0:1, 2 * l + 1, :], w["norm_ffn"][l:l + 1]).then_inc(m_gain_in, 16)
            for l in range(2):
                pool.wait_ge(rows_ready, l + 1)
                pool.dma_start(spill[l:l + 1], m_row[0:1, l]).then_inc(spilled, 16)
                pool.wait_ge(spilled, 16 * (l + 1))
                if l == 0:
                    load_mod(0)
                    load_mod(1)
            if stop >= 2:
                load_mod(2)
                for t in range(TT):
                    gathers(0, t)
            if stop >= 4:
                load_mod(3)
                for t in range(TT):
                    gathers(1, t)
            if stop >= 5:
                pool.wait_ge(u_used, 2 * TT * PICKS)
                rows = (w["norm_final"], w["g_mix_2"], w["g_xattn_2"], w["g_mlp_2"], w["g_final_2"])
                for n, row in enumerate(rows[:2 if stop == 5 else 3 if stop == 6 else 5]):
                    load_gain(n, row.rearrange("(a d) -> a d", a=1))

        @block.tensor
        def _(pe):
            def open_sum(name):
                i = SUM[name]
                if i >= 3:
                    pe.wait_ge(sum_taken[i % 3], i // 3)

            def open_small(name):
                i = SMALL[name]
                if i >= 2:
                    pe.wait_ge(small_taken[i % 2], i // 2)

            def split(i):
                pe.wait_ge(w_low, i + 1)
                return ring_high[:, i % RH], ring_low[:, i % R]

            def tile_of(lhs, k, t):
                return lhs[:, t, k, :] if len(lhs.shape) == 4 else lhs[:, k, t * P:(t + 1) * P]

            def rows_product(name, mat, n, lhs, kt):
                open_sum(name)
                acc = sum_of(name)
                for kb in range(kt // BK):
                    i = first_block_of[mat + (n,)] + kb
                    high, low = split(i)
                    for t in range(TT):
                        for k in range(BK):
                            kk = kb * BK + k
                            a_high, a_low = tile_of(lhs[0], kk, t), tile_of(lhs[1], kk, t)
                            for j, (a, b) in enumerate(((a_high, high), (a_high, low), (a_low, high))):
                                mm = nc.tensor.matmul(acc[:, t, :], a, b[:, k, :],
                                                      start=(kk == 0 and j == 0), stop=(kk == kt - 1 and j == 2))
                    mm.then_inc(sum_ready if kb == kt // BK - 1 else w_used, 1)

            def columns_product(name, mat, n, rhs, kt=KD):
                open_sum(name)
                acc = sum_of(name)
                for kb in range(kt // BK):
                    i = first_block_of[mat + (n,)] + kb
                    high, low = split(i)
                    for nt in range(4):
                        for k in range(BK):
                            kk = kb * BK + k
                            n_tile = slice(nt * P, (nt + 1) * P)
                            for j, (a, b) in enumerate(((high, rhs[0]), (high, rhs[1]), (low, rhs[0]))):
                                mm = nc.tensor.matmul(acc[:, nt // 2, nt % 2 * S:(nt % 2 + 1) * S], a[:, k, n_tile], b[:, kk, :],
                                                      start=(kk == 0 and nt % 2 == 0 and j == 0), stop=(kk == kt - 1 and j == 2),
                                                      skip_group_check=True)
                    mm.then_inc(sum_ready if kb == kt // BK - 1 else w_used, 1)

            def turn_rows(n, h):
                for t in range(TT):
                    pe.wait_ge(h_ready, TT * NORM[n] + t + 1)
                    for g in range(2):
                        name = ("hT", n, t, g)
                        open_small(name)
                        for k in range(4):
                            mm = nc.tensor.transpose(small_of(name)[:, k * P:(k + 1) * P],
                                                     h[:, t, (4 * g + k) * P:(4 * g + k + 1) * P], ident[:])
                        mm.then_inc(small_ready, 1)

            def wait_hT(n):
                for t in range(TT):
                    for g in range(2):
                        pe.wait_ge(*taken_small(("hT", n, t, g)))

            def retention():
                turn_rows(0, r_h)
                wait_hT(0)
                for c in range(4):
                    columns_product(("ret_in", c), ("ret_in",), c, hT)
                for c in range(4, 12):
                    rows_product(("ret_in", c), ("ret_in",), c, hT, KD)
                for h in range(RET_HEADS):
                    name = ("ret_s", h)
                    pe.wait_ge(*taken_sum(("ret_in", h // 2)))
                    pe.wait_ge(*taken_sum(("ret_in", 2 + h // 2)))
                    pe.wait_ge(rope_ready, 4)
                    open_small(name)
                    sc = small_of(name)
                    for jt in range(TT):
                        o = sc[:, 0:S] if jt == 0 else sc[:, S:S + P]
                        for half in range(2):
                            mm = nc.tensor.matmul(o, r_kT[:, 2 * h + half, jt * P:(jt + 1) * P],
                                                  r_qT[:, 2 * h + half, jt * P:S], start=(half == 0), stop=(half == 1))
                    mm.then_inc(small_ready, 1)
                for h in range(RET_HEADS):
                    name = ("ret_y", h)
                    pe.wait_ge(scores_ready, h + 1)
                    pe.wait_ge(*taken_sum(("ret_in", 4 + h)))
                    open_sum(name)
                    acc = sum_of(name)
                    vh = r_v[:, :, h * 512:(h + 1) * 512]
                    nc.tensor.matmul(acc[:, 0, :], r_sT[:, h, 0:P], vh[:, 0, :], start=True, stop=True)
                    nc.tensor.matmul(acc[:, 1, :], r_sT[:, h, P:S], vh[:, 0, :], start=True, stop=False)
                    nc.tensor.matmul(acc[:, 1, :], r_sT[:, h, S:S + P], vh[:, 1, :], start=False, stop=True)\
                        .then_inc(sum_ready, 1)
                for b in range(8):
                    name = ("ygT", b)
                    if b % 2 == 0:
                        pe.wait_ge(yg_ready, b // 2 + 1)
                    open_small(name)
                    for q in range(4):
                        t, f = q % 2, 2 * b + q // 2
                        mm = nc.tensor.transpose(small_of(name)[:, q * P:(q + 1) * P], r_g[:, t, f * P:(f + 1) * P], ident[:])
                    mm.then_inc(small_ready, 1)
                for b in range(8):
                    pe.wait_ge(*taken_small(("ygT", b)))
                for c in range(2):
                    rows_product(("ret_out", c), ("ret_out",), c, r_ygT, 16)

            def peer(l):
                n = 1 + 2 * l
                pe.wait_ge(keys_in, 16 * (l + 1))
                for b in range(4):
                    name = ("keysT", l, b)
                    open_small(name)
                    for q in range(4):
                        mm = nc.tensor.transpose(small_of(name)[:, q * P:(q + 1) * P], p_keys[:, 4 * b + q, :], ident[:])
                    mm.then_inc(small_ready, 1)
                turn_rows(n, p_h)
                wait_hT(n)
                for b in range(4):
                    pe.wait_ge(*taken_small(("keysT", l, b)))

                def scores(i):
                    t, h = divmod(i, PEER_HEADS)
                    name = ("scores", l, i)
                    pe.wait_ge(*taken_sum(("query", l, h // 2)))
                    open_small(name)
                    for p in range(2):
                        mm = nc.tensor.matmul(small_of(name)[:, p * P:(p + 1) * P], p_qT[:, 2 * h + p, t * P:(t + 1) * P],
                                              p_keysT[:, 2 * h + p, :], start=True, stop=True)
                    mm.then_inc(small_ready, 1)

                columns_product(("query", l, 0), ("query", l), 0, hT)
                scores(0)
                for c in range(1, 4):
                    columns_product(("query", l, c), ("query", l), c, hT)
                if l == 1:
                    turn_rows(6, m_h)
                scores(1)
                for i in range(UNITS):
                    t, h = divmod(i, PEER_HEADS)
                    if i + 2 < UNITS:
                        scores(i + 2)
                    if l == 1 and i < 8:
                        memory_block(i // 2, i % 2)
                    name = ("peer", l, t)
                    if h == 0:
                        open_sum(name)
                    acc = sum_of(name)
                    for k in range(h * TOPK, (h + 1) * TOPK):
                        s = (l * TT + t) * PICKS + k
                        pe.wait_ge(diag_ready, s + 1)
                        pe.wait_ge(v_in[s % V_SLOTS], 16 * (s // V_SLOTS + 1))
                        for half in range(2):
                            mm = nc.tensor.matmul(acc[:, half, :], p_diag[:, s % 4, :],
                                                  v_buf[:, s % V_SLOTS, half * 512:(half + 1) * 512],
                                                  start=(k == 0), stop=(k == PICKS - 1))
                        mm.then_inc(v_used, 1)
                    if h == PEER_HEADS - 1:
                        pe.wait_ge(v_used, (l * TT + t + 1) * PICKS)
                        pe.sem_inc(sum_ready, 1)

            def memory_block(c, kb):
                if c == 0 and kb == 0:
                    wait_hT(6)
                    last = max(i for i in SUM.values() if i < SUM[("peer", 1, 0)] and i % 3 == kv_pair)
                    pe.wait_ge(sum_taken[kv_pair], last // 3 + 1)
                if c and kb == 0:
                    pe.wait_ge(kv_taken, c)
                acc = pair[kv_pair]
                high, low = split(first_block_of[("mem_kv", c)] + kb)
                for k in range(BK):
                    kk = kb * BK + k
                    if c < 2:
                        for nt in range(4):
                            n_tile = slice(nt * P, (nt + 1) * P)
                            for j, (a, b) in enumerate(((high, hT[0]), (high, hT[1]), (low, hT[0]))):
                                mm = nc.tensor.matmul(acc[:, nt // 2, nt % 2 * S:(nt % 2 + 1) * S], a[:, k, n_tile], b[:, kk, :],
                                                      start=(kk == 0 and nt % 2 == 0 and j == 0), stop=(kk == KD - 1 and j == 2),
                                                      skip_group_check=True)
                    else:
                        for t in range(TT):
                            a_high, a_low = tile_of(hT[0], kk, t), tile_of(hT[1], kk, t)
                            for j, (a, b) in enumerate(((a_high, high), (a_high, low), (a_low, high))):
                                mm = nc.tensor.matmul(acc[:, t, :], a, b[:, k, :], start=(kk == 0 and j == 0),
                                                      stop=(kk == KD - 1 and j == 2))
                mm.then_inc(kv_ready if kb == 1 else w_used, 1)

            def sgu():
                pe.wait_ge(sgu_in, 16 * 6)
                for b in range(2):
                    name = ("wsT", b)
                    open_small(name)
                    for q in range(4):
                        mm = nc.tensor.transpose(small_of(name)[:, q * P:(q + 1) * P], s_ws[:, 4 * b + q, :], ident[:])
                    mm.then_inc(small_ready, 1)
                pe.wait_ge(ws_zero, 1)
                for b in range(2):
                    pe.wait_ge(*taken_small(("wsT", b)))
                for b in range(2):
                    name = ("ws_sum", b)
                    open_small(name)
                    nc.tensor.matmul(small_of(name)[:, :], ones[:], s_wsT[:, 4 * b:4 * b + 4, :].rearrange("p g i -> p (g i)"),
                                     start=True, stop=True).then_inc(small_ready, 1)
                turn_rows(2, s_h)
                wait_hT(2)
                for c in range(6):
                    rows_product(("sgu_v", c), ("sgu_v",), 6 + c, hT, KD)
                for c in range(6):
                    columns_product(("sgu_u", c), ("sgu_u",), c, hT)
                pe.wait_ge(v_ready, TT)
                for b in range(CU // 2):
                    name = ("mixed", b)
                    open_small(name)
                    for q in range(2):
                        f = 2 * b + q
                        for t in range(TT):
                            mm = nc.tensor.matmul(small_of(name)[:, q * S + t * P:q * S + (t + 1) * P],
                                                  s_v[:, t, f * P:(f + 1) * P], s_wsT[:, f // (CU // GROUPS), :],
                                                  start=True, stop=True)
                    mm.then_inc(small_ready, 1)
                pe.wait_ge(us_done, 1)
                for c in range(2):
                    rows_product(("sgu_out", c), ("sgu_out",), c, s_us, CU)

            def softmax_turned(tag, h, lhs, blocks_of):
                name = (tag + "T", h)
                open_small(name)
                for q, src in enumerate(blocks_of):
                    mm = nc.tensor.transpose(small_of(name)[:, q * P:(q + 1) * P], src, ident[:])
                mm.then_inc(small_ready, 1)

            def hybrid():
                pe.wait_ge(kv_taken, 4)
                turn_rows(5, b_h)
                wait_hT(5)
                for c in range(6):
                    if c == 2:
                        rows_product(("w_in", c), ("w_in",), c, hT, KD)
                    else:
                        columns_product(("w_in", c), ("w_in",), c, hT)
                pe.wait_ge(sq_ready, 1)
                open_small(("conv_sq",))
                for q in range(4):
                    mm = nc.tensor.matmul(small_of(("conv_sq",))[:, 0:S], ones[:], b_sq[:, q, :], start=(q == 0), stop=(q == 3))
                mm.then_inc(small_ready, 1)

                def att_scores(h):
                    name = ("att", h)
                    open_sum(name)
                    acc = sum_of(name)
                    lo = h % 2 * HD
                    for t in range(TT):
                        mm = nc.tensor.matmul(acc[:, t, 0:(t + 1) * P], b_qT[lo:lo + HD, h // 2, t * P:(t + 1) * P],
                                              b_kT[lo:lo + HD, h // 2, 0:(t + 1) * P], start=True, stop=True)
                    mm.then_inc(sum_ready, 1)

                def att_out(h):
                    pe.wait_ge(p_ready, h + 1)
                    softmax_turned("att", h, None, [b_p[:, h % 2, q * P:(q + 1) * P] for q in range(3)])
                    pe.wait_ge(*taken_small(("attT", h)))
                    name = ("atto", h)
                    open_small(name)
                    o, pT = small_of(name), b_pT[:, h % 2, :]
                    vh = b_v[:, :, h * HD:(h + 1) * HD]
                    nc.tensor.matmul(o[:, 0:HD], pT[:, 0:P], vh[:, 0, :], start=True, stop=True)
                    nc.tensor.matmul(o[:, HD:2 * HD], pT[:, P:2 * P], vh[:, 0, :], start=True, stop=False)
                    nc.tensor.matmul(o[:, HD:2 * HD], pT[:, 2 * P:3 * P], vh[:, 1, :], start=False, stop=True)\
                        .then_inc(small_ready, 1)

                for c in range(2):
                    pe.wait_ge(*taken_sum(("w_in", c)))
                for h in range(HEADS):
                    att_scores(h)
                    if h == 0:
                        pe.wait_ge(*taken_sum(("w_in", 2)))
                    if h >= 1:
                        att_out(h - 1)
                att_out(HEADS - 1)
                for t in range(TT):
                    pe.wait_ge(arow_ready, t + 1)
                    name = ("att_rows", t)
                    open_small(name)
                    for q in range(4):
                        mm = nc.tensor.transpose(small_of(name)[:, q * P:(q + 1) * P], b_att[:, t, q * P:(q + 1) * P], ident[:])
                    mm.then_inc(small_ready, 1)
                for t in range(TT):
                    pe.wait_ge(*taken_small(("att_rows", t)))
                pe.wait_ge(mcv_ready, 2)
                for c in range(2):
                    rows_product(("w_out", c), ("w_out",), c, b_mT, KD)

            def memory():
                turn_rows(7, b_h)
                wait_hT(7)
                for c in range(2):
                    columns_product(("q_mem", c), ("q_mem",), c, hT)

                def scores(h):
                    name = ("matt", h)
                    open_sum(name)
                    acc = sum_of(name)
                    for t in range(TT):
                        for e in range(2):
                            mm = nc.tensor.matmul(acc[:, t, 0:S], n_qT[:, 2 * h + e, t * P:(t + 1) * P],
                                                  m_kT[:, 2 * h + e, :], start=(e == 0), stop=(e == 1))
                    mm.then_inc(sum_ready, 1)

                def attend(h):
                    pe.wait_ge(p_ready, HEADS + h + 1)
                    softmax_turned("matt", h, None, [n_p[:, h % 2, t, m * P:(m + 1) * P] for m in range(2) for t in range(TT)])
                    pe.wait_ge(*taken_small(("mattT", h)))
                    name = ("matto", h)
                    open_small(name)
                    for e in range(2):
                        for m in range(2):
                            mm = nc.tensor.matmul(small_of(name)[:, e * S:(e + 1) * S],
                                                  m_v[:, m, h * S + e * P:h * S + (e + 1) * P], n_pT[:, h % 2, m, :],
                                                  start=(m == 0), stop=(m == 1))
                    mm.then_inc(small_ready, 1)

                for c in range(2):
                    pe.wait_ge(*taken_sum(("q_mem", c)))
                for h in range(MEM_HEADS):
                    scores(h)
                    if h >= 1:
                        attend(h - 1)
                attend(MEM_HEADS - 1)
                for h in range(MEM_HEADS):
                    pe.wait_ge(*taken_small(("matto", h)))
                for c in range(2):
                    rows_product(("o_mem", c), ("o_mem",), c, n_oT, KD)

            def mlp():
                turn_rows(8, b_h)
                wait_hT(8)
                for c in range(8):
                    columns_product(("up", c), ("up",), c, hT)
                pe.wait_ge(a_low, 8)
                for c in range(2):
                    rows_product(("down", c), ("down",), c, f_a, 32)

            pe.wait_ge(c_ready, 2)
            for l in range(2):
                for c in range(12):
                    name = ("ada", l, c)
                    open_sum(name)
                    for kb in range(2):
                        i = first_block_of[("ada", l, c)] + kb
                        high, low = split(i)
                        for k in range(BK):
                            kk = kb * BK + k
                            for j, (a, b) in enumerate(((c_high, high), (c_high, low), (c_low, high))):
                                mm = nc.tensor.matmul(sum_of(name)[:, 0, :], a[:, kk, :], b[:, k, :],
                                                      start=(kk == 0 and j == 0), stop=(kk == KD - 1 and j == 2))
                        mm.then_inc(sum_ready if kb == 1 else w_used, 1)
            pe.wait_ge(cst_in, 16)
            pe.wait_ge(ones_ready, 2)
            retention()
            if stop >= 2:
                peer(0)
            if stop >= 3:
                sgu()
            if stop >= 4:
                peer(1)
            if stop >= 5:
                hybrid()
            if stop >= 6:
                memory()
            if stop >= 7:
                mlp()

        @block.vector
        def _(dve):
            did, settle = own(dve, dve_step)
            V = nc.vector

            split_blocks = [0]

            def lows(upto):
                while split_blocks[0] <= upto:
                    i = split_blocks[0]
                    dve.wait_ge(w_high, i + 1)
                    did(V.tensor_tensor(ring_low[:, i % R], ring[:, i % R], ring_high[:, i % RH].bitcast(F32), ALU.subtract),
                        w_low, i + 1)
                    split_blocks[0] += 1

            lowered = [0]

            def low_of(dst, high, full, name=None):
                lowered[0] += 1
                dve.wait_ge(t_high, lowered[0])
                did(V.tensor_tensor(dst, full, high.bitcast(F32), ALU.subtract), *(taken_small(name) if name else (dve_step, None)))

            def lows_hT(n):
                for t in range(TT):
                    for g in range(2):
                        name = ("hT", n, t, g)
                        part = (slice(None), slice(4 * g, 4 * g + 4), slice(t * P, (t + 1) * P))
                        low_of(hT_low[part], hT_high[part], small_of(name)[:, :].rearrange("p (k t) -> p k t", t=P), name)

            def norm(n, src, dst, scale, shift=None, gain_row=None, tmp=None):
                i = NORM[n]
                tmp = dst if tmp is None else tmp
                settle()
                if n == 6:
                    dve.wait_ge(mem_in, 16)
                    dve.wait_ge(mem_gain_in, 16)
                dve.sem_inc(x_ready, 1)
                if gain_row is not None:
                    dve.wait_ge(gain_in[gain_row % 2], 16 * (gain_row // 2 + 1))
                if n != 6:
                    for t in range(TT):
                        did(V.tensor_tensor(tmp[:, t, :], src[:, t, :], scale, ALU.mult))
                    settle()
                if gain_row is not None:
                    dve.sem_inc(gain_used, 1)
                dve.wait_ge(root_ready, i + 1)
                did(V.reciprocal(rstd[:], root[:]))
                settle()
                for t in range(TT):
                    if n == 6:
                        ins = V.scalar_tensor_tensor(out=dst[:, t, :], in0=src[:, t, :], scalar=rstd[:, t:t + 1], in1=scale,
                                                     op0=ALU.mult, op1=ALU.mult)
                    elif shift is None:
                        ins = V.tensor_scalar(dst[:, t, :], tmp[:, t, :], rstd[:, t:t + 1], None, ALU.mult)
                    else:
                        ins = V.scalar_tensor_tensor(out=dst[:, t, :], in0=tmp[:, t, :], scalar=rstd[:, t:t + 1], in1=shift,
                                                     op0=ALU.mult, op1=ALU.add)
                    did(ins, h_ready, TT * i + t + 1)

            def add_product(name, c, tmp, gate=None):
                dve.wait_ge(sum_ready, SUM[name] + 1)
                acc = sum_of(name)
                xc = x[:, :, c * 512:(c + 1) * 512]
                if gate is None:
                    did(V.tensor_tensor(xc, xc, acc[:, :, :], ALU.add), *taken_sum(name))
                else:
                    did(V.tensor_tensor(tmp, acc[:, :, :], bc(gate[:, c * 512:(c + 1) * 512].unsqueeze(1), [P, TT, 512]), ALU.mult),
                        *taken_sum(name))
                    settle()
                    did(V.tensor_tensor(xc, xc, tmp, ALU.add))
                settle()

            def sublayer_done():
                dve.sem_inc(mod_used, 1)

            def modulations():
                dve.wait_ge(c_ready, 1)
                did(V.tensor_tensor(c_low, c_full, c_high.bitcast(F32), ALU.subtract), c_ready, 2)
                dve.wait_ge(bias_in, 16)
                for l in range(2):
                    flat = m_row[0:1, l].rearrange("p a d -> p (a d)")
                    for c in range(12):
                        name = ("ada", l, c)
                        lows(block_after(("ada", l), c))
                        dve.wait_ge(sum_ready, SUM[name] + 1)
                        did(V.tensor_tensor(flat[:, c * BN:(c + 1) * BN], sum_of(name)[0:1, 0, :],
                                            flat[:, c * BN:(c + 1) * BN], ALU.add), *taken_sum(name))
                    settle()
                    dve.wait_ge(m_gain_in, 64)
                    for j, part in enumerate((1, 4)):
                        did(V.scalar_tensor_tensor(out=m_row[0:1, l, part, :], in0=m_row[0:1, l, part, :], scalar=1.0,
                                                   in1=m_gain[0:1, 2 * l + j, :], op0=ALU.add, op1=ALU.mult))
                    settle()
                    dve.sem_inc(rows_ready, 1)

            def rotary_tables():
                dve.wait_ge(rope_in, 32)
                did(V.tensor_copy(r_ang, r_pos))
                settle()
                did(V.tensor_scalar(r_ang, r_ang, col[:, 8:9], None, ALU.mult))
                settle()
                did(V.tensor_scalar(r_int, r_ang, float(1 / (2 * np.pi)), None, ALU.mult))
                settle()
                did(V.tensor_copy(r_turn, r_int))
                settle()
                for part in (TWO_PI_1, TWO_PI_2, TWO_PI_3):
                    did(V.scalar_tensor_tensor(out=r_ang, in0=r_turn, scalar=-part, in1=r_ang, op0=ALU.mult, op1=ALU.add))
                    settle()
                did(V.tensor_scalar(r_ang, r_ang, PI_SAFE, -PI_SAFE, ALU.min, ALU.max), rope_ang, 1)
                dve.wait_ge(rope_raw, 2)
                did(V.tensor_tensor(r_turn, r_cos, r_cos, ALU.mult))
                settle()
                did(V.tensor_scalar(r_cos, r_turn, -2.0, 1.0, ALU.mult, ALU.add))
                settle()

            def rotate(c):
                name = ("ret_in", c)
                dve.wait_ge(sum_ready, SUM[name] + 1)
                acc = sum_of(name)
                dst = r_qT if c < 2 else r_kT
                x1, x2 = acc[:, :, 0:S], acc[:, :, S:2 * S]
                both = [P, 2, S]
                cs, sn = bc(r_cos.unsqueeze(1), both), bc(r_sin.unsqueeze(1), both)
                d = dst.rearrange("p (h e) t -> p h e t", e=2)[:, 2 * (c % 2):2 * (c % 2) + 2]
                ta = r_tmp[:, 0, :].rearrange("p (h t) -> p h t", t=S)
                tb = r_tmp[:, 1, :].rearrange("p (h t) -> p h t", t=S)
                did(V.tensor_tensor(ta, x2, sn, ALU.mult))
                did(V.tensor_tensor(tb, x2, cs, ALU.mult))
                did(V.tensor_tensor(d[:, :, 0, :], x1, cs, ALU.mult))
                did(V.tensor_tensor(d[:, :, 1, :], x1, sn, ALU.mult), *taken_sum(name))
                settle()
                did(V.tensor_tensor(d[:, :, 0, :], d[:, :, 0, :], ta, ALU.subtract))
                did(V.tensor_tensor(d[:, :, 1, :], d[:, :, 1, :], tb, ALU.add), rope_ready, c + 1)
                settle()

            def retention():
                dve.wait_ge(x_in, 16)
                rotary_tables()
                dve.wait_ge(spilled, 32)
                dve.wait_ge(mod_in[0], 16)
                norm(0, x, r_h, mod[:, 0, 1, :], mod[:, 0, 0, :])
                lows_hT(0)
                for c in range(12):
                    lows(block_after(("ret_in",), c))
                    if c < 4:
                        rotate(c)
                dve.wait_ge(decay_in, 16)
                for h in range(RET_HEADS):
                    name = ("ret_s", h)
                    dve.wait_ge(small_ready, SMALL[name] + 1)
                    did(V.tensor_tensor(r_sT[:, h, :], small_of(name)[:, 0:384], r_decay[:, h, :], ALU.mult),
                        *taken_small(name))
                    settle()
                    dve.sem_inc(scores_ready, 1)
                for h in range(RET_HEADS):
                    dve.wait_ge(y_sq, 2 * (h + 1))
                    did(V.tensor_scalar(hs[:, 2:4], hs[:, 0:2], 1.0 / 512, EPS, ALU.mult, ALU.add), y_ms, h + 1)
                    dve.wait_ge(y_root, h + 1)
                    did(V.reciprocal(hs[:, 6:8], hs[:, 4:6]))
                    settle()
                    dve.wait_ge(*taken_sum(("ret_in", 8 + h)))
                    name = ("ret_y", h)
                    for t in range(TT):
                        g = r_g[:, t, h * 512:(h + 1) * 512]
                        ins = V.scalar_tensor_tensor(out=g, in0=sum_of(name)[:, t, :], scalar=hs[:, 6 + t:7 + t], in1=g,
                                                     op0=ALU.mult, op1=ALU.mult)
                        did(ins, *(taken_sum(name) if t else (dve_step, None)))
                    settle()
                    dve.sem_inc(yg_ready, 1)
                for b in range(8):
                    name = ("ygT", b)
                    low_of(r_ygT[1][:, 2 * b:2 * b + 2, :].rearrange("p f t -> p (f t)"),
                           r_ygT[0][:, 2 * b:2 * b + 2, :].rearrange("p f t -> p (f t)"), small_of(name)[:, :], name)
                for c in range(2):
                    lows(block_after(("ret_out",), c))
                    add_product(("ret_out", c), c, r_tmp[:, :, :], mod[:, 0, 2, :])
                sublayer_done()

            def first_level(l, t, h):
                name = ("scores", l, t * PEER_HEADS + h)
                dve.wait_ge(small_ready, SMALL[name] + 1)
                for p in range(2):
                    srow, rest = small_of(name)[:, p * P:(p + 1) * P], p_row[:, p, :]
                    top, pos = p_top[:, p, :], p_pos[:, p, :]
                    did(V.max(top[:, 0:8], srow))
                    settle()
                    did(V.max_index(pos[:, 0:8], top[:, 0:8], srow))
                    settle()
                    did(V.match_replace(rest, top[:, 0:8], srow, LOWEST), *(taken_small(name) if p else (dve_step, None)))
                    settle()
                    did(V.max(top[:, 8:16], rest))
                    settle()
                    did(V.max_index(pos[:, 8:16], top[:, 8:16], rest))
                settle()

            def second_level(l, t, h):
                sq = [P, TOPK, TOPK]
                did(V.tensor_copy(p_posf, p_pos))
                did(V.tensor_tensor(p_cand, bc(p_top[:, 0, :].unsqueeze(2), sq), bc(p_top[:, 1, :].unsqueeze(1), sq), ALU.add))
                settle()
                cand = p_cand.rearrange("p a b -> p (a b)")
                did(V.max(p_best[:, 0:8], cand))
                settle()
                did(V.max_index(p_at[:, 0:8], p_best[:, 0:8], cand))
                settle()
                did(V.match_replace(cand, p_best[:, 0:8], cand, LOWEST))
                settle()
                did(V.max(p_best[:, 8:16], cand))
                settle()
                did(V.max_index(p_at[:, 8:16], p_best[:, 8:16], cand))
                settle()
                did(V.tensor_scalar(p_d, p_best, p_best[:, 0:1], None, ALU.subtract), best_ready, (l * TT + t) * 8 + h + 1)

            def choose(l, t, h):
                sq = [P, TOPK, TOPK]
                did(V.tensor_scalar(p_ij[:, 0, :], p_at, 4, None, ALU.logical_shift_right))
                did(V.tensor_scalar(p_ij[:, 1, :], p_at, 15, None, ALU.bitwise_and))
                settle()
                did(V.tensor_copy(p_ijf, p_ij))
                settle()
                for p in range(2):
                    eq = p_eq[:, p, :].rearrange("p (a b) -> p a b", b=TOPK)
                    did(V.tensor_tensor(eq, bc(p_ijf[:, p, :].unsqueeze(2), sq), bc(p_iota.unsqueeze(1), sq), ALU.is_equal))
                settle()
                for p in range(2):
                    eq = p_eq[:, p, :].rearrange("p (a b) -> p a b", b=TOPK)
                    did(V.tensor_tensor(eq, eq, bc(p_posf[:, p, :].unsqueeze(1), sq), ALU.mult))
                settle()
                did(V.tensor_reduce(p_i.rearrange("p a b -> p (a b)"), p_eq.rearrange("p a (b c) -> p (a b) c", c=TOPK), AX_X, ALU.add))
                settle()
                did(V.tensor_scalar(p_ef, p_i[:, 0, :], float(NKEYS), float(l * EXPERTS), ALU.mult, ALU.add))
                settle()
                did(V.tensor_tensor(p_idx[:, h * TOPK:(h + 1) * TOPK], p_ef, p_i[:, 1, :], ALU.add),
                    idx_ready, (l * TT + t) * 8 + h + 1)

            def gates(l, t, h):
                unit = (l * TT + t) * 8 + h
                dve.wait_ge(exp_ready, unit + 1)
                did(V.tensor_reduce(p_z[:, 0:1], p_e, AX_X, ALU.add))
                settle()
                did(V.reciprocal(p_z[:, 1:2], p_z[:, 0:1]))
                settle()
                did(V.tensor_scalar(p_gate[:, h * TOPK:(h + 1) * TOPK], p_e, p_z[:, 1:2], None, ALU.mult))
                settle()

            def group(l, t, q):
                for k in range(q * GROUP, (q + 1) * GROUP):
                    s = (l * TT + t) * PICKS + k
                    dve.wait_ge(u_in[s % U_SLOTS], 16 * (s // U_SLOTS + 1))
                    ub = u_buf[:, s % U_SLOTS, :]
                    did(V.tensor_tensor_reduce(out=ub, in0=ub, in1=p_h[:, t, :], scale=1.0, scalar=0.0, op0=ALU.mult,
                                               op1=ALU.add, accum_out=p_dot[:, q % 2, k % GROUP:k % GROUP + 1]), u_used, s + 1)
                n = (l * TT + t) * (PICKS // GROUP) + q
                dve.wait_ge(act_ready, n + 1)
                did(V.tensor_tensor(p_w[:, q % 2, :], p_act[:, q % 2, :], p_gate[:, q * GROUP:(q + 1) * GROUP], ALU.mult),
                    weight_ready, n + 1)

            def peer(l):
                n = 1 + 2 * l
                dve.wait_ge(mod_in[1], 16 * (l + 1))
                norm(n, x, p_h, mod[:, 1, 1, :], mod[:, 1, 0, :])
                lows_hT(n)
                lows(block_after(("query", l), 0))
                dve.wait_ge(iota_in, 16 * (l + 1))
                units = [divmod(i, PEER_HEADS) for i in range(UNITS)]
                first_level(l, 0, 0)
                second_level(l, 0, 0)
                choose(l, 0, 0)
                lows(block_after(("query", l), 1))
                gates(l, 0, 0)
                for c in range(2, 4):
                    lows(block_after(("query", l), c))
                if l == 1:
                    norm(6, m_h, m_h, m_row_gain)
                    lows_hT(6)
                for i in range(UNITS):
                    t, h = units[i]
                    nxt = units[i + 1] if i + 1 < UNITS else None
                    if l == 1 and i < 8:
                        lows(min(first_block_of[("mem_kv", 0)] + i + 2, limit - 1))
                    for g in range(4):
                        group(l, t, h * 4 + g)
                        if g == 0 and nxt:
                            first_level(l, *nxt)
                            second_level(l, *nxt)
                        if g == 1 and nxt:
                            choose(l, *nxt)
                        if g == 3 and nxt:
                            gates(l, *nxt)
                    if i == PEER_HEADS:
                        add_experts(l, 0)
                add_experts(l, 1)
                sublayer_done()

            def add_experts(l, t):
                name = ("peer", l, t)
                dve.wait_ge(sum_ready, SUM[name] + 1)
                did(V.tensor_tensor(p_tmp.rearrange("p (a b) -> p a b", b=512), sum_of(name)[:, :, :],
                                    mod[:, 1, 2, :].rearrange("p (a b) -> p a b", b=512), ALU.mult), *taken_sum(name))
                settle()
                did(V.tensor_tensor(x[:, t, :], x[:, t, :], p_tmp, ALU.add))
                settle()

            def us_low(b):
                high = s_us[0][:, 2 * b:2 * b + 2, :].rearrange("p f (t i) -> p t f i", i=P)
                us = s_t[:, 4 + 2 * (b % 2):6 + 2 * (b % 2), :].rearrange("p f (t i) -> p t f i", i=P)
                low_of(s_us[1][:, :, 2 * b:2 * b + 2, :], high, us)

            def sgu():
                did(V.memset(s_wsT[CHUNK:P, :, 0:CHUNK], 0.0), ws_zero, 1)
                dve.wait_ge(mod_in[0], 32)
                norm(2, x, s_h, mod[:, 0, 1, :], mod[:, 0, 0, :])
                lows_hT(2)
                dve.wait_ge(sgu_in, 16 * 6)
                for c in range(6):
                    name = ("sgu_v", c)
                    lows(block_after(("sgu_v",), 6 + c))
                    dve.wait_ge(sum_ready, SUM[name] + 1)
                    vc = s_v[:, :, c * BN:(c + 1) * BN]
                    did(V.tensor_tensor(vc, sum_of(name)[:, :, :], bc(s_vbias[:, c * BN:(c + 1) * BN].unsqueeze(1), [P, TT, BN]), ALU.add),
                        *taken_sum(name))
                    settle()
                    dve.sem_inc(v_raw, 1)
                lows(block_after(("sgu_u",), 0))
                dve.wait_ge(v_gelu, 6)
                for t in range(TT):
                    did(V.tensor_reduce(hs[:, t:t + 1], s_v[:, t, :], AX_X, ALU.add))
                settle()
                lows(block_after(("sgu_u",), 1))
                did(V.tensor_scalar(hs[:, 2:4], hs[:, 0:2], -1.0 / HALF, None, ALU.mult))
                settle()
                for t in range(TT):
                    did(V.tensor_scalar(s_v[:, t, :], s_v[:, t, :], hs[:, 2 + t:3 + t], None, ALU.add))
                settle()
                lows(block_after(("sgu_u",), 2))
                for t in range(TT):
                    did(V.tensor_tensor_reduce(out=s_t.rearrange("p a b -> p (a b)"), in0=s_v[:, t, :], in1=s_v[:, t, :],
                                               scale=1.0, scalar=0.0, op0=ALU.mult, op1=ALU.add, accum_out=hs[:, 4 + t:5 + t]))
                    settle()
                lows(block_after(("sgu_u",), 3))
                did(V.tensor_scalar(ms[:], hs[:, 4:6], 1.0 / HALF, EPS, ALU.mult, ALU.add), v_ms, 1)
                lows(block_after(("sgu_u",), 4))
                dve.wait_ge(v_root, 1)
                did(V.reciprocal(rstd[:], root[:]))
                settle()
                for t in range(TT):
                    did(V.tensor_scalar(s_v[:, t, :], s_v[:, t, :], rstd[:, t:t + 1], None, ALU.mult), v_ready, t + 1)
                lows(block_after(("sgu_u",), 5))
                for b in range(CU // 2):
                    name = ("mixed", b)
                    for q in range(2):
                        f = 2 * b + q
                        g = f // (CU // GROUPS)
                        did(V.scalar_tensor_tensor(out=s_t[:, q, 0:P], in0=s_wsum[:, g, :], scalar=col[:, 56 + f:57 + f],
                                                   in1=s_bs[:, g, :], op0=ALU.mult, op1=ALU.add))
                    settle()
                    dve.wait_ge(small_ready, SMALL[name] + 1)
                    for q in range(2):
                        f = 2 * b + q
                        ins = V.scalar_tensor_tensor(out=s_t[:, 2 + q, :].rearrange("p (t i) -> p t i", i=P),
                                                     in0=small_of(name)[:, q * S:(q + 1) * S].rearrange("p (t i) -> p t i", i=P),
                                                     scalar=col[:, 32 + f:33 + f],
                                                     in1=bc(s_t[:, q, 0:P].unsqueeze(1), [P, TT, P]), op0=ALU.mult, op1=ALU.add)
                        did(ins, *((dve_step, None) if q == 0 else taken_small(name)))
                    settle()
                    if b % 2 == 0:
                        dve.wait_ge(*taken_sum(("sgu_u", b // 2)))
                    us = s_t[:, 4 + 2 * (b % 2):6 + 2 * (b % 2), :]
                    did(V.tensor_tensor(us, s_u[:, 2 * b:2 * b + 2, :], s_t[:, 2:4, :], ALU.mult), us_ready, b + 1)
                    if b:
                        us_low(b - 1)
                us_low(CU // 2 - 1)
                for c in range(2):
                    if c == 0:
                        settle()
                        dve.sem_inc(us_done, 1)
                    lows(block_after(("sgu_out",), c))
                    add_product(("sgu_out", c), c, s_vbias[:, 0:1024].rearrange("p (a b) -> p a b", b=512), mod[:, 0, 2, :])
                sublayer_done()

            def hybrid():
                norm(4, x, x, gain[:, 0, :], gain_row=0, tmp=b_h)
                norm(5, x, b_h, gain[:, 1, :], gain_row=1)
                lows_hT(5)
                for c in range(6):
                    lows(block_after(("w_in",), c))
                did(V.memset(b_uT[:, :, 0:2], 0.0))
                dve.wait_ge(hyb_in, 16 * 5)
                name = ("w_in", 5)
                dve.wait_ge(sum_ready, SUM[name] + 1)
                dve.wait_ge(*taken_sum(("w_in", 4)))
                did(V.tensor_tensor(b_uT[:, :, 2:258], sum_of(name)[:, :, :].rearrange("p a (b t) -> p (a b) t", t=S), b_cgT, ALU.mult),
                    *taken_sum(name))
                settle()
                for q in range(4):
                    did(V.tensor_scalar(b_cv[:, q, :], b_uT[:, q, 0:S], col[:, 40 + q:41 + q], None, ALU.mult))
                settle()
                for tap in (1, 2):
                    for q in range(4):
                        did(V.scalar_tensor_tensor(out=b_cv[:, q, :], in0=b_uT[:, q, tap:tap + S],
                                                   scalar=col[:, 40 + 4 * tap + q:41 + 4 * tap + q], in1=b_cv[:, q, :],
                                                   op0=ALU.mult, op1=ALU.add))
                    settle()
                dve.wait_ge(*taken_sum(("w_in", 3)))
                did(V.tensor_tensor(b_cv, b_cv, b_bgT, ALU.mult))
                settle()
                did(V.tensor_tensor(b_sq, b_cv, b_cv, ALU.mult), sq_ready, 1)
                name = ("conv_sq",)
                dve.wait_ge(small_ready, SMALL[name] + 1)
                did(V.tensor_scalar(b_rs, small_of(name)[:, 0:S], 1.0 / 512, EPS, ALU.mult, ALU.add), *taken_small(name))
                settle()
                dve.sem_inc(cms_ready, 1)
                dve.wait_ge(croot_ready, 1)
                did(V.reciprocal(b_rs, b_rs))
                settle()
                for q in range(4):
                    did(V.scalar_tensor_tensor(out=b_cvn[:, q, :], in0=b_cv[:, q, :], scalar=col[:, 36 + q:37 + q], in1=b_rs,
                                               op0=ALU.mult, op1=ALU.mult))
                settle()
                dve.sem_inc(mcv_ready, 1)
                low_of(b_mT[1][:, 4:8, :], b_mT[0][:, 4:8, :], b_cvn)
                settle()
                dve.sem_inc(mcv_ready, 1)

                def att_max(h):
                    name = ("att", h)
                    dve.wait_ge(sum_ready, SUM[name] + 1)
                    acc = sum_of(name)
                    sm = b_sm[:, h % 2, :]
                    did(V.tensor_tensor(sm[:, 0:P], acc[:, 0, 0:P], b_mask[:, 0:P], ALU.add))
                    did(V.tensor_tensor(sm[:, P:384], acc[:, 1, 0:S], b_mask[:, P:384], ALU.add), *taken_sum(name))
                    settle()
                    did(V.tensor_reduce(hp[h % 2][:, 0:1], sm[:, 0:P], AX_X, ALU.max))
                    did(V.tensor_reduce(hp[h % 2][:, 1:2], sm[:, P:384], AX_X, ALU.max))
                    settle()
                    did(V.tensor_scalar(hp[h % 2][:, 2:4], hp[h % 2][:, 0:2], -(HD ** -0.5), None, ALU.mult), smax_ready, h + 1)

                def att_sum(h):
                    dve.wait_ge(e_ready, 2 * (h + 1))
                    for t, (a, b) in enumerate(((0, P), (P, 384))):
                        e = b_sm[:, h % 2, a:b]
                        did(V.tensor_tensor_reduce(out=b_p[:, h % 2, a:b], in0=e, in1=b_many[:, a:b], scale=1.0, scalar=0.0,
                                                   op0=ALU.mult, op1=ALU.add, accum_out=hp[h % 2][:, 4 + t:5 + t]), *((dve_step, None) if t == 0 else (p_ready, h + 1)))
                    settle()
                    did(V.reciprocal(hp[h % 2][:, 6:8], hp[h % 2][:, 4:6]))
                    settle()

                def att_take(h):
                    name = ("atto", h)
                    dve.wait_ge(small_ready, SMALL[name] + 1)
                    for t in range(TT):
                        did(V.tensor_scalar(b_att[:, t, h * HD:(h + 1) * HD], small_of(name)[:, t * HD:(t + 1) * HD],
                                            hp[h % 2][:, 6 + t:7 + t], None, ALU.mult), *((dve_step, None) if t == 0 else taken_small(name)))
                    settle()

                att_max(0)
                for h in range(HEADS):
                    att_sum(h)
                    if h + 1 < HEADS:
                        att_max(h + 1)
                    att_take(h)
                for t in range(TT):
                    did(V.tensor_tensor_reduce(out=b_sq.rearrange("p a b -> p (a b)")[:, t * 512:(t + 1) * 512], in0=b_att[:, t, :], in1=b_att[:, t, :],
                                               scale=1.0, scalar=0.0, op0=ALU.mult, op1=ALU.add, accum_out=hs[:, t:t + 1]))
                settle()
                did(V.tensor_scalar(ms[:], hs[:, 0:2], 1.0 / 512, EPS, ALU.mult, ALU.add))
                settle()
                dve.sem_inc(cms_ready, 1)
                dve.wait_ge(croot_ready, 2)
                did(V.reciprocal(rstd[:], root[:]))
                settle()
                for t in range(TT):
                    did(V.scalar_tensor_tensor(out=b_att[:, t, :], in0=b_att[:, t, :], scalar=rstd[:, t:t + 1], in1=b_ga,
                                               op0=ALU.mult, op1=ALU.mult), arow_ready, t + 1)
                for t in range(TT):
                    name = ("att_rows", t)
                    low_of(b_mT[1][:, 0:4, t * P:(t + 1) * P], b_mT[0][:, 0:4, t * P:(t + 1) * P],
                           small_of(name)[:, :].rearrange("p (k t) -> p k t", t=P), name)
                for c in range(2):
                    lows(block_after(("w_out",), c))
                    add_product(("w_out", c), c, None)

            def memory():
                norm(7, x, b_h, gain[:, 0, :], gain_row=2)
                lows_hT(7)
                for c in range(2):
                    lows(block_after(("q_mem",), c))

                def head_max(h):
                    name, hm = ("matt", h), hp[h % 2]
                    dve.wait_ge(sum_ready, SUM[name] + 1)
                    did(V.tensor_reduce(hm[:, 0:2], sum_of(name)[:, :, 0:S], AX_X, ALU.max))
                    settle()
                    did(V.tensor_scalar(hm[:, 2:4], hm[:, 0:2], -(256 ** -0.5), None, ALU.mult), smax_ready, HEADS + h + 1)

                head_max(0)
                for h in range(MEM_HEADS):
                    name, hm = ("matt", h), hp[h % 2]
                    dve.wait_ge(e_ready, 2 * (HEADS + h + 1))
                    dve.sem_inc(taken_sum(name)[0], 1)
                    did(V.reciprocal(hm[:, 6:8], hm[:, 4:6]))
                    settle()
                    for t in range(TT):
                        did(V.tensor_scalar(n_p[:, h % 2, t, :], n_p[:, h % 2, t, :], hm[:, 6 + t:7 + t], None, ALU.mult),
                            *((dve_step, None) if t == 0 else (p_ready, HEADS + h + 1)))
                    settle()
                    if h + 1 < MEM_HEADS:
                        head_max(h + 1)
                    name = ("matto", h)
                    low_of(n_oT[1][:, 2 * h:2 * h + 2, :].rearrange("p e t -> p (e t)"),
                           n_oT[0][:, 2 * h:2 * h + 2, :].rearrange("p e t -> p (e t)"), small_of(name)[:, :], name)
                for c in range(2):
                    lows(block_after(("o_mem",), c))
                    add_product(("o_mem", c), c, None)

            def mlp():
                norm(8, x, b_h, gain[:, 1, :], gain_row=3)
                lows_hT(8)
                for c in range(8):
                    lows(block_after(("up",), c))
                    dve.wait_ge(relu_ready, c + 1)
                    did(V.tensor_tensor(f_t[:, c % 2], f_t[:, c % 2], f_t[:, c % 2], ALU.mult), a_ready, c + 1)
                    low_of(f_a[1][:, 4 * c:4 * c + 4, :], f_a[0][:, 4 * c:4 * c + 4, :], f_t[:, c % 2])
                    settle()
                    dve.sem_inc(a_low, 1)
                for c in range(2):
                    lows(block_after(("down",), c))
                    add_product(("down", c), c, None)
                norm(9, x, b_h, gain[:, 0, :], gain_row=4)

            did(V.memset(ones[:], 1.0), ones_ready, 1)
            did(V.memset(eps[:], EPS), ones_ready, 2)
            modulations()
            retention()
            if stop >= 2:
                peer(0)
            if stop >= 3:
                sgu()
            if stop >= 4:
                peer(1)
            if stop >= 5:
                hybrid()
            if stop >= 6:
                memory()
            if stop >= 7:
                mlp()
            settle()
            dve.sem_inc(out_ready, 1)

        @block.scalar
        def _(act):
            did, settle = own(act, act_step)
            A = nc.scalar

            split_blocks = [0]

            def highs(upto):
                while split_blocks[0] <= upto:
                    i = split_blocks[0]
                    if i >= RH:
                        wait_block_free(act, i - RH)
                    act.wait_ge(w_in[i % R], 16 * (i // R + 1))
                    did(A.activation(ring_high[:, i % RH], ring[:, i % R], ACT.Copy), w_high, i + 1)
                    split_blocks[0] += 1

            raised = [0]

            def high_of(dst, full):
                raised[0] += 1
                did(A.activation(dst, full, ACT.Copy), t_high, raised[0])

            def norm_root(n, src):
                did(A.activation(eps[:, 1:2], eps[:, 0:1], ACT.Sqrt))
                act.wait_ge(x_ready, NORM[n] + 1)
                for t in range(TT):
                    did(A.activation(junk[:], src[:, t, :], ACT.Square, accum_out=ss[:, t:t + 1]))
                    settle()
                did(A.activation(root[:], ss[:], ACT.Sqrt, scale=1.0 / D, bias=eps[:, 0:1]), root_ready, NORM[n] + 1)

            def take_hT(n):
                for t in range(TT):
                    for g in range(2):
                        name = ("hT", n, t, g)
                        act.wait_ge(small_ready, SMALL[name] + 1)
                        high_of(hT_high[:, 4 * g:4 * g + 4, t * P:(t + 1) * P],
                                small_of(name)[:, :].rearrange("p (k t) -> p k t", t=P))

            def take_small(name, dst, src):
                act.wait_ge(small_ready, SMALL[name] + 1)
                did(A.activation(dst, src, ACT.Copy), *taken_small(name))

            def take_sum(name, dst, func=ACT.Copy):
                act.wait_ge(sum_ready, SUM[name] + 1)
                did(A.activation(dst, sum_of(name)[:, :, :], func), *taken_sum(name))

            def columns(t):
                return t.rearrange("p (a b) t -> p a (b t)", b=2)

            def retention():
                act.wait_ge(rope_ang, 1)
                did(A.activation(r_sin, r_ang, ACT.Sin), rope_raw, 1)
                did(A.activation(r_cos, r_ang, ACT.Sin, scale=0.5), rope_raw, 2)
                norm_root(0, x)
                act.dma_start(r_decay, w["decay"].rearrange("h p i -> p h i")).then_inc(decay_in, 16)
                take_hT(0)
                for c in range(4):
                    highs(block_after(("ret_in",), c))
                for c in range(4):
                    highs(block_after(("ret_in",), 4 + c))
                    take_sum(("ret_in", 4 + c), r_v[:, :, c * 512:(c + 1) * 512])
                for c in range(4):
                    highs(block_after(("ret_in",), 8 + c))
                    take_sum(("ret_in", 8 + c), r_g[:, :, c * 512:(c + 1) * 512], ACT.Silu)
                for h in range(RET_HEADS):
                    act.wait_ge(sum_ready, SUM[("ret_y", h)] + 1)
                    if h:
                        act.wait_ge(y_ms, h)
                    for t in range(TT):
                        did(A.activation(junk[:, 0:512], sum_of(("ret_y", h))[:, t, :], ACT.Square, accum_out=hs[:, t:t + 1]),
                            y_sq, 2 * h + t + 1)
                        settle()
                    act.wait_ge(y_ms, h + 1)
                    if h:
                        act.wait_ge(yg_ready, h)
                    did(A.activation(hs[:, 4:6], hs[:, 2:4], ACT.Sqrt), y_root, h + 1)
                for b in range(8):
                    act.wait_ge(small_ready, SMALL[("ygT", b)] + 1)
                    high_of(r_ygT[0][:, 2 * b:2 * b + 2, :].rearrange("p f t -> p (f t)"), small_of(("ygT", b))[:, :])
                for c in range(2):
                    highs(block_after(("ret_out",), c))

            def peer(l):
                n = 1 + 2 * l
                act.wait_ge(x_ready, NORM[n] + 1)
                act.dma_start(p_keys, w["peer_sub_keys"][l].rearrange("h p k d -> k (h p) d")).then_inc(keys_in, 16)
                if l == 1:
                    act.dma_start(m_row_gain, bc(w["g_mem_2"].rearrange("(a d) -> a d", a=1), [P, D])).then_inc(mem_gain_in, 16)
                    act.dma_start(m_h, w["mem_2"][0].rearrange("(t p) d -> p t d", p=P)).then_inc(mem_in, 16)
                act.dma_start(p_iota, bc(w["iota"], [P, TOPK])).then_inc(iota_in, 16)
                norm_root(n, x)
                for b in range(4):
                    take_small(("keysT", l, b), p_keysT[:, 4 * b:4 * b + 4, :].rearrange("p a k -> p (a k)"), small_of(("keysT", l, b))[:, :])
                take_hT(n)
                def exponentials(i):
                    act.wait_ge(best_ready, l * UNITS + i + 1)
                    did(A.activation(p_e, p_d, ACT.Exp), exp_ready, l * UNITS + i + 1)

                for c in range(4):
                    highs(block_after(("query", l), c))
                    take_sum(("query", l, c), columns(p_qT[:, 4 * c:4 * c + 4, :]))
                    if c == 0:
                        highs(block_after(("query", l), 1))
                        exponentials(0)
                if l == 1:
                    norm_root(6, m_h)
                    take_hT(6)
                for i in range(UNITS):
                    if l == 1 and i < 8:
                        highs(min(first_block_of[("mem_kv", 0)] + i + 2, limit - 1))
                    if l == 1 and i in (2, 4, 6, 8):
                        c = i // 2 - 1
                        act.wait_ge(kv_ready, c + 1)
                        dst = columns(m_kT[:, 4 * c:4 * c + 4, :]) if c < 2 else m_v[:, :, (c - 2) * 512:(c - 1) * 512]
                        did(A.activation(dst, pair[kv_pair][:, :, :], ACT.Copy), kv_taken, c + 1)
                    for g in range(4):
                        n = (l * UNITS + i) * 4 + g
                        q = n % 2
                        act.wait_ge(u_used, GROUP * (n + 1))
                        did(A.activation(p_act[:, q, :], p_dot[:, q, :], ACT.Gelu_apprx_tanh), act_ready, n + 1)
                        act.wait_ge(weight_ready, n + 1)
                        for k in range(GROUP):
                            s = n * GROUP + k
                            if s >= 4:
                                act.wait_ge(v_used, s - 3)
                            did(A.activation(p_diag[:, s % 4, :], ident[:], ACT.Copy, scale=p_w[:, q, k:k + 1]),
                                diag_ready, s + 1)
                        if g == 2 and i + 1 < UNITS:
                            exponentials(i + 1)

            def sgu():
                act.wait_ge(x_ready, NORM[2] + 1)
                act.dma_start(s_ws, w["sgu_w_s"][0].rearrange("g i j -> i g j")).then_inc(sgu_in, 16)
                act.dma_start(s_vbias, bc(w["sgu_b_in"][0:1, HALF:2 * HALF], [P, HALF])).then_inc(sgu_in, 16)
                act.dma_start(s_bs.rearrange("p g i -> p (g i)"), bc(w["sgu_b_s"].rearrange("a g i -> a (g i)"), [P, GROUPS * P])).then_inc(sgu_in, 16)
                with nc.allow_non_contiguous_dma(reason="vectors by feature"):
                    act.dma_start(col[:, 8:32], w["sgu_b_in"][0, 0:HALF].rearrange("(k p) -> p k", p=P)).then_inc(sgu_in, 16)
                    act.dma_start(col[:, 32:56], w["sgu_ln_g"][0].rearrange("(k p) -> p k", p=P)).then_inc(sgu_in, 16)
                    act.dma_start(col[:, 56:80], w["sgu_ln_b"][0].rearrange("(k p) -> p k", p=P)).then_inc(sgu_in, 16)
                norm_root(2, x)
                for b in range(2):
                    name = ("wsT", b)
                    act.wait_ge(small_ready, SMALL[name] + 1)
                    src = small_of(name)[:, :].rearrange("p (g i) -> p g i", i=P)
                    did(A.activation(s_wsT[0:CHUNK, 4 * b:4 * b + 4, :], src[0:CHUNK], ACT.Copy))
                    did(A.activation(s_wsT[CHUNK:P, 4 * b:4 * b + 4, CHUNK:P], src[CHUNK:P, :, CHUNK:P], ACT.Copy), *taken_small(name))
                for b in range(2):
                    take_small(("ws_sum", b), s_wsum[:, 4 * b:4 * b + 4, :].rearrange("p g i -> p (g i)"), small_of(("ws_sum", b))[:, :])
                take_hT(2)
                for c in range(6):
                    highs(block_after(("sgu_v",), 6 + c))
                    act.wait_ge(v_raw, c + 1)
                    vc = s_v[:, :, c * BN:(c + 1) * BN]
                    did(A.activation(vc, vc, ACT.Gelu_apprx_tanh), v_gelu, c + 1)
                act.wait_ge(sgu_in, 16 * 6)
                for c in range(6):
                    name = ("sgu_u", c)
                    highs(block_after(("sgu_u",), c))
                    act.wait_ge(sum_ready, SUM[name] + 1)
                    for q in range(4):
                        f = 4 * c + q
                        did(A.activation(s_u[:, f, :], sum_of(name)[:, q // 2, q % 2 * S:(q % 2 + 1) * S], ACT.Gelu_apprx_tanh,
                                         bias=col[:, 8 + f:9 + f]), *((act_step, None) if q < 3 else taken_sum(name)))
                    settle()
                    if c == 3:
                        act.wait_ge(v_ms, 1)
                        did(A.activation(root[:], ms[:], ACT.Sqrt), v_root, 1)
                for b in range(CU // 2):
                    act.wait_ge(us_ready, b + 1)
                    high_of(s_us[0][:, 2 * b:2 * b + 2, :], s_t[:, 4 + 2 * (b % 2):6 + 2 * (b % 2), :])
                for c in range(2):
                    highs(block_after(("sgu_out",), c))

            def hybrid():
                norm_root(4, x)
                act.wait_ge(x_ready, NORM[5] + 1)
                act.dma_start(b_mask, w["att_mask"]).then_inc(hyb_in, 16)
                act.dma_start(b_many, w["att_many"]).then_inc(hyb_in, 16)
                act.dma_start(b_ga, bc(w["g_attn_out_2"].rearrange("(a d) -> a d", a=1), [P, 512])).then_inc(hyb_in, 16)
                with nc.allow_non_contiguous_dma(reason="vectors by feature"):
                    act.dma_start(col[:, 36:40], w["g_conv_out_2"].rearrange("(k p) -> p k", p=P)).then_inc(hyb_in, 16)
                    act.dma_start(col[:, 40:52].rearrange("p (a k) -> p a k", k=4), w["conv_w_2"].rearrange("a (k p) -> p a k", p=P)).then_inc(hyb_in, 16)
                norm_root(5, x)
                take_hT(5)
                for c, dst in enumerate((columns(b_qT), columns(b_kT), b_v, columns(b_bgT), columns(b_cgT))):
                    highs(block_after(("w_in",), c))
                    take_sum(("w_in", c), dst)
                highs(block_after(("w_in",), 5))
                act.wait_ge(cms_ready, 1)
                did(A.activation(b_rs, b_rs, ACT.Sqrt), croot_ready, 1)
                act.wait_ge(mcv_ready, 1)
                high_of(b_mT[0][:, 4:8, :], b_cvn)

                def exponentials(h):
                    act.wait_ge(smax_ready, h + 1)
                    for t, (a, b) in enumerate(((0, P), (P, 384))):
                        sm = b_sm[:, h % 2, a:b]
                        did(A.activation(sm, sm, ACT.Exp, bias=hp[h % 2][:, 2 + t:3 + t], scale=HD ** -0.5), e_ready, 2 * h + t + 1)

                exponentials(0)
                for h in range(HEADS):
                    if h + 1 < HEADS:
                        exponentials(h + 1)
                    take_small(("attT", h), b_pT[:, h % 2, :], small_of(("attT", h))[:, 0:384])
                act.wait_ge(cms_ready, 2)
                did(A.activation(root[:], ms[:], ACT.Sqrt), croot_ready, 2)
                for t in range(TT):
                    act.wait_ge(small_ready, SMALL[("att_rows", t)] + 1)
                    high_of(b_mT[0][:, 0:4, t * P:(t + 1) * P], small_of(("att_rows", t))[:, :].rearrange("p (k t) -> p k t", t=P))
                for c in range(2):
                    highs(block_after(("w_out",), c))

            def memory():
                norm_root(7, x)
                take_hT(7)
                for c in range(2):
                    highs(block_after(("q_mem",), c))
                    take_sum(("q_mem", c), columns(n_qT[:, 4 * c:4 * c + 4, :]))

                def exponentials(h):
                    act.wait_ge(smax_ready, HEADS + h + 1)
                    if h >= 2:
                        act.wait_ge(*taken_small(("mattT", h - 2)))
                    for t in range(TT):
                        did(A.activation(n_p[:, h % 2, t, :], sum_of(("matt", h))[:, t, 0:S], ACT.Exp, bias=hp[h % 2][:, 2 + t:3 + t],
                                         scale=256 ** -0.5, accum_out=hp[h % 2][:, 4 + t:5 + t]), e_ready, 2 * (HEADS + h) + t + 1)

                exponentials(0)
                for h in range(MEM_HEADS):
                    if h + 1 < MEM_HEADS:
                        exponentials(h + 1)
                    take_small(("mattT", h), n_pT[:, h % 2, :, :].rearrange("p m t -> p (m t)"), small_of(("mattT", h))[:, :])
                    act.wait_ge(small_ready, SMALL[("matto", h)] + 1)
                    high_of(n_oT[0][:, 2 * h:2 * h + 2, :].rearrange("p e t -> p (e t)"), small_of(("matto", h))[:, :])
                for c in range(2):
                    highs(block_after(("o_mem",), c))

            def mlp():
                norm_root(8, x)
                take_hT(8)
                for c in range(8):
                    name = ("up", c)
                    highs(block_after(("up",), c))
                    act.wait_ge(sum_ready, SUM[name] + 1)
                    if c >= 2:
                        act.wait_ge(a_low, c - 1)
                    did(A.activation(f_t[:, c % 2].rearrange("p (a b) t -> p a (b t)", b=2), sum_of(name)[:, :, :], ACT.Relu), *taken_sum(name))
                    settle()
                    act.sem_inc(relu_ready, 1)
                    act.wait_ge(a_ready, c + 1)
                    high_of(f_a[0][:, 4 * c:4 * c + 4, :], f_t[:, c % 2])
                for c in range(2):
                    highs(block_after(("down",), c))
                norm_root(9, x)

            act.dma_start(r_pos, bc(w["positions"], [P, S])).then_inc(rope_in, 16)
            act.dma_start(col[:, 8:9], w["inv_freq"]).then_inc(rope_in, 16)
            act.wait_ge(c_in, 16)
            act.wait_ge(ones_ready, 2)
            for k in range(KD):
                did(A.activation(c_full[:, k, :], ones[:], ACT.Silu, scale=col[:, k:k + 1]))
            settle()
            did(A.activation(c_high, c_full, ACT.Copy), c_ready, 1)
            for l in range(2):
                for c in range(12):
                    highs(block_after(("ada", l), c))
            retention()
            if stop >= 2:
                peer(0)
            if stop >= 3:
                sgu()
            if stop >= 4:
                peer(1)
            if stop >= 5:
                hybrid()
            if stop >= 6:
                memory()
            if stop >= 7:
                mlp()


def shape_constants():
    f = np.float32
    i = np.arange(S)
    j = np.arange(S)[:, None]
    decay = np.zeros((RET_HEADS, P, 384), f)
    for h in range(RET_HEADS):
        log_gamma = np.log(1.0 - 2.0 ** (-5.0 - h))
        table = np.exp(log_gamma * np.abs(i - j)) * (j // CHUNK <= i // CHUNK) * RET_QK ** -0.5
        decay[h] = np.concatenate([table[0:P], table[P:S, P:S]], axis=1)
    q, k = np.arange(S)[:, None], np.arange(S)[None, :]
    many = np.zeros((S, S), f)
    for window, dilation in ((128, 1), (512, 4), (2048, 16)):
        many += (k <= q) & (q - k <= window) & ((q - k) % dilation == 0)
    mask = np.where(many > 0, 0.0, NEG).astype(f)
    fold = lambda m: np.ascontiguousarray(np.concatenate([m[0:P, 0:P], m[P:S]], axis=1))
    half = RET_QK // 2
    inv_freq = (1.0 / (f(ROPE_BASE) ** (np.arange(half, dtype=f) / f(half)))).astype(f)
    return {"ident": np.eye(P, dtype=f), "decay": decay, "att_mask": fold(mask), "att_many": fold(many),
            "inv_freq": inv_freq.reshape(P, 1), "iota": np.arange(TOPK, dtype=f).reshape(1, TOPK)}


INPUTS = ["x", "c", "positions", "norm_mix", "norm_ffn", "ada_w", "ada_b", "ret_w_in", "ret_w_out", "sgu_w_in",
          "sgu_b_in", "sgu_ln_g", "sgu_ln_b", "sgu_w_s", "sgu_b_s", "sgu_w_out", "peer_w_query", "peer_sub_keys",
          "peer_u", "peer_v", "norm_final", "mem_2", "g_mix_2", "w_in_2", "conv_w_2", "g_attn_out_2",
          "g_conv_out_2", "w_out_2", "g_xattn_2", "g_mem_2", "w_q_mem_2", "w_kv_mem_2", "w_o_mem_2", "g_mlp_2",
          "w_up_2", "w_down_2", "g_final_2"]


def kernel(**inputs):
    import concourse.bacc as bacc
    from concourse.bass_utils import run_bass_kernel_spmd

    nc = bacc.Bacc("TRN2", target_bir_lowering=False, num_devices=1)
    arrays = {name: np.ascontiguousarray(inputs[name]) for name in INPUTS}
    arrays.update(shape_constants())
    arrays = {f"in_{name}": a for name, a in arrays.items()}
    w = {name[3:]: nc.dram_tensor(name, a.shape, mybir.dt.from_np(a.dtype), kind="ExternalInput").ap()
         for name, a in arrays.items()}
    out = nc.dram_tensor("out", (1, S, D), F32, kind="ExternalOutput").ap()
    two_blocks(nc, w, out)
    return run_bass_kernel_spmd(nc, [arrays], core_ids=[0]).results[0]["out"]
```

```python
from contextlib import ExitStack

import numpy as np

import concourse.bass as bass
from concourse import mybir

F32 = mybir.dt.float32
F32R = mybir.dt.float32r
BF16 = mybir.dt.bfloat16
I32 = mybir.dt.int32
U32 = mybir.dt.uint32
ALU = mybir.AluOpType
ACT = mybir.ActivationFunctionType
AX_X = mybir.AxisListType.X

P = 128
D = 1024
S = 256
TT = S // P
KD = D // P
EPS = 1e-6
CHUNK = 64
RET_HEADS = 4
RET_QK = D // RET_HEADS
ROPE_BASE = 10000.0
HALF = 3072
CU = HALF // P
GROUPS = 8
PEER_HEADS = 8
TOPK = 16
NKEYS = 128
EXPERTS = NKEYS * NKEYS
PICKS = PEER_HEADS * TOPK
UNITS = TT * PEER_HEADS
HEADS = 8
HD = 64
MEM_HEADS = 4
NEG = -1e30
LOWEST = -3.0e38

R = 4
RH = 4
BN = 512
BK = 4
U_SLOTS = 4
V_SLOTS = 8
V_LAG = 3
CONV_AT = 4
GROUP = 4

TWO_PI_1 = 6.28125
TWO_PI_2 = 0.0019350051879882812
TWO_PI_3 = float(2 * np.pi - 6.28125 - 0.0019350051879882812)
PI_SAFE = 3.1415925

NORM = {0: 0, 1: 1, 2: 2, 3: 3, 6: 4, 4: 5, 5: 6, 7: 7, 8: 8, 9: 9}


def matrices(w):
    out = [(("ada", l), w["ada_w"][l], 8, range(12)) for l in range(2)]
    out += [(("ret_in",), w["ret_w_in"][0], 8, range(12)), (("ret_out",), w["ret_w_out"][0], 16, range(2)),
            (("query", 0), w["peer_w_query"][0], 8, range(4)),
            (("sgu_v",), w["sgu_w_in"][0], 8, range(6, 12)), (("sgu_u",), w["sgu_w_in"][0], 8, range(6)),
            (("sgu_out",), w["sgu_w_out"][0], 24, range(2)),
            (("query", 1), w["peer_w_query"][1], 8, range(4)),
            (("mem_kv",), w["w_kv_mem_2"], 8, range(4)), (("w_in",), w["w_in_2"], 8, (0, 1, 2, 4, 5, 3)),
            (("w_out",), w["w_out_2"], 8, range(2)), (("q_mem",), w["w_q_mem_2"], 8, range(2)),
            (("o_mem",), w["w_o_mem_2"], 8, range(2)), (("up",), w["w_up_2"], 8, range(8)),
            (("down",), w["w_down_2"], 32, range(2))]
    return out


def k_order(mat, kt):
    order = list(range(kt // BK))
    return order[::-1] if mat == ("w_out",) else order


def numbered(names):
    return {name: i for i, name in enumerate(names)}


def sums_in_order():
    out = [("ada", l, c) for l in range(2) for c in range(12)]
    out += [("ret_in", c) for c in range(12)] + [("ret_y", h) for h in range(RET_HEADS)] + [("ret_out", c) for c in range(2)]
    out += [("query", 0, c) for c in range(4)] + [("peer", 0, t) for t in range(TT)]
    out += [("sgu_v", c) for c in range(6)] + [("sgu_u", c) for c in range(6)] + [("sgu_out", c) for c in range(2)]
    out += [("query", 1, c) for c in range(4)] + [("peer", 1, t) for t in range(TT)]
    out += [("w_in", 0), ("w_in", 1), ("w_in", 2), ("att", 0), ("w_in", 4), ("att", 1), ("w_in", 5), ("att", 2), ("w_in", 3)]
    out += [("att", h) for h in range(3, HEADS)]
    out += [("w_out", c) for c in range(2)]
    out += [("q_mem", 0), ("matt", 0), ("matt", 1), ("q_mem", 1), ("matt", 2), ("matt", 3)]
    out += [("o_mem", c) for c in range(2)] + [("up", c) for c in range(8)] + [("down", c) for c in range(2)]
    return numbered(out)


def small_in_order():
    def turned(n):
        return [("hT", n, t, g) for t in range(TT) for g in range(2)]
    out = turned(0) + [("ret_s", h) for h in range(RET_HEADS)] + [("ygT", b) for b in range(8)]
    for l in range(2):
        out += [("keysT", l, b) for b in range(4)] + turned(1 + 2 * l)
        out += [("scores", l, 0)]
        if l == 1:
            out += turned(6)
        out += [("scores", l, i) for i in range(1, UNITS)]
        if l == 0:
            out += turned(2) + [("wsT", b) for b in range(2)] + [("ws_sum", b) for b in range(2)]
            out += [("mixed", b) for b in range(CU // 2)]
    out += turned(5) + [("attT", 0)]
    for h in range(HEADS):
        out += [("atto", h)] + ([("attT", h + 1)] if h + 1 < HEADS else []) + ([("conv_sq",)] if h == CONV_AT else [])
    out += [("att_rows", t) for t in range(TT)] + turned(7)
    for h in range(0, MEM_HEADS, 2):
        out += [("mattT", h), ("mattT", h + 1), ("matto", h), ("matto", h + 1)]
    out += turned(8)
    return numbered(out)


def two_blocks(nc, w, out):
    MATS = matrices(w)
    blocks, first_block_of = [], {}
    for name, ap, kt, ns in MATS:
        for n in ns:
            first_block_of[name + (n,)] = len(blocks)
            for kb in k_order(name, kt):
                blocks.append(ap[kb * BK * P:(kb + 1) * BK * P, n * BN:(n + 1) * BN].rearrange("(k p) n -> p k n", p=P))
    SUM = sums_in_order()
    SMALL = small_in_order()

    ends_sum, mat_ends = {}, {}
    for (name, _, kt, ns) in MATS:
        for n in ns:
            label = name + (n - 6 if name == ("sgu_v",) else n,)
            last = first_block_of[name + (n,)] + kt // BK - 1
            ends_sum[last] = ("kv", n + 1) if name == ("mem_kv",) else ("sum", SUM[label] + 1)
            mat_ends[name + (n,)] = [first_block_of[name + (n,)] + kt // BK - 1]
    limit = len(blocks)

    with ExitStack() as ctx:
        def sb(name, shape, dt=F32):
            return ctx.enter_context(nc.sbuf_tensor(name, shape, dt))

        def sem(name):
            return ctx.enter_context(nc.semaphore(name))

        mod_base = (nc.sbuf_base + 31) // 32 * 32
        mod = sb("mod", [P, 2, 3, D])
        ring_base = (nc.sbuf_base + 31) // 32 * 32
        ring = sb("ring", [P, R, BK, BN])
        arena_base = (nc.sbuf_base + 31) // 32 * 32
        ARENA = 24832
        arena = sb("arena", [P, ARENA])
        ring_low = nc.alloc_sbuf_tensor_at("ring_low", [P, R, BK, BN], F32R, offset=ring_base)
        ring_high = sb("ring_high", [P, RH, BK, BN], F32R)
        x = sb("x", [P, TT, D])
        gain_base = (nc.sbuf_base + 31) // 32 * 32
        gain = sb("gain", [P, 2, D])
        ident = sb("ident", [P, P])
        ones = sb("ones", [P, P])
        junk = sb("junk", [P, D], BF16)
        ss = sb("ss", [P, TT])
        ms = sb("ms", [P, TT])
        eps = sb("eps", [P, 2])
        root = sb("root", [P, TT])
        rstd = sb("rstd", [P, TT])
        hp = [sb("head_even", [P, 8]), sb("head_odd", [P, 8])]
        hs = hp[0]
        col = sb("col", [P, 96])

        def at(name, offset, *shape, dt=F32):
            assert offset + int(np.prod(shape)) <= ARENA, name
            return nc.alloc_sbuf_tensor_at(name, [P, *shape], dt, offset=arena_base + 4 * offset)[:]

        hT_high, hT_low = at("hT_high", 0, KD, S, dt=F32R), at("hT_low", 2048, KD, S, dt=F32R)
        hT = (hT_high, hT_low)
        m_row, m_gain = at("m_row", 0, 2, 6, D), at("m_gain", 16384, 4, D)
        c_high, c_low, c_full = at("c_high", 12288, KD, P, dt=F32R), at("c_low", 13312, KD, P, dt=F32R), at("c_full", 14336, KD, P)
        r_qT, r_kT = at("r_qT", 4096, KD, S), at("r_kT", 6144, KD, S)
        r_ygT = (at("r_yg_high", 4096, 16, S, dt=F32R), at("r_yg_low", 8192, 16, S, dt=F32R))
        r_v, r_h, r_g = at("r_v", 8192, TT, 2048), at("r_h", 4096, TT, D), at("r_g", 12288, TT, 2048)
        r_sT, r_decay = at("r_sT", 16384, RET_HEADS, 384), at("r_decay", 17920, RET_HEADS, 384)
        r_cos, r_sin, r_tmp = at("r_cos", 19456, S), at("r_sin", 19712, S), at("r_tmp", 19968, 2, 512)
        r_turn, r_int = at("r_turn", 19968, S), at("r_int", 20224, S, dt=I32)
        r_pos, r_ang = at("r_pos", 22016, S, dt=I32), at("r_ang", 22272, S)
        p_qT, p_keysT, p_keys = at("p_qT", 4096, 16, S), at("p_keysT", 8192, 16, P), at("p_keys", 14336, 16, P)
        u_buf, v_buf = at("u_buf", 10240, U_SLOTS, D), at("v_buf", 14336, V_SLOTS, D)
        p_h = nc.alloc_sbuf_tensor_at("p_h", [P, TT, D], F32, offset=gain_base)[:]
        p_tmp = at("p_tmp", 0, D)
        p_row, p_top, p_pos = at("p_row", 22528, 2, NKEYS), at("p_top", 22784, 2, TOPK), at("p_pos", 22816, 2, TOPK, dt=U32)
        p_posf = at("p_posf", 22848, 2, TOPK)
        p_cand, p_best, p_at = at("p_cand", 22880, TOPK, TOPK), at("p_best", 23136, TOPK), at("p_at", 23152, TOPK, dt=U32)
        p_ij, p_ijf, p_eq = at("p_ij", 23168, 2, TOPK, dt=U32), at("p_ijf", 23200, 2, TOPK), at("p_eq", 23232, 2, 256)
        p_i, p_ef, p_d, p_e = (at("p_i", 23744, 2, TOPK), at("p_ef", 23776, TOPK), at("p_d", 23792, TOPK),
                               at("p_e", 23808, TOPK))
        p_idx, p_gate = at("p_idx", 23824, PICKS, dt=I32), at("p_gate", 23952, PICKS)
        p_z, p_dot, p_act, p_w = (at("p_z", 24080, 8), at("p_dot", 24088, 2, GROUP), at("p_act", 24096, 2, GROUP),
                                  at("p_w", 24104, 2, GROUP))
        p_iota, p_diag = at("p_iota", 24112, TOPK), at("p_diag", 24128, 4, P)
        s_u, s_v, s_h = at("s_u", 4096, CU, S), at("s_v", 10240, TT, HALF), at("s_h", 10240, TT, D)
        s_us = (at("s_us_high", 4096, CU, S, dt=F32R), at("s_us_low", 10240, TT, CU, P, dt=F32R))
        s_vbias, s_t = at("s_vbias", 16384, HALF), at("s_t", 16384, 12, S)
        s_bs, s_wsT = at("s_bs", 19456, GROUPS, P), at("s_wsT", 20480, GROUPS, P)
        s_ws, s_wsum = at("s_ws", 21504, GROUPS, P), at("s_wsum", 21504, GROUPS, P)
        m_h = nc.alloc_sbuf_tensor_at("m_h", [P, TT, D], F32, offset=mod_base)[:]
        m_kT = nc.alloc_sbuf_tensor_at("m_kT", [P, KD, S], F32, offset=mod_base + 8192)[:]
        m_v = nc.alloc_sbuf_tensor_at("m_v", [P, TT, D], F32, offset=mod_base)[:]
        m_row_gain = nc.alloc_sbuf_tensor_at("m_row_gain", [P, D], F32, offset=mod_base + 8192)[:]
        b_h = at("b_h", 4096, TT, D)
        b_qT, b_kT, b_v = at("b_qT", 4096, 4, S), at("b_kT", 5120, 4, S), at("b_v", 6144, TT, 512)
        b_bgT, b_cgT, b_uT = at("b_bgT", 7168, 4, S), at("b_cgT", 8192, 4, S), at("b_uT", 9216, 4, 258)
        b_cv, b_sq = at("b_cv", 10248, 4, S), at("b_sq", 11272, 4, S)
        b_mT = (at("b_m_high", 12296, KD, S, dt=F32R), at("b_m_low", 14344, KD, S, dt=F32R))
        b_sm, b_p, b_pT = at("b_sm", 16392, 2, 384), at("b_p", 17160, 2, 384), at("b_pT", 17928, 2, 384)
        b_att, b_mask, b_many = at("b_att", 18696, TT, 512), at("b_mask", 19720, 384), at("b_many", 20104, 384)
        b_rs, b_ga, b_cvn = at("b_rs", 20488, S), at("b_ga", 20744, 512), b_sq
        n_qT, n_p, n_pT = at("n_qT", 6144, KD, S), at("n_p", 8192, 2, TT, S), at("n_pT", 9216, 2, TT, S)
        n_oT = (at("n_o_high", 10240, KD, S, dt=F32R), at("n_o_low", 12288, KD, S, dt=F32R))
        f_a = (at("f_a_high", 4096, 32, S, dt=F32R), at("f_a_low", 12288, 32, S, dt=F32R))
        f_t = at("f_t", 20480, 2, 4, S)
        spill = nc.dram_tensor("modulations", (2, 6, D), F32).ap()

        pair = [ctx.enter_context(nc.psum_tensor(f"pair{i}", [P, 2, 512], F32)) for i in range(3)]
        small = [ctx.enter_context(nc.psum_tensor(f"small{i}", [P, 512], F32)) for i in range(2)]

        w_in = [sem(f"w_in{i}") for i in range(R)]
        w_high, w_low = sem("w_high"), sem("w_low")
        t_high = sem("t_high")
        w_used = sem("w_used")
        sum_ready = sem("sum_ready")
        sum_taken = [sem(f"sum_taken{i}") for i in range(3)]
        small_ready = sem("small_ready")
        small_taken = [sem(f"small_taken{i}") for i in range(2)]
        x_in, c_in, cst_in, bias_in = sem("x_in"), sem("c_in"), sem("cst_in"), sem("bias_in")
        rope_in, decay_in = sem("rope_in"), sem("decay_in")
        gain_in = [sem("gain_in0"), sem("gain_in1")]
        gain_used = sem("gain_used")
        c_ready, ones_ready = sem("c_ready"), sem("ones_ready")
        x_ready, root_ready, h_ready = sem("x_ready"), sem("root_ready"), sem("h_ready")
        rows_ready, spilled, mod_used = sem("rows_ready"), sem("spilled"), sem("mod_used")
        kv_ready, kv_taken, mem_gain_in = sem("kv_ready"), sem("kv_taken"), sem("mem_gain_in")
        mod_in = [sem("mod_in0"), sem("mod_in1")]
        m_gain_in = sem("m_gain_in")
        rope_ang, rope_raw, rope_ready = sem("rope_ang"), sem("rope_raw"), sem("rope_ready")
        scores_ready = sem("scores_ready")
        y_sq, y_ms, y_root, yg_ready = sem("y_sq"), sem("y_ms"), sem("y_root"), sem("yg_ready")
        keys_in, iota_in = sem("keys_in"), sem("iota_in")
        best_ready, exp_ready, idx_ready = sem("best_ready"), sem("exp_ready"), sem("idx_ready")
        u_in = [sem(f"u_in{i}") for i in range(U_SLOTS)]
        v_in = [sem(f"v_in{i}") for i in range(V_SLOTS)]
        u_used, v_used = sem("u_used"), sem("v_used")
        act_ready, weight_ready, diag_ready = sem("act_ready"), sem("weight_ready"), sem("diag_ready")
        sgu_in, ws_zero = sem("sgu_in"), sem("ws_zero")
        v_raw, v_gelu, v_ms, v_root, v_ready = (sem(n) for n in ("v_raw", "v_gelu", "v_ms", "v_root", "v_ready"))
        us_ready, us_done = sem("us_ready"), sem("us_done")
        mem_in, hyb_in = sem("mem_in"), sem("hyb_in")
        sq_ready, cms_ready, croot_ready, mcv_ready = sem("sq_ready"), sem("cms_ready"), sem("croot_ready"), sem("mcv_ready")
        smax_ready, e_ready, p_ready = sem("smax_ready"), sem("e_ready"), sem("p_ready")
        arow_ready = sem("arow_ready")
        relu_ready, a_ready, a_low = sem("relu_ready"), sem("a_ready"), sem("a_low")
        out_ready, out_done = sem("out_ready"), sem("out_done")
        dve_step, act_step, pool_step = sem("dve_step"), sem("act_step"), sem("pool_step")
        conv_in_ready = sem("conv_in_ready")

        def own(eng, step):
            count, pending = [0], {}

            def did(ins, signal=step, value=None):
                if signal is step:
                    count[0] += 1
                    value = count[0]
                ins.then_inc(signal, 1)
                pending[signal.name] = (signal, value)

            def settle():
                for signal, value in pending.values():
                    eng.wait_ge(signal, value)
                pending.clear()

            return did, settle

        def wait_block_free(eng, old):
            if old in ends_sum:
                which, value = ends_sum[old]
                eng.wait_ge(kv_ready if which == "kv" else sum_ready, value)
            else:
                eng.wait_ge(w_used, old + 1 - sum(e <= old for e in ends_sum))

        def block_after(mat, n):
            return min(mat_ends[mat + (n,)][0] + 2, limit - 1)

        def taken_sum(name):
            i = SUM[name]
            return sum_taken[i % 3], i // 3 + 1

        def taken_small(name):
            i = SMALL[name]
            return small_taken[i % 2], i // 2 + 1

        def sum_of(name):
            return pair[SUM[name] % 3]

        def small_of(name):
            return small[SMALL[name] % 2]

        kv_pair = (SUM[("peer", 1, 1)] + 1) % 3

        block = ctx.enter_context(nc.Block())
        bc = lambda ap, shape: ap.broadcast_to(shape)

        @block.sync
        def _(sp):
            with nc.allow_non_contiguous_dma(reason="one vector of 1024"):
                sp.dma_start(col[:, 0:KD], w["c"][0].rearrange("(k p) -> p k", p=P)).then_inc(c_in, 16)
            for i in range(limit):
                if i >= R:
                    wait_block_free(sp, i - R)
                sp.dma_start(ring[:, i % R], blocks[i]).then_inc(w_in[i % R], 16)
                if i == 1:
                    sp.dma_start(m_row[0:1].rearrange("p l a d -> p (l a d)"),
                                 w["ada_b"].rearrange("(o l) n -> o (l n)", o=1)).then_inc(bias_in, 16)
                if i == 3:
                    sp.dma_start(ident[:], w["ident"]).then_inc(cst_in, 16)
                    sp.dma_start(x[:], w["x"][0].rearrange("(t p) d -> p t d", p=P)).then_inc(x_in, 16)
            sp.wait_ge(out_ready, 1)
            sp.dma_start(out[0].rearrange("(t p) d -> p t d", p=P), b_h[:, :, :]).then_inc(out_done, 16)
            sp.wait_ge(out_done, 16)

        @block.gpsimd
        def _(pool):
            def load_gain(n, row):
                if n >= 2:
                    pool.wait_ge(gain_used, n - 1)
                pool.dma_start(gain[:, n % 2, :], bc(row, [P, D])).then_inc(gain_in[n % 2], 16)

            def gather_u(l, t, k):
                s = (l * TT + t) * PICKS + k
                if k % TOPK == 0:
                    pool.wait_ge(idx_ready, s // TOPK + 1)
                if s >= U_SLOTS:
                    pool.wait_ge(u_used, s - U_SLOTS + 1)
                nc.gpsimd.indirect_dma_start(u_buf[:, s % U_SLOTS, :], None, experts_u,
                                             bass.IndirectOffsetOnAxis(ap=p_idx[:, k:k + 1], axis=0))\
                    .then_inc(u_in[s % U_SLOTS], 16)

            def gather_v(l, t, k):
                s = (l * TT + t) * PICKS + k
                if s >= V_SLOTS:
                    pool.wait_ge(v_used, s - V_SLOTS + 1)
                nc.gpsimd.indirect_dma_start(v_buf[:, s % V_SLOTS, :], None, experts_v,
                                             bass.IndirectOffsetOnAxis(ap=p_idx[:, k:k + 1], axis=0))\
                    .then_inc(v_in[s % V_SLOTS], 16)

            def gathers(l):
                picks = [(l, t, k) for t in range(TT) for k in range(PICKS)]
                for n in range(len(picks) + V_LAG):
                    if n < len(picks):
                        gather_u(*picks[n])
                    if n >= V_LAG:
                        gather_v(*picks[n - V_LAG])

            def convolution():
                G = nc.gpsimd
                did, settle = own(pool, pool_step)
                pool.wait_ge(conv_in_ready, 1)
                for q in range(4):
                    did(G.tensor_scalar(b_cv[:, q, :], b_uT[:, q, 0:S], col[:, 40 + q:41 + q], None, ALU.mult))
                settle()
                for tap in (1, 2):
                    for q in range(4):
                        did(G.tensor_scalar(b_sq[:, q, :], b_uT[:, q, tap:tap + S],
                                            col[:, 40 + 4 * tap + q:41 + 4 * tap + q], None, ALU.mult))
                    settle()
                    did(G.tensor_tensor(b_cv, b_cv, b_sq, ALU.add))
                    settle()
                pool.wait_ge(*taken_sum(("w_in", 3)))
                did(G.tensor_tensor(b_cv, b_cv, b_bgT, ALU.mult))
                settle()
                did(G.tensor_tensor(b_sq, b_cv, b_cv, ALU.mult), sq_ready, 1)

            experts_u = w["peer_u"].rearrange("l e d -> (l e) d")
            experts_v = w["peer_v"].rearrange("l e d -> (l e) d")
            def load_mod(n):
                if n >= 2:
                    pool.wait_ge(mod_used, n - 1)
                pool.dma_start(mod[:, n % 2], bc(spill[n // 2:n // 2 + 1, 3 * (n % 2):3 * (n % 2) + 3, :], [P, 3, D]))\
                    .then_inc(mod_in[n % 2], 16)

            for l in range(2):
                pool.dma_start(m_gain[0:1, 2 * l, :], w["norm_mix"][l:l + 1]).then_inc(m_gain_in, 16)
                pool.dma_start(m_gain[0:1, 2 * l + 1, :], w["norm_ffn"][l:l + 1]).then_inc(m_gain_in, 16)
            for l in range(2):
                pool.wait_ge(rows_ready, l + 1)
                pool.dma_start(spill[l:l + 1], m_row[0:1, l]).then_inc(spilled, 16)
                pool.wait_ge(spilled, 16 * (l + 1))
                load_mod(l)
            load_mod(2)
            gathers(0)
            load_mod(3)
            gathers(1)
            pool.wait_ge(u_used, 2 * TT * PICKS)
            rows = (w["norm_final"], w["g_mix_2"], w["g_xattn_2"], w["g_mlp_2"], w["g_final_2"])
            for n, row in enumerate(rows):
                if n == 4:
                    convolution()
                load_gain(n, row.rearrange("(a d) -> a d", a=1))

        @block.tensor
        def _(pe):
            def open_sum(name):
                i = SUM[name]
                if i >= 3:
                    pe.wait_ge(sum_taken[i % 3], i // 3)

            def open_small(name):
                i = SMALL[name]
                if i >= 2:
                    pe.wait_ge(small_taken[i % 2], i // 2)

            def split(i):
                pe.wait_ge(w_low, i + 1)
                return ring_high[:, i % RH], ring_low[:, i % R]

            def tile_of(lhs, k, t):
                return lhs[:, t, k, :] if len(lhs.shape) == 4 else lhs[:, k, t * P:(t + 1) * P]

            def rows_product(name, mat, n, lhs, kt, before=None):
                open_sum(name)
                acc = sum_of(name)
                order = k_order(mat, kt)
                for step, kb in enumerate(order):
                    if before:
                        before(kb)
                    high, low = split(first_block_of[mat + (n,)] + step)
                    for t in range(TT):
                        for k in range(BK):
                            kk = kb * BK + k
                            a_high, a_low = tile_of(lhs[0], kk, t), tile_of(lhs[1], kk, t)
                            for j, (a, b) in enumerate(((a_high, high), (a_high, low), (a_low, high))):
                                mm = nc.tensor.matmul(acc[:, t, :], a, b[:, k, :],
                                                      start=(step == 0 and k == 0 and j == 0),
                                                      stop=(step == len(order) - 1 and k == BK - 1 and j == 2))
                    mm.then_inc(sum_ready if step == len(order) - 1 else w_used, 1)

            def columns_product(name, mat, n, rhs, kt=KD, before=None):
                open_sum(name)
                acc = sum_of(name)
                for kb in range(kt // BK):
                    if before:
                        before(kb)
                    i = first_block_of[mat + (n,)] + kb
                    high, low = split(i)
                    for nt in range(4):
                        for k in range(BK):
                            kk = kb * BK + k
                            n_tile = slice(nt * P, (nt + 1) * P)
                            for j, (a, b) in enumerate(((high, rhs[0]), (high, rhs[1]), (low, rhs[0]))):
                                mm = nc.tensor.matmul(acc[:, nt // 2, nt % 2 * S:(nt % 2 + 1) * S], a[:, k, n_tile], b[:, kk, :],
                                                      start=(kk == 0 and nt % 2 == 0 and j == 0), stop=(kk == kt - 1 and j == 2),
                                                      skip_group_check=True)
                    mm.then_inc(sum_ready if kb == kt // BK - 1 else w_used, 1)

            def turn_rows(n, h):
                for t in range(TT):
                    pe.wait_ge(h_ready, TT * NORM[n] + t + 1)
                    for g in range(2):
                        name = ("hT", n, t, g)
                        open_small(name)
                        for k in range(4):
                            mm = nc.tensor.transpose(small_of(name)[:, k * P:(k + 1) * P],
                                                     h[:, t, (4 * g + k) * P:(4 * g + k + 1) * P], ident[:])
                        mm.then_inc(small_ready, 1)

            def parts_of_hT(n):
                def wait(kb):
                    for t in range(TT):
                        pe.wait_ge(*taken_small(("hT", n, t, kb)))
                return wait

            def wait_hT(n):
                for t in range(TT):
                    for g in range(2):
                        pe.wait_ge(*taken_small(("hT", n, t, g)))

            def retention():
                for c in range(4):
                    columns_product(("ret_in", c), ("ret_in",), c, hT, before=parts_of_hT(0))
                for c in range(4, 12):
                    rows_product(("ret_in", c), ("ret_in",), c, hT, KD)
                for h in range(RET_HEADS):
                    name = ("ret_s", h)
                    pe.wait_ge(*taken_sum(("ret_in", h // 2)))
                    pe.wait_ge(*taken_sum(("ret_in", 2 + h // 2)))
                    pe.wait_ge(rope_ready, 4)
                    open_small(name)
                    sc = small_of(name)
                    for jt in range(TT):
                        o = sc[:, 0:S] if jt == 0 else sc[:, S:S + P]
                        for half in range(2):
                            mm = nc.tensor.matmul(o, r_kT[:, 2 * h + half, jt * P:(jt + 1) * P],
                                                  r_qT[:, 2 * h + half, jt * P:S], start=(half == 0), stop=(half == 1))
                    mm.then_inc(small_ready, 1)
                for h in range(RET_HEADS):
                    name = ("ret_y", h)
                    pe.wait_ge(scores_ready, h + 1)
                    pe.wait_ge(*taken_sum(("ret_in", 4 + h)))
                    open_sum(name)
                    acc = sum_of(name)
                    vh = r_v[:, :, h * 512:(h + 1) * 512]
                    nc.tensor.matmul(acc[:, 0, :], r_sT[:, h, 0:P], vh[:, 0, :], start=True, stop=True)
                    nc.tensor.matmul(acc[:, 1, :], r_sT[:, h, P:S], vh[:, 0, :], start=True, stop=False)
                    nc.tensor.matmul(acc[:, 1, :], r_sT[:, h, S:S + P], vh[:, 1, :], start=False, stop=True)\
                        .then_inc(sum_ready, 1)

                def turn_head(h):
                    pe.wait_ge(yg_ready, h + 1)
                    for b in (2 * h, 2 * h + 1):
                        name = ("ygT", b)
                        open_small(name)
                        for q in range(4):
                            t, f = q % 2, 2 * b + q // 2
                            mm = nc.tensor.transpose(small_of(name)[:, q * P:(q + 1) * P], r_g[:, t, f * P:(f + 1) * P], ident[:])
                        mm.then_inc(small_ready, 1)

                def next_head(kb):
                    if kb + 1 < RET_HEADS:
                        turn_head(kb + 1)
                    for b in (2 * kb, 2 * kb + 1):
                        pe.wait_ge(*taken_small(("ygT", b)))

                turn_head(0)
                rows_product(("ret_out", 0), ("ret_out",), 0, r_ygT, 16, next_head)
                rows_product(("ret_out", 1), ("ret_out",), 1, r_ygT, 16)

            def peer(l):
                n = 1 + 2 * l
                pe.wait_ge(keys_in, 16 * (l + 1))
                for b in range(4):
                    name = ("keysT", l, b)
                    open_small(name)
                    for q in range(4):
                        mm = nc.tensor.transpose(small_of(name)[:, q * P:(q + 1) * P], p_keys[:, 4 * b + q, :], ident[:])
                    mm.then_inc(small_ready, 1)
                turn_rows(n, p_h)
                for b in range(4):
                    pe.wait_ge(*taken_small(("keysT", l, b)))

                def scores(i):
                    t, h = divmod(i, PEER_HEADS)
                    name = ("scores", l, i)
                    pe.wait_ge(*taken_sum(("query", l, h // 2)))
                    open_small(name)
                    for p in range(2):
                        mm = nc.tensor.matmul(small_of(name)[:, p * P:(p + 1) * P], p_qT[:, 2 * h + p, t * P:(t + 1) * P],
                                              p_keysT[:, 2 * h + p, :], start=True, stop=True)
                    mm.then_inc(small_ready, 1)

                columns_product(("query", l, 0), ("query", l), 0, hT, before=parts_of_hT(n))
                scores(0)
                for c in range(1, 4):
                    columns_product(("query", l, c), ("query", l), c, hT)
                if l == 1:
                    turn_rows(6, m_h)
                scores(1)
                for i in range(UNITS):
                    t, h = divmod(i, PEER_HEADS)
                    if i + 2 < UNITS:
                        scores(i + 2)
                    if l == 1 and i < 8:
                        memory_block(i // 2, i % 2)
                    name = ("peer", l, t)
                    if h == 0:
                        open_sum(name)
                    acc = sum_of(name)
                    for k in range(h * TOPK, (h + 1) * TOPK):
                        s = (l * TT + t) * PICKS + k
                        pe.wait_ge(diag_ready, s + 1)
                        pe.wait_ge(v_in[s % V_SLOTS], 16 * (s // V_SLOTS + 1))
                        for half in range(2):
                            mm = nc.tensor.matmul(acc[:, half, :], p_diag[:, s % 4, :],
                                                  v_buf[:, s % V_SLOTS, half * 512:(half + 1) * 512],
                                                  start=(k == 0), stop=(k == PICKS - 1))
                        mm.then_inc(v_used, 1)
                    if h == PEER_HEADS - 1:
                        pe.wait_ge(v_used, (l * TT + t + 1) * PICKS)
                        pe.sem_inc(sum_ready, 1)

            def memory_block(c, kb):
                if c == 0 and kb == 0:
                    wait_hT(6)
                    last = max(i for i in SUM.values() if i < SUM[("peer", 1, 0)] and i % 3 == kv_pair)
                    pe.wait_ge(sum_taken[kv_pair], last // 3 + 1)
                if c and kb == 0:
                    pe.wait_ge(kv_taken, c)
                acc = pair[kv_pair]
                high, low = split(first_block_of[("mem_kv", c)] + kb)
                for k in range(BK):
                    kk = kb * BK + k
                    if c < 2:
                        for nt in range(4):
                            n_tile = slice(nt * P, (nt + 1) * P)
                            for j, (a, b) in enumerate(((high, hT[0]), (high, hT[1]), (low, hT[0]))):
                                mm = nc.tensor.matmul(acc[:, nt // 2, nt % 2 * S:(nt % 2 + 1) * S], a[:, k, n_tile], b[:, kk, :],
                                                      start=(kk == 0 and nt % 2 == 0 and j == 0), stop=(kk == KD - 1 and j == 2),
                                                      skip_group_check=True)
                    else:
                        for t in range(TT):
                            a_high, a_low = tile_of(hT[0], kk, t), tile_of(hT[1], kk, t)
                            for j, (a, b) in enumerate(((a_high, high), (a_high, low), (a_low, high))):
                                mm = nc.tensor.matmul(acc[:, t, :], a, b[:, k, :], start=(kk == 0 and j == 0),
                                                      stop=(kk == KD - 1 and j == 2))
                mm.then_inc(kv_ready if kb == 1 else w_used, 1)

            def sgu():
                turn_rows(2, s_h)
                for c in range(6):
                    rows_product(("sgu_v", c), ("sgu_v",), 6 + c, hT, KD, parts_of_hT(2))
                pe.wait_ge(sgu_in, 16 * 6)
                for b in range(2):
                    name = ("wsT", b)
                    open_small(name)
                    for q in range(4):
                        mm = nc.tensor.transpose(small_of(name)[:, q * P:(q + 1) * P], s_ws[:, 4 * b + q, :], ident[:])
                    mm.then_inc(small_ready, 1)
                pe.wait_ge(ws_zero, 1)
                for b in range(2):
                    pe.wait_ge(*taken_small(("wsT", b)))
                for b in range(2):
                    name = ("ws_sum", b)
                    open_small(name)
                    nc.tensor.matmul(small_of(name)[:, :], ones[:], s_wsT[:, 4 * b:4 * b + 4, :].rearrange("p g i -> p (g i)"),
                                     start=True, stop=True).then_inc(small_ready, 1)
                for c in range(6):
                    columns_product(("sgu_u", c), ("sgu_u",), c, hT)
                pe.wait_ge(v_ready, TT)

                def mix(b):
                    name = ("mixed", b)
                    open_small(name)
                    for q in range(2):
                        f = 2 * b + q
                        for t in range(TT):
                            mm = nc.tensor.matmul(small_of(name)[:, q * S + t * P:q * S + (t + 1) * P],
                                                  s_v[:, t, f * P:(f + 1) * P], s_wsT[:, f // (CU // GROUPS), :],
                                                  start=True, stop=True)
                    mm.then_inc(small_ready, 1)

                def mix_next(kb):
                    for b in (2 * kb + 2, 2 * kb + 3):
                        if b < CU // 2:
                            mix(b)
                    pe.wait_ge(us_done, 2 * kb + 2)

                mix(0)
                mix(1)
                rows_product(("sgu_out", 0), ("sgu_out",), 0, s_us, CU, mix_next)
                rows_product(("sgu_out", 1), ("sgu_out",), 1, s_us, CU)

            def softmax_turned(tag, h, blocks_of):
                name = (tag + "T", h)
                open_small(name)
                for q, src in enumerate(blocks_of):
                    mm = nc.tensor.transpose(small_of(name)[:, q * P:(q + 1) * P], src, ident[:])
                mm.then_inc(small_ready, 1)

            def hybrid():
                pe.wait_ge(kv_taken, 4)
                turn_rows(5, b_h)
                def att_scores(h):
                    name = ("att", h)
                    open_sum(name)
                    acc = sum_of(name)
                    lo = h % 2 * HD
                    for t in range(TT):
                        mm = nc.tensor.matmul(acc[:, t, 0:(t + 1) * P], b_qT[lo:lo + HD, h // 2, t * P:(t + 1) * P],
                                              b_kT[lo:lo + HD, h // 2, 0:(t + 1) * P], start=True, stop=True)
                    mm.then_inc(sum_ready, 1)

                def att_turn(h):
                    pe.wait_ge(p_ready, h + 1)
                    softmax_turned("att", h, [b_p[:, h % 2, q * P:(q + 1) * P] for q in range(3)])

                def att_out(h):
                    pe.wait_ge(*taken_small(("attT", h)))
                    name = ("atto", h)
                    open_small(name)
                    o, pT = small_of(name), b_pT[:, h % 2, :]
                    vh = b_v[:, :, h * HD:(h + 1) * HD]
                    nc.tensor.matmul(o[:, 0:HD], pT[:, 0:P], vh[:, 0, :], start=True, stop=True)
                    nc.tensor.matmul(o[:, HD:2 * HD], pT[:, P:2 * P], vh[:, 0, :], start=True, stop=False)
                    nc.tensor.matmul(o[:, HD:2 * HD], pT[:, 2 * P:3 * P], vh[:, 1, :], start=False, stop=True)\
                        .then_inc(small_ready, 1)

                columns_product(("w_in", 0), ("w_in",), 0, hT, before=parts_of_hT(5))
                columns_product(("w_in", 1), ("w_in",), 1, hT)
                rows_product(("w_in", 2), ("w_in",), 2, hT, KD)
                for c in range(2):
                    pe.wait_ge(*taken_sum(("w_in", c)))
                att_scores(0)
                columns_product(("w_in", 4), ("w_in",), 4, hT)
                att_scores(1)
                att_turn(0)
                columns_product(("w_in", 5), ("w_in",), 5, hT)
                pe.wait_ge(*taken_sum(("w_in", 2)))
                for h in range(HEADS):
                    att_out(h)
                    if h + 2 < HEADS:
                        att_scores(h + 2)
                    if h + 1 < HEADS:
                        att_turn(h + 1)
                    if h == 0:
                        columns_product(("w_in", 3), ("w_in",), 3, hT)
                    if h == CONV_AT:
                        pe.wait_ge(sq_ready, 1)
                        open_small(("conv_sq",))
                        for q in range(4):
                            mm = nc.tensor.matmul(small_of(("conv_sq",))[:, 0:S], ones[:], b_sq[:, q, :], start=(q == 0), stop=(q == 3))
                        mm.then_inc(small_ready, 1)
                def halves(kb):
                    if kb == 1:
                        pe.wait_ge(mcv_ready, 2)
                        return
                    for t in range(TT):
                        pe.wait_ge(arow_ready, t + 1)
                        name = ("att_rows", t)
                        open_small(name)
                        for q in range(4):
                            mm = nc.tensor.transpose(small_of(name)[:, q * P:(q + 1) * P], b_att[:, t, q * P:(q + 1) * P], ident[:])
                        mm.then_inc(small_ready, 1)
                    for t in range(TT):
                        pe.wait_ge(*taken_small(("att_rows", t)))

                rows_product(("w_out", 0), ("w_out",), 0, b_mT, KD, halves)
                rows_product(("w_out", 1), ("w_out",), 1, b_mT, KD)

            def memory():
                turn_rows(7, b_h)

                def scores(h):
                    name = ("matt", h)
                    open_sum(name)
                    acc = sum_of(name)
                    for t in range(TT):
                        for e in range(2):
                            mm = nc.tensor.matmul(acc[:, t, 0:S], n_qT[:, 2 * h + e, t * P:(t + 1) * P],
                                                  m_kT[:, 2 * h + e, :], start=(e == 0), stop=(e == 1))
                    mm.then_inc(sum_ready, 1)

                def turn(h):
                    pe.wait_ge(p_ready, HEADS + h + 1)
                    softmax_turned("matt", h, [n_p[:, h % 2, t, m * P:(m + 1) * P] for m in range(2) for t in range(TT)])

                def attend(h):
                    pe.wait_ge(*taken_small(("mattT", h)))
                    name = ("matto", h)
                    open_small(name)
                    for e in range(2):
                        for m in range(2):
                            mm = nc.tensor.matmul(small_of(name)[:, e * S:(e + 1) * S],
                                                  m_v[:, m, h * S + e * P:h * S + (e + 1) * P], n_pT[:, h % 2, m, :],
                                                  start=(m == 0), stop=(m == 1))
                    mm.then_inc(small_ready, 1)

                def later_heads(kb):
                    if kb == 0:
                        return
                    turn(2)
                    turn(3)
                    attend(2)
                    attend(3)
                    for h in (2, 3):
                        pe.wait_ge(*taken_small(("matto", h)))

                columns_product(("q_mem", 0), ("q_mem",), 0, hT, before=parts_of_hT(7))
                pe.wait_ge(*taken_sum(("q_mem", 0)))
                scores(0)
                scores(1)
                columns_product(("q_mem", 1), ("q_mem",), 1, hT)
                turn(0)
                turn(1)
                pe.wait_ge(*taken_sum(("q_mem", 1)))
                scores(2)
                attend(0)
                attend(1)
                scores(3)
                for h in range(2):
                    pe.wait_ge(*taken_small(("matto", h)))
                rows_product(("o_mem", 0), ("o_mem",), 0, n_oT, KD, later_heads)
                rows_product(("o_mem", 1), ("o_mem",), 1, n_oT, KD)

            def mlp():
                turn_rows(8, b_h)
                for c in range(8):
                    columns_product(("up", c), ("up",), c, hT, before=parts_of_hT(8))
                for c in range(2):
                    rows_product(("down", c), ("down",), c, f_a, 32, lambda kb: pe.wait_ge(a_low, kb + 1))

            pe.wait_ge(c_ready, 2)
            for l in range(2):
                for c in range(12):
                    if l == 1 and c == 9:
                        pe.wait_ge(cst_in, 16)
                        turn_rows(0, r_h)
                    name = ("ada", l, c)
                    open_sum(name)
                    for kb in range(2):
                        i = first_block_of[("ada", l, c)] + kb
                        high, low = split(i)
                        for k in range(BK):
                            kk = kb * BK + k
                            for j, (a, b) in enumerate(((c_high, high), (c_high, low), (c_low, high))):
                                mm = nc.tensor.matmul(sum_of(name)[:, 0, :], a[:, kk, :], b[:, k, :],
                                                      start=(kk == 0 and j == 0), stop=(kk == KD - 1 and j == 2))
                        mm.then_inc(sum_ready if kb == 1 else w_used, 1)
            pe.wait_ge(ones_ready, 2)
            retention()
            peer(0)
            sgu()
            peer(1)
            hybrid()
            memory()
            mlp()

        @block.vector
        def _(dve):
            did, settle = own(dve, dve_step)
            V = nc.vector

            split_blocks = [0]

            def lows(upto):
                while split_blocks[0] <= upto:
                    i = split_blocks[0]
                    dve.wait_ge(w_high, i + 1)
                    did(V.tensor_tensor(ring_low[:, i % R], ring[:, i % R], ring_high[:, i % RH].bitcast(F32), ALU.subtract),
                        w_low, i + 1)
                    split_blocks[0] += 1

            lowered = [0]

            def low_of(dst, high, full, name=None, signal=(dve_step, None)):
                lowered[0] += 1
                dve.wait_ge(t_high, lowered[0])
                did(V.tensor_tensor(dst, full, high.bitcast(F32), ALU.subtract), *(taken_small(name) if name else signal))

            def lows_hT(n):
                for t in range(TT):
                    for g in range(2):
                        name = ("hT", n, t, g)
                        part = (slice(None), slice(4 * g, 4 * g + 4), slice(t * P, (t + 1) * P))
                        low_of(hT_low[part], hT_high[part], small_of(name)[:, :].rearrange("p (k t) -> p k t", t=P), name)

            def norm(n, src, dst, scale, shift=None, gain_row=None, tmp=None):
                i = NORM[n]
                tmp = dst if tmp is None else tmp
                settle()
                if n == 6:
                    dve.wait_ge(mem_in, 16)
                    dve.wait_ge(mem_gain_in, 16)
                dve.sem_inc(x_ready, 1)
                if gain_row is not None:
                    dve.wait_ge(gain_in[gain_row % 2], 16 * (gain_row // 2 + 1))
                if n != 6:
                    for t in range(TT):
                        did(V.tensor_tensor(tmp[:, t, :], src[:, t, :], scale, ALU.mult))
                    settle()
                if gain_row is not None:
                    dve.sem_inc(gain_used, 1)
                dve.wait_ge(root_ready, i + 1)
                did(V.reciprocal(rstd[:], root[:]))
                settle()
                for t in range(TT):
                    if n == 6:
                        ins = V.scalar_tensor_tensor(out=dst[:, t, :], in0=src[:, t, :], scalar=rstd[:, t:t + 1], in1=scale,
                                                     op0=ALU.mult, op1=ALU.mult)
                    elif shift is None:
                        ins = V.tensor_scalar(dst[:, t, :], tmp[:, t, :], rstd[:, t:t + 1], None, ALU.mult)
                    else:
                        ins = V.scalar_tensor_tensor(out=dst[:, t, :], in0=tmp[:, t, :], scalar=rstd[:, t:t + 1], in1=shift,
                                                     op0=ALU.mult, op1=ALU.add)
                    did(ins, h_ready, TT * i + t + 1)

            def add_product(name, c, tmp, gate=None):
                dve.wait_ge(sum_ready, SUM[name] + 1)
                acc = sum_of(name)
                xc = x[:, :, c * 512:(c + 1) * 512]
                if gate is None:
                    did(V.tensor_tensor(xc, xc, acc[:, :, :], ALU.add), *taken_sum(name))
                else:
                    did(V.tensor_tensor(tmp, acc[:, :, :], bc(gate[:, c * 512:(c + 1) * 512].unsqueeze(1), [P, TT, 512]), ALU.mult),
                        *taken_sum(name))
                    settle()
                    did(V.tensor_tensor(xc, xc, tmp, ALU.add))
                settle()

            def sublayer_done():
                dve.sem_inc(mod_used, 1)

            def modulations():
                dve.wait_ge(c_ready, 1)
                did(V.tensor_tensor(c_low, c_full, c_high.bitcast(F32), ALU.subtract), c_ready, 2)
                dve.wait_ge(bias_in, 16)
                for l in range(2):
                    flat = m_row[0:1, l].rearrange("p a d -> p (a d)")
                    for c in range(12):
                        name = ("ada", l, c)
                        lows(block_after(("ada", l), c))
                        dve.wait_ge(sum_ready, SUM[name] + 1)
                        did(V.tensor_tensor(flat[:, c * BN:(c + 1) * BN], sum_of(name)[0:1, 0, :],
                                            flat[:, c * BN:(c + 1) * BN], ALU.add), *taken_sum(name))
                        if l == 1 and c == 7:
                            dve.wait_ge(x_in, 16)
                            dve.wait_ge(mod_in[0], 16)
                            norm(0, x, r_h, mod[:, 0, 1, :], mod[:, 0, 0, :])
                            lows(block_after(("ada", l), 8))
                            lows_hT(0)
                    settle()
                    dve.wait_ge(m_gain_in, 64)
                    for j, part in enumerate((1, 4)):
                        did(V.scalar_tensor_tensor(out=m_row[0:1, l, part, :], in0=m_row[0:1, l, part, :], scalar=1.0,
                                                   in1=m_gain[0:1, 2 * l + j, :], op0=ALU.add, op1=ALU.mult))
                    settle()
                    dve.sem_inc(rows_ready, 1)

            def rotary_tables():
                dve.wait_ge(rope_in, 32)
                did(V.tensor_copy(r_ang, r_pos))
                settle()
                did(V.tensor_scalar(r_ang, r_ang, col[:, 8:9], None, ALU.mult))
                settle()
                did(V.tensor_scalar(r_int, r_ang, float(1 / (2 * np.pi)), None, ALU.mult))
                settle()
                did(V.tensor_copy(r_turn, r_int))
                settle()
                for part in (TWO_PI_1, TWO_PI_2, TWO_PI_3):
                    did(V.scalar_tensor_tensor(out=r_ang, in0=r_turn, scalar=-part, in1=r_ang, op0=ALU.mult, op1=ALU.add))
                    settle()
                did(V.tensor_scalar(r_ang, r_ang, PI_SAFE, -PI_SAFE, ALU.min, ALU.max), rope_ang, 1)
                dve.wait_ge(rope_raw, 2)
                did(V.tensor_tensor(r_turn, r_cos, r_cos, ALU.mult))
                settle()
                did(V.tensor_scalar(r_cos, r_turn, -2.0, 1.0, ALU.mult, ALU.add))
                settle()

            def rotate(c):
                name = ("ret_in", c)
                dve.wait_ge(sum_ready, SUM[name] + 1)
                acc = sum_of(name)
                dst = r_qT if c < 2 else r_kT
                x1, x2 = acc[:, :, 0:S], acc[:, :, S:2 * S]
                both = [P, 2, S]
                cs, sn = bc(r_cos.unsqueeze(1), both), bc(r_sin.unsqueeze(1), both)
                d = dst.rearrange("p (h e) t -> p h e t", e=2)[:, 2 * (c % 2):2 * (c % 2) + 2]
                ta = r_tmp[:, 0, :].rearrange("p (h t) -> p h t", t=S)
                tb = r_tmp[:, 1, :].rearrange("p (h t) -> p h t", t=S)
                did(V.tensor_tensor(ta, x2, sn, ALU.mult))
                did(V.tensor_tensor(tb, x2, cs, ALU.mult))
                did(V.tensor_tensor(d[:, :, 0, :], x1, cs, ALU.mult))
                did(V.tensor_tensor(d[:, :, 1, :], x1, sn, ALU.mult), *taken_sum(name))
                settle()
                did(V.tensor_tensor(d[:, :, 0, :], d[:, :, 0, :], ta, ALU.subtract))
                did(V.tensor_tensor(d[:, :, 1, :], d[:, :, 1, :], tb, ALU.add), rope_ready, c + 1)
                settle()

            def retention():
                for c in range(12):
                    lows(block_after(("ret_in",), c))
                    if c == 0:
                        rotary_tables()
                        dve.wait_ge(spilled, 32)
                    if c < 4:
                        rotate(c)
                dve.wait_ge(decay_in, 16)
                for h in range(RET_HEADS):
                    name = ("ret_s", h)
                    dve.wait_ge(small_ready, SMALL[name] + 1)
                    did(V.tensor_tensor(r_sT[:, h, :], small_of(name)[:, 0:384], r_decay[:, h, :], ALU.mult),
                        *taken_small(name))
                    settle()
                    dve.sem_inc(scores_ready, 1)

                def yg_low(h):
                    for b in (2 * h, 2 * h + 1):
                        name = ("ygT", b)
                        low_of(r_ygT[1][:, 2 * b:2 * b + 2, :].rearrange("p f t -> p (f t)"),
                               r_ygT[0][:, 2 * b:2 * b + 2, :].rearrange("p f t -> p (f t)"), small_of(name)[:, :], name)

                for h in range(RET_HEADS):
                    dve.wait_ge(y_sq, 2 * (h + 1))
                    did(V.tensor_scalar(hs[:, 2:4], hs[:, 0:2], 1.0 / 512, EPS, ALU.mult, ALU.add), y_ms, h + 1)
                    dve.wait_ge(y_root, h + 1)
                    did(V.reciprocal(hs[:, 6:8], hs[:, 4:6]))
                    settle()
                    dve.wait_ge(*taken_sum(("ret_in", 8 + h)))
                    name = ("ret_y", h)
                    for t in range(TT):
                        g = r_g[:, t, h * 512:(h + 1) * 512]
                        ins = V.scalar_tensor_tensor(out=g, in0=sum_of(name)[:, t, :], scalar=hs[:, 6 + t:7 + t], in1=g,
                                                     op0=ALU.mult, op1=ALU.mult)
                        did(ins, *(taken_sum(name) if t else (dve_step, None)))
                    settle()
                    dve.sem_inc(yg_ready, 1)
                    if h:
                        yg_low(h - 1)
                yg_low(RET_HEADS - 1)
                for c in range(2):
                    lows(block_after(("ret_out",), c))
                    add_product(("ret_out", c), c, r_tmp[:, :, :], mod[:, 0, 2, :])
                sublayer_done()

            def first_level(l, t, h):
                name = ("scores", l, t * PEER_HEADS + h)
                dve.wait_ge(small_ready, SMALL[name] + 1)
                for p in range(2):
                    srow, rest = small_of(name)[:, p * P:(p + 1) * P], p_row[:, p, :]
                    top, pos = p_top[:, p, :], p_pos[:, p, :]
                    did(V.max(top[:, 0:8], srow))
                    settle()
                    did(V.max_index(pos[:, 0:8], top[:, 0:8], srow))
                    settle()
                    did(V.match_replace(rest, top[:, 0:8], srow, LOWEST), *(taken_small(name) if p else (dve_step, None)))
                    settle()
                    did(V.max(top[:, 8:16], rest))
                    settle()
                    did(V.max_index(pos[:, 8:16], top[:, 8:16], rest))
                settle()

            def second_level(l, t, h):
                sq = [P, TOPK, TOPK]
                did(V.tensor_copy(p_posf, p_pos))
                did(V.tensor_tensor(p_cand, bc(p_top[:, 0, :].unsqueeze(2), sq), bc(p_top[:, 1, :].unsqueeze(1), sq), ALU.add))
                settle()
                cand = p_cand.rearrange("p a b -> p (a b)")
                did(V.max(p_best[:, 0:8], cand))
                settle()
                did(V.max_index(p_at[:, 0:8], p_best[:, 0:8], cand))
                settle()
                did(V.match_replace(cand, p_best[:, 0:8], cand, LOWEST))
                settle()
                did(V.max(p_best[:, 8:16], cand))
                settle()
                did(V.max_index(p_at[:, 8:16], p_best[:, 8:16], cand))
                settle()
                did(V.tensor_scalar(p_d, p_best, p_best[:, 0:1], None, ALU.subtract), best_ready, (l * TT + t) * 8 + h + 1)

            def choose(l, t, h):
                sq = [P, TOPK, TOPK]
                did(V.tensor_scalar(p_ij[:, 0, :], p_at, 4, None, ALU.logical_shift_right))
                did(V.tensor_scalar(p_ij[:, 1, :], p_at, 15, None, ALU.bitwise_and))
                settle()
                did(V.tensor_copy(p_ijf, p_ij))
                settle()
                for p in range(2):
                    eq = p_eq[:, p, :].rearrange("p (a b) -> p a b", b=TOPK)
                    did(V.tensor_tensor(eq, bc(p_ijf[:, p, :].unsqueeze(2), sq), bc(p_iota.unsqueeze(1), sq), ALU.is_equal))
                settle()
                for p in range(2):
                    eq = p_eq[:, p, :].rearrange("p (a b) -> p a b", b=TOPK)
                    did(V.tensor_tensor(eq, eq, bc(p_posf[:, p, :].unsqueeze(1), sq), ALU.mult))
                settle()
                did(V.tensor_reduce(p_i.rearrange("p a b -> p (a b)"), p_eq.rearrange("p a (b c) -> p (a b) c", c=TOPK), AX_X, ALU.add))
                settle()
                did(V.tensor_scalar(p_ef, p_i[:, 0, :], float(NKEYS), float(l * EXPERTS), ALU.mult, ALU.add))
                settle()
                did(V.tensor_tensor(p_idx[:, h * TOPK:(h + 1) * TOPK], p_ef, p_i[:, 1, :], ALU.add),
                    idx_ready, (l * TT + t) * 8 + h + 1)

            def gates(l, t, h):
                unit = (l * TT + t) * 8 + h
                dve.wait_ge(exp_ready, unit + 1)
                did(V.tensor_reduce(p_z[:, 0:1], p_e, AX_X, ALU.add))
                settle()
                did(V.reciprocal(p_z[:, 1:2], p_z[:, 0:1]))
                settle()
                did(V.tensor_scalar(p_gate[:, h * TOPK:(h + 1) * TOPK], p_e, p_z[:, 1:2], None, ALU.mult))
                settle()

            def group(l, t, q):
                for k in range(q * GROUP, (q + 1) * GROUP):
                    s = (l * TT + t) * PICKS + k
                    dve.wait_ge(u_in[s % U_SLOTS], 16 * (s // U_SLOTS + 1))
                    ub = u_buf[:, s % U_SLOTS, :]
                    did(V.tensor_tensor_reduce(out=ub, in0=ub, in1=p_h[:, t, :], scale=1.0, scalar=0.0, op0=ALU.mult,
                                               op1=ALU.add, accum_out=p_dot[:, q % 2, k % GROUP:k % GROUP + 1]), u_used, s + 1)
                n = (l * TT + t) * (PICKS // GROUP) + q
                dve.wait_ge(act_ready, n + 1)
                did(V.tensor_tensor(p_w[:, q % 2, :], p_act[:, q % 2, :], p_gate[:, q * GROUP:(q + 1) * GROUP], ALU.mult),
                    weight_ready, n + 1)

            def peer(l):
                n = 1 + 2 * l
                dve.wait_ge(mod_in[1], 16 * (l + 1))
                norm(n, x, p_h, mod[:, 1, 1, :], mod[:, 1, 0, :])
                lows_hT(n)
                lows(block_after(("query", l), 0))
                dve.wait_ge(iota_in, 16 * (l + 1))
                units = [divmod(i, PEER_HEADS) for i in range(UNITS)]
                first_level(l, 0, 0)
                second_level(l, 0, 0)
                choose(l, 0, 0)
                lows(block_after(("query", l), 1))
                gates(l, 0, 0)
                for c in range(2, 4):
                    lows(block_after(("query", l), c))
                if l == 1:
                    norm(6, m_h, m_h, m_row_gain)
                    lows_hT(6)
                for i in range(UNITS):
                    t, h = units[i]
                    nxt = units[i + 1] if i + 1 < UNITS else None
                    if l == 1 and i < 8:
                        lows(min(first_block_of[("mem_kv", 0)] + i + 2, limit - 1))
                    for g in range(4):
                        group(l, t, h * 4 + g)
                        if g == 0 and nxt:
                            first_level(l, *nxt)
                            second_level(l, *nxt)
                        if g == 1 and nxt:
                            choose(l, *nxt)
                        if g == 3 and nxt:
                            gates(l, *nxt)
                    if i == PEER_HEADS:
                        add_experts(l, 0)
                add_experts(l, 1)
                sublayer_done()

            def add_experts(l, t):
                name = ("peer", l, t)
                dve.wait_ge(sum_ready, SUM[name] + 1)
                did(V.tensor_tensor(p_tmp.rearrange("p (a b) -> p a b", b=512), sum_of(name)[:, :, :],
                                    mod[:, 1, 2, :].rearrange("p (a b) -> p a b", b=512), ALU.mult), *taken_sum(name))
                settle()
                did(V.tensor_tensor(x[:, t, :], x[:, t, :], p_tmp, ALU.add))
                settle()

            def us_low(b):
                high = s_us[0][:, 2 * b:2 * b + 2, :].rearrange("p f (t i) -> p t f i", i=P)
                us = s_t[:, 4 + 2 * (b % 2):6 + 2 * (b % 2), :].rearrange("p f (t i) -> p t f i", i=P)
                low_of(s_us[1][:, :, 2 * b:2 * b + 2, :], high, us, signal=(us_done, b + 1))

            def sgu():
                did(V.memset(s_wsT[CHUNK:P, :, 0:CHUNK], 0.0), ws_zero, 1)
                dve.wait_ge(mod_in[0], 32)
                norm(2, x, s_h, mod[:, 0, 1, :], mod[:, 0, 0, :])
                lows_hT(2)
                dve.wait_ge(sgu_in, 16 * 6)
                for c in range(6):
                    name = ("sgu_v", c)
                    lows(block_after(("sgu_v",), 6 + c))
                    dve.wait_ge(sum_ready, SUM[name] + 1)
                    vc = s_v[:, :, c * BN:(c + 1) * BN]
                    did(V.tensor_tensor(vc, sum_of(name)[:, :, :], bc(s_vbias[:, c * BN:(c + 1) * BN].unsqueeze(1), [P, TT, BN]), ALU.add),
                        *taken_sum(name))
                    settle()
                    dve.sem_inc(v_raw, 1)
                lows(block_after(("sgu_u",), 0))
                dve.wait_ge(v_gelu, 6)
                for t in range(TT):
                    did(V.tensor_reduce(hs[:, t:t + 1], s_v[:, t, :], AX_X, ALU.add))
                settle()
                lows(block_after(("sgu_u",), 1))
                did(V.tensor_scalar(hs[:, 2:4], hs[:, 0:2], -1.0 / HALF, None, ALU.mult))
                settle()
                for t in range(TT):
                    did(V.tensor_scalar(s_v[:, t, :], s_v[:, t, :], hs[:, 2 + t:3 + t], None, ALU.add))
                settle()
                lows(block_after(("sgu_u",), 2))
                for t in range(TT):
                    did(V.tensor_tensor_reduce(out=s_t.rearrange("p a b -> p (a b)"), in0=s_v[:, t, :], in1=s_v[:, t, :],
                                               scale=1.0, scalar=0.0, op0=ALU.mult, op1=ALU.add, accum_out=hs[:, 4 + t:5 + t]))
                    settle()
                lows(block_after(("sgu_u",), 3))
                did(V.tensor_scalar(ms[:], hs[:, 4:6], 1.0 / HALF, EPS, ALU.mult, ALU.add), v_ms, 1)
                lows(block_after(("sgu_u",), 4))
                dve.wait_ge(v_root, 1)
                did(V.reciprocal(rstd[:], root[:]))
                settle()
                for t in range(TT):
                    did(V.tensor_scalar(s_v[:, t, :], s_v[:, t, :], rstd[:, t:t + 1], None, ALU.mult), v_ready, t + 1)
                lows(block_after(("sgu_u",), 5))
                for b in range(CU // 2):
                    name = ("mixed", b)
                    for q in range(2):
                        f = 2 * b + q
                        g = f // (CU // GROUPS)
                        did(V.scalar_tensor_tensor(out=s_t[:, q, 0:P], in0=s_wsum[:, g, :], scalar=col[:, 56 + f:57 + f],
                                                   in1=s_bs[:, g, :], op0=ALU.mult, op1=ALU.add))
                    settle()
                    dve.wait_ge(small_ready, SMALL[name] + 1)
                    for q in range(2):
                        f = 2 * b + q
                        ins = V.scalar_tensor_tensor(out=s_t[:, 2 + q, :].rearrange("p (t i) -> p t i", i=P),
                                                     in0=small_of(name)[:, q * S:(q + 1) * S].rearrange("p (t i) -> p t i", i=P),
                                                     scalar=col[:, 32 + f:33 + f],
                                                     in1=bc(s_t[:, q, 0:P].unsqueeze(1), [P, TT, P]), op0=ALU.mult, op1=ALU.add)
                        did(ins, *((dve_step, None) if q == 0 else taken_small(name)))
                    settle()
                    if b % 2 == 0:
                        dve.wait_ge(*taken_sum(("sgu_u", b // 2)))
                    us = s_t[:, 4 + 2 * (b % 2):6 + 2 * (b % 2), :]
                    did(V.tensor_tensor(us, s_u[:, 2 * b:2 * b + 2, :], s_t[:, 2:4, :], ALU.mult), us_ready, b + 1)
                    if b:
                        us_low(b - 1)
                    if b >= 2 and b % 2 == 0:
                        lows(first_block_of[("sgu_out", 0)] + b // 2 + 1)
                us_low(CU // 2 - 1)
                for c in range(2):
                    lows(block_after(("sgu_out",), c))
                    add_product(("sgu_out", c), c, s_vbias[:, 0:1024].rearrange("p (a b) -> p a b", b=512), mod[:, 0, 2, :])
                sublayer_done()

            def hybrid():
                norm(4, x, x, gain[:, 0, :], gain_row=0, tmp=b_h)
                norm(5, x, b_h, gain[:, 1, :], gain_row=1)
                lows_hT(5)

                def att_max(h):
                    name = ("att", h)
                    dve.wait_ge(sum_ready, SUM[name] + 1)
                    for t, (a, b) in enumerate(((0, P), (P, 384))):
                        did(V.tensor_tensor(b_sm[:, h % 2, a:b], sum_of(name)[:, t, 0:b - a], b_mask[:, a:b], ALU.add),
                            *((dve_step, None) if t == 0 else taken_sum(name)))
                    settle()
                    for t, (a, b) in enumerate(((0, P), (P, 384))):
                        did(V.tensor_reduce(hp[h % 2][:, t:t + 1], b_sm[:, h % 2, a:b], AX_X, ALU.max))
                    settle()
                    did(V.tensor_scalar(hp[h % 2][:, 2:4], hp[h % 2][:, 0:2], -(HD ** -0.5), None, ALU.mult), smax_ready, h + 1)

                def att_sum(h):
                    dve.wait_ge(e_ready, 2 * (h + 1))
                    for t, (a, b) in enumerate(((0, P), (P, 384))):
                        e = b_sm[:, h % 2, a:b]
                        did(V.tensor_tensor_reduce(out=b_p[:, h % 2, a:b], in0=e, in1=b_many[:, a:b], scale=1.0, scalar=0.0,
                                                   op0=ALU.mult, op1=ALU.add, accum_out=hp[h % 2][:, 4 + t:5 + t]),
                            *((dve_step, None) if t == 0 else (p_ready, h + 1)))
                    settle()
                    did(V.reciprocal(hp[h % 2][:, 6:8], hp[h % 2][:, 4:6]))
                    settle()

                def att_step(h):
                    if h + 1 < HEADS:
                        att_sum(h + 1)
                    name = ("atto", h)
                    dve.wait_ge(small_ready, SMALL[name] + 1)
                    did(V.tensor_tensor(b_att[:, :, h * HD:(h + 1) * HD],
                                        small_of(name)[:, 0:TT * HD].rearrange("p (t e) -> p t e", e=HD),
                                        bc(hp[h % 2][:, 6:8].unsqueeze(2), [P, TT, HD]), ALU.mult), *taken_small(name))
                    settle()
                    if h + 2 < HEADS:
                        att_max(h + 2)

                for c in range(3):
                    lows(block_after(("w_in",), c))
                did(V.memset(b_uT[:, :, 0:2], 0.0))
                dve.wait_ge(hyb_in, 16 * 5)
                att_max(0)
                att_sum(0)
                lows(block_after(("w_in",), 4))
                att_max(1)
                lows(block_after(("w_in",), 5))
                att_step(0)
                name = ("w_in", 5)
                dve.wait_ge(sum_ready, SUM[name] + 1)
                dve.wait_ge(*taken_sum(("w_in", 4)))
                did(V.tensor_tensor(b_uT[:, :, 2:258], sum_of(name)[:, :, :].rearrange("p a (b t) -> p (a b) t", t=S), b_cgT, ALU.mult),
                    *taken_sum(name))
                settle()
                dve.sem_inc(conv_in_ready, 1)
                lows(block_after(("w_in",), 3))
                for h in range(1, CONV_AT + 1):
                    att_step(h)
                name = ("conv_sq",)
                dve.wait_ge(small_ready, SMALL[name] + 1)
                did(V.tensor_scalar(b_rs, small_of(name)[:, 0:S], 1.0 / 512, EPS, ALU.mult, ALU.add), *taken_small(name))
                settle()
                dve.sem_inc(cms_ready, 1)
                dve.wait_ge(croot_ready, 1)
                did(V.reciprocal(b_rs, b_rs))
                settle()
                for q in range(4):
                    did(V.scalar_tensor_tensor(out=b_cvn[:, q, :], in0=b_cv[:, q, :], scalar=col[:, 36 + q:37 + q], in1=b_rs,
                                               op0=ALU.mult, op1=ALU.mult))
                settle()
                dve.sem_inc(mcv_ready, 1)
                low_of(b_mT[1][:, 4:8, :], b_mT[0][:, 4:8, :], b_cvn)
                settle()
                dve.sem_inc(mcv_ready, 1)

                for h in range(CONV_AT + 1, HEADS):
                    att_step(h)
                for t in range(TT):
                    did(V.tensor_tensor_reduce(out=b_sq.rearrange("p a b -> p (a b)")[:, t * 512:(t + 1) * 512], in0=b_att[:, t, :], in1=b_att[:, t, :],
                                               scale=1.0, scalar=0.0, op0=ALU.mult, op1=ALU.add, accum_out=hs[:, t:t + 1]))
                settle()
                did(V.tensor_scalar(ms[:], hs[:, 0:2], 1.0 / 512, EPS, ALU.mult, ALU.add))
                settle()
                dve.sem_inc(cms_ready, 1)
                dve.wait_ge(croot_ready, 2)
                did(V.reciprocal(rstd[:], root[:]))
                settle()
                for t in range(TT):
                    did(V.scalar_tensor_tensor(out=b_att[:, t, :], in0=b_att[:, t, :], scalar=rstd[:, t:t + 1], in1=b_ga,
                                               op0=ALU.mult, op1=ALU.mult), arow_ready, t + 1)
                for t in range(TT):
                    name = ("att_rows", t)
                    low_of(b_mT[1][:, 0:4, t * P:(t + 1) * P], b_mT[0][:, 0:4, t * P:(t + 1) * P],
                           small_of(name)[:, :].rearrange("p (k t) -> p k t", t=P), name)
                for c in range(2):
                    lows(block_after(("w_out",), c))
                    add_product(("w_out", c), c, None)

            def memory():
                norm(7, x, b_h, gain[:, 0, :], gain_row=2)
                lows_hT(7)
                lows(block_after(("q_mem",), 0))

                def head_max(h):
                    name, hm = ("matt", h), hp[h % 2]
                    dve.wait_ge(sum_ready, SUM[name] + 1)
                    did(V.tensor_reduce(hm[:, 0:2], sum_of(name)[:, :, 0:S], AX_X, ALU.max))
                    settle()
                    did(V.tensor_scalar(hm[:, 2:4], hm[:, 0:2], -(256 ** -0.5), None, ALU.mult), smax_ready, HEADS + h + 1)

                def head_probs(h):
                    name, hm = ("matt", h), hp[h % 2]
                    dve.wait_ge(e_ready, 2 * (HEADS + h + 1))
                    dve.sem_inc(taken_sum(name)[0], 1)
                    did(V.reciprocal(hm[:, 6:8], hm[:, 4:6]))
                    settle()
                    for t in range(TT):
                        did(V.tensor_scalar(n_p[:, h % 2, t, :], n_p[:, h % 2, t, :], hm[:, 6 + t:7 + t], None, ALU.mult),
                            *((dve_step, None) if t == 0 else (p_ready, HEADS + h + 1)))
                    settle()

                for h in range(0, MEM_HEADS, 2):
                    if h == 0:
                        head_max(0)
                        head_max(1)
                    head_probs(h)
                    head_probs(h + 1)
                    if h == 0:
                        lows(block_after(("q_mem",), 1))
                        head_max(2)
                    for g in (h, h + 1):
                        name = ("matto", g)
                        low_of(n_oT[1][:, 2 * g:2 * g + 2, :].rearrange("p e t -> p (e t)"),
                               n_oT[0][:, 2 * g:2 * g + 2, :].rearrange("p e t -> p (e t)"), small_of(name)[:, :], name)
                    if h == 0:
                        head_max(3)
                for c in range(2):
                    lows(block_after(("o_mem",), c))
                    add_product(("o_mem", c), c, None)

            def mlp():
                norm(8, x, b_h, gain[:, 1, :], gain_row=3)
                lows_hT(8)
                for c in range(8):
                    lows(block_after(("up",), c))
                    dve.wait_ge(relu_ready, c + 1)
                    did(V.tensor_tensor(f_t[:, c % 2], f_t[:, c % 2], f_t[:, c % 2], ALU.mult), a_ready, c + 1)
                    low_of(f_a[1][:, 4 * c:4 * c + 4, :], f_a[0][:, 4 * c:4 * c + 4, :], f_t[:, c % 2])
                    settle()
                    dve.sem_inc(a_low, 1)
                for c in range(2):
                    lows(block_after(("down",), c))
                    add_product(("down", c), c, None)
                norm(9, x, b_h, gain[:, 0, :], gain_row=4)

            did(V.memset(ones[:], 1.0), ones_ready, 1)
            did(V.memset(eps[:], EPS), ones_ready, 2)
            modulations()
            retention()
            peer(0)
            sgu()
            peer(1)
            hybrid()
            memory()
            mlp()
            settle()
            dve.sem_inc(out_ready, 1)

        @block.scalar
        def _(act):
            did, settle = own(act, act_step)
            A = nc.scalar

            split_blocks = [0]

            def highs(upto):
                while split_blocks[0] <= upto:
                    i = split_blocks[0]
                    if i >= RH:
                        wait_block_free(act, i - RH)
                    act.wait_ge(w_in[i % R], 16 * (i // R + 1))
                    did(A.activation(ring_high[:, i % RH], ring[:, i % R], ACT.Copy), w_high, i + 1)
                    split_blocks[0] += 1

            raised = [0]

            def high_of(dst, full):
                raised[0] += 1
                did(A.activation(dst, full, ACT.Copy), t_high, raised[0])

            def norm_root(n, src):
                did(A.activation(eps[:, 1:2], eps[:, 0:1], ACT.Sqrt))
                act.wait_ge(x_ready, NORM[n] + 1)
                for t in range(TT):
                    did(A.activation(junk[:], src[:, t, :], ACT.Square, accum_out=ss[:, t:t + 1]))
                    settle()
                did(A.activation(root[:], ss[:], ACT.Sqrt, scale=1.0 / D, bias=eps[:, 0:1]), root_ready, NORM[n] + 1)

            def take_hT(n):
                for t in range(TT):
                    for g in range(2):
                        name = ("hT", n, t, g)
                        act.wait_ge(small_ready, SMALL[name] + 1)
                        high_of(hT_high[:, 4 * g:4 * g + 4, t * P:(t + 1) * P],
                                small_of(name)[:, :].rearrange("p (k t) -> p k t", t=P))

            def take_small(name, dst, src):
                act.wait_ge(small_ready, SMALL[name] + 1)
                did(A.activation(dst, src, ACT.Copy), *taken_small(name))

            def take_sum(name, dst, func=ACT.Copy):
                act.wait_ge(sum_ready, SUM[name] + 1)
                did(A.activation(dst, sum_of(name)[:, :, :], func), *taken_sum(name))

            def columns(t):
                return t.rearrange("p (a b) t -> p a (b t)", b=2)

            def retention():
                for c in range(4):
                    highs(block_after(("ret_in",), c))
                    if c == 0:
                        act.wait_ge(rope_ang, 1)
                        did(A.activation(r_sin, r_ang, ACT.Sin), rope_raw, 1)
                        did(A.activation(r_cos, r_ang, ACT.Sin, scale=0.5), rope_raw, 2)
                        act.dma_start(r_decay, w["decay"].rearrange("h p i -> p h i")).then_inc(decay_in, 16)
                for c in range(4):
                    highs(block_after(("ret_in",), 4 + c))
                    take_sum(("ret_in", 4 + c), r_v[:, :, c * 512:(c + 1) * 512])
                for c in range(4):
                    highs(block_after(("ret_in",), 8 + c))
                    take_sum(("ret_in", 8 + c), r_g[:, :, c * 512:(c + 1) * 512], ACT.Silu)

                def yg_high(h):
                    for b in (2 * h, 2 * h + 1):
                        act.wait_ge(small_ready, SMALL[("ygT", b)] + 1)
                        high_of(r_ygT[0][:, 2 * b:2 * b + 2, :].rearrange("p f t -> p (f t)"), small_of(("ygT", b))[:, :])

                for h in range(RET_HEADS):
                    act.wait_ge(sum_ready, SUM[("ret_y", h)] + 1)
                    if h:
                        act.wait_ge(y_ms, h)
                    for t in range(TT):
                        did(A.activation(junk[:, 0:512], sum_of(("ret_y", h))[:, t, :], ACT.Square, accum_out=hs[:, t:t + 1]),
                            y_sq, 2 * h + t + 1)
                        settle()
                    act.wait_ge(y_ms, h + 1)
                    if h:
                        act.wait_ge(yg_ready, h)
                    did(A.activation(hs[:, 4:6], hs[:, 2:4], ACT.Sqrt), y_root, h + 1)
                    if h:
                        yg_high(h - 1)
                yg_high(RET_HEADS - 1)
                for c in range(2):
                    highs(block_after(("ret_out",), c))

            def peer(l):
                n = 1 + 2 * l
                act.wait_ge(x_ready, NORM[n] + 1)
                act.dma_start(p_keys, w["peer_sub_keys"][l].rearrange("h p k d -> k (h p) d")).then_inc(keys_in, 16)
                if l == 1:
                    act.dma_start(m_row_gain, bc(w["g_mem_2"].rearrange("(a d) -> a d", a=1), [P, D])).then_inc(mem_gain_in, 16)
                    act.dma_start(m_h, w["mem_2"][0].rearrange("(t p) d -> p t d", p=P)).then_inc(mem_in, 16)
                act.dma_start(p_iota, bc(w["iota"], [P, TOPK])).then_inc(iota_in, 16)
                norm_root(n, x)
                for b in range(4):
                    take_small(("keysT", l, b), p_keysT[:, 4 * b:4 * b + 4, :].rearrange("p a k -> p (a k)"), small_of(("keysT", l, b))[:, :])
                take_hT(n)
                def exponentials(i):
                    act.wait_ge(best_ready, l * UNITS + i + 1)
                    did(A.activation(p_e, p_d, ACT.Exp), exp_ready, l * UNITS + i + 1)

                for c in range(4):
                    highs(block_after(("query", l), c))
                    take_sum(("query", l, c), columns(p_qT[:, 4 * c:4 * c + 4, :]))
                    if c == 0:
                        highs(block_after(("query", l), 1))
                        exponentials(0)
                if l == 1:
                    norm_root(6, m_h)
                    take_hT(6)
                for i in range(UNITS):
                    if l == 1 and i < 8:
                        highs(min(first_block_of[("mem_kv", 0)] + i + 2, limit - 1))
                    if l == 1 and i in (2, 4, 6, 8):
                        c = i // 2 - 1
                        act.wait_ge(kv_ready, c + 1)
                        dst = columns(m_kT[:, 4 * c:4 * c + 4, :]) if c < 2 else m_v[:, :, (c - 2) * 512:(c - 1) * 512]
                        did(A.activation(dst, pair[kv_pair][:, :, :], ACT.Copy), kv_taken, c + 1)
                    for g in range(4):
                        n = (l * UNITS + i) * 4 + g
                        q = n % 2
                        act.wait_ge(u_used, GROUP * (n + 1))
                        did(A.activation(p_act[:, q, :], p_dot[:, q, :], ACT.Gelu_apprx_tanh), act_ready, n + 1)
                        act.wait_ge(weight_ready, n + 1)
                        for k in range(GROUP):
                            s = n * GROUP + k
                            if s >= 4:
                                act.wait_ge(v_used, s - 3)
                            did(A.activation(p_diag[:, s % 4, :], ident[:], ACT.Copy, scale=p_w[:, q, k:k + 1]),
                                diag_ready, s + 1)
                        if g == 2 and i + 1 < UNITS:
                            exponentials(i + 1)

            def sgu():
                act.wait_ge(x_ready, NORM[2] + 1)
                act.dma_start(s_ws, w["sgu_w_s"][0].rearrange("g i j -> i g j")).then_inc(sgu_in, 16)
                act.dma_start(s_vbias, bc(w["sgu_b_in"][0:1, HALF:2 * HALF], [P, HALF])).then_inc(sgu_in, 16)
                act.dma_start(s_bs.rearrange("p g i -> p (g i)"), bc(w["sgu_b_s"].rearrange("a g i -> a (g i)"), [P, GROUPS * P])).then_inc(sgu_in, 16)
                with nc.allow_non_contiguous_dma(reason="vectors by feature"):
                    act.dma_start(col[:, 8:32], w["sgu_b_in"][0, 0:HALF].rearrange("(k p) -> p k", p=P)).then_inc(sgu_in, 16)
                    act.dma_start(col[:, 32:56], w["sgu_ln_g"][0].rearrange("(k p) -> p k", p=P)).then_inc(sgu_in, 16)
                    act.dma_start(col[:, 56:80], w["sgu_ln_b"][0].rearrange("(k p) -> p k", p=P)).then_inc(sgu_in, 16)
                norm_root(2, x)
                take_hT(2)
                for c in range(6):
                    highs(block_after(("sgu_v",), 6 + c))
                    act.wait_ge(v_raw, c + 1)
                    vc = s_v[:, :, c * BN:(c + 1) * BN]
                    did(A.activation(vc, vc, ACT.Gelu_apprx_tanh), v_gelu, c + 1)
                for b in range(2):
                    name = ("wsT", b)
                    act.wait_ge(small_ready, SMALL[name] + 1)
                    src = small_of(name)[:, :].rearrange("p (g i) -> p g i", i=P)
                    did(A.activation(s_wsT[0:CHUNK, 4 * b:4 * b + 4, :], src[0:CHUNK], ACT.Copy))
                    did(A.activation(s_wsT[CHUNK:P, 4 * b:4 * b + 4, CHUNK:P], src[CHUNK:P, :, CHUNK:P], ACT.Copy), *taken_small(name))
                for b in range(2):
                    take_small(("ws_sum", b), s_wsum[:, 4 * b:4 * b + 4, :].rearrange("p g i -> p (g i)"), small_of(("ws_sum", b))[:, :])
                act.wait_ge(sgu_in, 16 * 6)
                for c in range(6):
                    name = ("sgu_u", c)
                    highs(block_after(("sgu_u",), c))
                    act.wait_ge(sum_ready, SUM[name] + 1)
                    for q in range(4):
                        f = 4 * c + q
                        did(A.activation(s_u[:, f, :], sum_of(name)[:, q // 2, q % 2 * S:(q % 2 + 1) * S], ACT.Gelu_apprx_tanh,
                                         bias=col[:, 8 + f:9 + f]), *((act_step, None) if q < 3 else taken_sum(name)))
                    settle()
                    if c == 3:
                        act.wait_ge(v_ms, 1)
                        did(A.activation(root[:], ms[:], ACT.Sqrt), v_root, 1)
                for b in range(CU // 2):
                    act.wait_ge(us_ready, b + 1)
                    high_of(s_us[0][:, 2 * b:2 * b + 2, :], s_t[:, 4 + 2 * (b % 2):6 + 2 * (b % 2), :])
                    if b >= 2 and b % 2 == 0:
                        highs(first_block_of[("sgu_out", 0)] + b // 2 + 1)
                for c in range(2):
                    highs(block_after(("sgu_out",), c))

            def hybrid():
                norm_root(4, x)
                act.wait_ge(x_ready, NORM[5] + 1)
                act.dma_start(b_mask, w["att_mask"]).then_inc(hyb_in, 16)
                act.dma_start(b_many, w["att_many"]).then_inc(hyb_in, 16)
                act.dma_start(b_ga, bc(w["g_attn_out_2"].rearrange("(a d) -> a d", a=1), [P, 512])).then_inc(hyb_in, 16)
                with nc.allow_non_contiguous_dma(reason="vectors by feature"):
                    act.dma_start(col[:, 36:40], w["g_conv_out_2"].rearrange("(k p) -> p k", p=P)).then_inc(hyb_in, 16)
                    act.dma_start(col[:, 40:52].rearrange("p (a k) -> p a k", k=4), w["conv_w_2"].rearrange("a (k p) -> p a k", p=P)).then_inc(hyb_in, 16)
                norm_root(5, x)
                take_hT(5)

                def exponentials(h):
                    act.wait_ge(smax_ready, h + 1)
                    for t, (a, b) in enumerate(((0, P), (P, 384))):
                        sm = b_sm[:, h % 2, a:b]
                        did(A.activation(sm, sm, ACT.Exp, bias=hp[h % 2][:, 2 + t:3 + t], scale=HD ** -0.5), e_ready, 2 * h + t + 1)

                def take_turned(h):
                    take_small(("attT", h), b_pT[:, h % 2, :], small_of(("attT", h))[:, 0:384])

                chunks = ((0, columns(b_qT)), (1, columns(b_kT)), (2, b_v), (4, columns(b_cgT)), (5, None), (3, columns(b_bgT)))
                for step, (c, dst) in enumerate(chunks):
                    highs(block_after(("w_in",), c))
                    if dst is not None:
                        take_sum(("w_in", c), dst)
                    if step >= 3:
                        take_turned(step - 3)
                    if step >= 2:
                        exponentials(step - 2)
                for h in range(2, HEADS - 1):
                    take_turned(h + 1)
                    if h + 2 < HEADS:
                        exponentials(h + 2)
                    if h == CONV_AT:
                        act.wait_ge(cms_ready, 1)
                        did(A.activation(b_rs, b_rs, ACT.Sqrt), croot_ready, 1)
                        act.wait_ge(mcv_ready, 1)
                        high_of(b_mT[0][:, 4:8, :], b_cvn)
                act.wait_ge(cms_ready, 2)
                did(A.activation(root[:], ms[:], ACT.Sqrt), croot_ready, 2)
                for t in range(TT):
                    act.wait_ge(small_ready, SMALL[("att_rows", t)] + 1)
                    high_of(b_mT[0][:, 0:4, t * P:(t + 1) * P], small_of(("att_rows", t))[:, :].rearrange("p (k t) -> p k t", t=P))
                for c in range(2):
                    highs(block_after(("w_out",), c))

            def memory():
                norm_root(7, x)
                take_hT(7)
                def queries(c):
                    take_sum(("q_mem", c), columns(n_qT[:, 4 * c:4 * c + 4, :]))

                def exponentials(h):
                    act.wait_ge(smax_ready, HEADS + h + 1)
                    if h >= 2:
                        act.wait_ge(*taken_small(("mattT", h - 2)))
                    for t in range(TT):
                        did(A.activation(n_p[:, h % 2, t, :], sum_of(("matt", h))[:, t, 0:S], ACT.Exp, bias=hp[h % 2][:, 2 + t:3 + t],
                                         scale=256 ** -0.5, accum_out=hp[h % 2][:, 4 + t:5 + t]), e_ready, 2 * (HEADS + h) + t + 1)

                def turned_and_out(h):
                    for g in (h, h + 1):
                        take_small(("mattT", g), n_pT[:, g % 2, :, :].rearrange("p m t -> p (m t)"), small_of(("mattT", g))[:, :])
                    for g in (h, h + 1):
                        act.wait_ge(small_ready, SMALL[("matto", g)] + 1)
                        high_of(n_oT[0][:, 2 * g:2 * g + 2, :].rearrange("p e t -> p (e t)"), small_of(("matto", g))[:, :])
                        if h == 0:
                            exponentials(g + 2)

                highs(block_after(("q_mem",), 0))
                queries(0)
                exponentials(0)
                exponentials(1)
                highs(block_after(("q_mem",), 1))
                queries(1)
                turned_and_out(0)
                turned_and_out(2)
                for c in range(2):
                    highs(block_after(("o_mem",), c))

            def mlp():
                norm_root(8, x)
                take_hT(8)
                for c in range(8):
                    name = ("up", c)
                    highs(block_after(("up",), c))
                    act.wait_ge(sum_ready, SUM[name] + 1)
                    if c >= 2:
                        act.wait_ge(a_low, c - 1)
                    did(A.activation(f_t[:, c % 2].rearrange("p (a b) t -> p a (b t)", b=2), sum_of(name)[:, :, :], ACT.Relu), *taken_sum(name))
                    settle()
                    act.sem_inc(relu_ready, 1)
                    act.wait_ge(a_ready, c + 1)
                    high_of(f_a[0][:, 4 * c:4 * c + 4, :], f_t[:, c % 2])
                for c in range(2):
                    highs(block_after(("down",), c))
                norm_root(9, x)

            act.dma_start(r_pos, bc(w["positions"], [P, S])).then_inc(rope_in, 16)
            act.dma_start(col[:, 8:9], w["inv_freq"]).then_inc(rope_in, 16)
            act.wait_ge(c_in, 16)
            act.wait_ge(ones_ready, 2)
            for k in range(KD):
                did(A.activation(c_full[:, k, :], ones[:], ACT.Silu, scale=col[:, k:k + 1]))
            settle()
            did(A.activation(c_high, c_full, ACT.Copy), c_ready, 1)
            for l in range(2):
                for c in range(12):
                    highs(block_after(("ada", l), c))
                    if l == 1 and c == 7:
                        norm_root(0, x)
                        highs(block_after(("ada", l), 8))
                        take_hT(0)
            retention()
            peer(0)
            sgu()
            peer(1)
            hybrid()
            memory()
            mlp()


def shape_constants():
    f = np.float32
    i = np.arange(S)
    j = np.arange(S)[:, None]
    decay = np.zeros((RET_HEADS, P, 384), f)
    for h in range(RET_HEADS):
        log_gamma = np.log(1.0 - 2.0 ** (-5.0 - h))
        table = np.exp(log_gamma * np.abs(i - j)) * (j // CHUNK <= i // CHUNK) * RET_QK ** -0.5
        decay[h] = np.concatenate([table[0:P], table[P:S, P:S]], axis=1)
    q, k = np.arange(S)[:, None], np.arange(S)[None, :]
    many = np.zeros((S, S), f)
    for window, dilation in ((128, 1), (512, 4), (2048, 16)):
        many += (k <= q) & (q - k <= window) & ((q - k) % dilation == 0)
    mask = np.where(many > 0, 0.0, NEG).astype(f)
    fold = lambda m: np.ascontiguousarray(np.concatenate([m[0:P, 0:P], m[P:S]], axis=1))
    half = RET_QK // 2
    inv_freq = (1.0 / (f(ROPE_BASE) ** (np.arange(half, dtype=f) / f(half)))).astype(f)
    return {"ident": np.eye(P, dtype=f), "decay": decay, "att_mask": fold(mask), "att_many": fold(many),
            "inv_freq": inv_freq.reshape(P, 1), "iota": np.arange(TOPK, dtype=f).reshape(1, TOPK)}


INPUTS = ["x", "c", "positions", "norm_mix", "norm_ffn", "ada_w", "ada_b", "ret_w_in", "ret_w_out", "sgu_w_in",
          "sgu_b_in", "sgu_ln_g", "sgu_ln_b", "sgu_w_s", "sgu_b_s", "sgu_w_out", "peer_w_query", "peer_sub_keys",
          "peer_u", "peer_v", "norm_final", "mem_2", "g_mix_2", "w_in_2", "conv_w_2", "g_attn_out_2",
          "g_conv_out_2", "w_out_2", "g_xattn_2", "g_mem_2", "w_q_mem_2", "w_kv_mem_2", "w_o_mem_2", "g_mlp_2",
          "w_up_2", "w_down_2", "g_final_2"]


def kernel(**inputs):
    import concourse.bacc as bacc
    from concourse.bass_utils import run_bass_kernel_spmd

    nc = bacc.Bacc("TRN2", target_bir_lowering=False, num_devices=1)
    arrays = {name: np.ascontiguousarray(inputs[name]) for name in INPUTS}
    arrays.update(shape_constants())
    arrays = {f"in_{name}": a for name, a in arrays.items()}
    w = {name[3:]: nc.dram_tensor(name, a.shape, mybir.dt.from_np(a.dtype), kind="ExternalInput").ap()
         for name, a in arrays.items()}
    out = nc.dram_tensor("out", (1, S, D), F32, kind="ExternalOutput").ap()
    two_blocks(nc, w, out)
    return run_bass_kernel_spmd(nc, [arrays], core_ids=[0]).results[0]["out"]
```
